# Optimizing a Trainium2 kernel written in Bass

```python
import math
import jax, jax.numpy as jnp
from jax import lax
import numpy as np

D_MODEL = 1024
BATCH = 1
SEQ = 512
DEPTH = 1

CHUNK = 64
NORM_EPS = 1e-6
GDN_HEADS = 4
GDN_DK = 64
GDN_DV = 64
GDN_CONV = 4
DIFF_HEADS = 4
DIFF_DV = 64
DIFF_DQK = DIFF_DV // 2
Q_BLOCK = 128
SGU_GROUPS = 4
SGU_DG = 64
SGU_LEN = 128
SWA_HEADS = 4
SWA_KV_HEADS = 2
SWA_DH = 64
WINDOW = 128
WIN_CHUNKS = WINDOW // CHUNK
N_EXPERTS = 16
N_EXPERT_GROUPS = 4
EXPERTS_PER_GROUP = N_EXPERTS // N_EXPERT_GROUPS
TOP_K = 2
D_EXPERT = 512

GDN_W = GDN_HEADS * GDN_DV
DIFF_W = DIFF_HEADS * DIFF_DV
SGU_W = SGU_GROUPS * SGU_DG
SWA_W = SWA_HEADS * SWA_DH
SWA_KV_W = SWA_KV_HEADS * SWA_DH
D_MIX = GDN_W + DIFF_W + SGU_W + SWA_W
GDN_QKV = 2 * GDN_HEADS * GDN_DK + GDN_W
DIFF_QK = DIFF_HEADS * 2 * DIFF_DQK
SPLIT_SIZES = (GDN_QKV, GDN_W, GDN_HEADS, GDN_HEADS, DIFF_QK, DIFF_QK, DIFF_W, 2 * SGU_W, SWA_W, SWA_KV_W, SWA_KV_W)
D_IN = sum(SPLIT_SIZES)

kernel_name = "hybrid_parallel_heads_moe_encoder"

def _rms_norm(x, gain):
    xf = x.astype(jnp.float32)
    y = xf * lax.rsqrt(jnp.mean(xf * xf, axis=-1, keepdims=True) + NORM_EPS)
    return (y * gain.astype(jnp.float32)).astype(x.dtype)

def _modulate(h, shift, scale):
    return h * (1 + scale[:, None, :]) + shift[:, None, :]

def _l2norm(x):
    return x * lax.rsqrt(jnp.sum(x * x, axis=-1, keepdims=True) + NORM_EPS)

def _alibi_slopes(n):
    return 2.0 ** (-8.0 * (jnp.arange(n, dtype=jnp.float32) + 1.0) / n)

def _causal_depthwise_conv(x, w):
    k_len, ch = w.shape
    return lax.conv_general_dilated(x, w[:, None, :], window_strides=(1,), padding=[(k_len - 1, 0)],
                                    dimension_numbers=('NWC', 'WIO', 'NWC'), feature_group_count=ch)

def _gated_delta_rule(q, k, v, g, beta):
    bsz, t_len, n_h, dk = q.shape
    dv = v.shape[-1]
    n = t_len // CHUNK
    q = q * dk ** -0.5

    def chunks(a):
        return a.reshape(bsz, n, CHUNK, *a.shape[2:]).swapaxes(2, 3)

    qc, kc, vc, gc, bc = chunks(q), chunks(k), chunks(v), chunks(g), chunks(beta)
    gcum = jnp.cumsum(gc, axis=-1)
    causal = jnp.tril(jnp.ones((CHUNK, CHUNK), dtype=bool))
    strict = jnp.tril(jnp.ones((CHUNK, CHUNK), dtype=bool), -1)
    decay = jnp.exp(jnp.where(causal, gcum[..., :, None] - gcum[..., None, :], -jnp.inf))
    kb = kc * bc[..., None]
    vb = vc * bc[..., None]
    low = jnp.where(strict, jnp.einsum('bnhid,bnhjd->bnhij', kb, kc) * decay, 0.0)
    rhs = jnp.concatenate([vb, kb * jnp.exp(gcum)[..., None]], axis=-1)
    sol = lax.linalg.triangular_solve(low + jnp.eye(CHUNK, dtype=low.dtype), rhs,
                                      left_side=True, lower=True, unit_diagonal=True)
    u, w = sol[..., :dv], sol[..., dv:]
    attn_intra = jnp.einsum('bnhid,bnhjd->bnhij', qc, kc) * decay
    q_dec = qc * jnp.exp(gcum)[..., None]
    g_last = gcum[..., -1]
    k_tail = kc * jnp.exp(g_last[..., None] - gcum)[..., None]

    def step(state, inp):
        qd, w_c, u_c, a_c, kt, gl = inp
        v_new = u_c - jnp.einsum('bhcd,bhde->bhce', w_c, state)
        o = jnp.einsum('bhcd,bhde->bhce', qd, state) + jnp.einsum('bhij,bhje->bhie', a_c, v_new)
        state = state * jnp.exp(gl)[..., None, None] + jnp.einsum('bhcd,bhce->bhde', kt, v_new)
        return state, o

    xs = tuple(jnp.moveaxis(a, 1, 0) for a in (q_dec, w, u, attn_intra, k_tail, g_last))
    s0 = jnp.zeros((bsz, n_h, dk, dv), jnp.float32)
    _, o = lax.scan(step, s0, xs)
    return o.transpose(1, 0, 3, 2, 4).reshape(bsz, t_len, n_h, dv)

def _mixer_gdn(qkv, gate, alpha, beta, conv_w, a_log, dt_bias, norm_g):
    bsz, t_len, _ = qkv.shape
    dtype = qkv.dtype
    qkv = jax.nn.silu(_causal_depthwise_conv(qkv, conv_w)).astype(jnp.float32)
    q, k, v = jnp.split(qkv, [GDN_HEADS * GDN_DK, 2 * GDN_HEADS * GDN_DK], axis=-1)
    q = _l2norm(q.reshape(bsz, t_len, GDN_HEADS, GDN_DK))
    k = _l2norm(k.reshape(bsz, t_len, GDN_HEADS, GDN_DK))
    v = v.reshape(bsz, t_len, GDN_HEADS, GDN_DV)
    g = -jnp.exp(a_log.astype(jnp.float32)) * jax.nn.softplus((alpha + dt_bias).astype(jnp.float32))
    b = jax.nn.sigmoid(beta.astype(jnp.float32))
    o = _gated_delta_rule(q, k, v, g, b)
    o = _rms_norm(o, norm_g) * jax.nn.silu(gate.astype(jnp.float32).reshape(bsz, t_len, GDN_HEADS, GDN_DV))
    return o.reshape(bsz, t_len, GDN_W).astype(dtype)

def _mixer_diff(q, k, v, lq1, lk1, lq2, lk2, norm_g, lam_init, slopes):
    bsz, t_len, _ = q.shape
    dtype = q.dtype
    f32 = jnp.float32
    q = q.astype(f32).reshape(bsz, t_len, DIFF_HEADS, 2, DIFF_DQK).transpose(3, 0, 2, 1, 4)
    k = k.astype(f32).reshape(bsz, t_len, DIFF_HEADS, 2, DIFF_DQK).transpose(3, 0, 2, 1, 4)
    v = v.astype(f32).reshape(bsz, t_len, DIFF_HEADS, DIFF_DV).transpose(0, 2, 1, 3)
    lam = (jnp.exp(jnp.sum(lq1.astype(f32) * lk1.astype(f32)))
           - jnp.exp(jnp.sum(lq2.astype(f32) * lk2.astype(f32))) + lam_init)
    nb = t_len // Q_BLOCK
    qb = q.reshape(2, bsz, DIFF_HEADS, nb, Q_BLOCK, DIFF_DQK).transpose(3, 0, 1, 2, 4, 5)
    kpos = jnp.arange(t_len)
    scale = DIFF_DQK ** -0.5

    def block(args):
        qq, start = args
        qpos = start + jnp.arange(Q_BLOCK)
        allowed = (kpos[None, :] // CHUNK) <= (qpos[:, None] // CHUNK)
        dist = jnp.abs(qpos[:, None] - kpos[None, :]).astype(f32)
        bias = jnp.where(allowed, -slopes[:, None, None] * dist, -jnp.inf)
        s = jnp.einsum('mbhqd,mbhkd->mbhqk', qq, k) * scale + bias
        p = jax.nn.softmax(s, axis=-1)
        return jnp.einsum('bhqk,bhkd->bhqd', p[0] - lam * p[1], v)

    o = lax.map(block, (qb, jnp.arange(nb) * Q_BLOCK))
    o = o.transpose(1, 0, 3, 2, 4).reshape(bsz, t_len, DIFF_HEADS, DIFF_DV)
    o = _rms_norm(o, norm_g) * (1.0 - lam_init)
    return o.reshape(bsz, t_len, DIFF_W).astype(dtype)

def _mixer_sgu(uv, norm_g, w_s, b_s):
    bsz, t_len, _ = uv.shape
    u, v = jnp.split(jax.nn.gelu(uv), 2, axis=-1)
    v = _rms_norm(v.reshape(bsz, t_len, SGU_GROUPS, SGU_DG), norm_g)
    v = v.reshape(bsz, t_len // SGU_LEN, SGU_LEN, SGU_GROUPS, SGU_DG)
    pos_chunk = jnp.arange(SGU_LEN) // CHUNK
    mask = pos_chunk[None, :] <= pos_chunk[:, None]
    w = jnp.where(mask, w_s, 0)
    mixed = jnp.einsum('gij,bnjgc->bnigc', w, v) + b_s.T[None, None, :, :, None]
    return u * mixed.reshape(bsz, t_len, SGU_W)

def _mixer_swa(q, k, v, sinks, slopes):
    bsz, t_len, _ = q.shape
    dtype = q.dtype
    f32 = jnp.float32
    n = t_len // CHUNK
    grp = SWA_HEADS // SWA_KV_HEADS
    q = q.astype(f32).reshape(bsz, n, CHUNK, SWA_KV_HEADS, grp, SWA_DH)
    k = k.astype(f32).reshape(bsz, n, CHUNK, SWA_KV_HEADS, SWA_DH)
    v = v.astype(f32).reshape(bsz, n, CHUNK, SWA_KV_HEADS, SWA_DH)

    def band(a):
        padded = jnp.pad(a, ((0, 0), (WIN_CHUNKS - 1, 0), (0, 0), (0, 0), (0, 0)))
        return jnp.concatenate([padded[:, i:i + n] for i in range(WIN_CHUNKS)], axis=2)

    kb, vb = band(k), band(v)
    s = jnp.einsum('bnqhgd,bnkhd->bhgnqk', q, kb) * SWA_DH ** -0.5
    qi = jnp.arange(CHUNK)
    kj = jnp.arange(WINDOW)
    dist = jnp.abs((WIN_CHUNKS - 1) * CHUNK + qi[:, None] - kj[None, :]).astype(f32)
    bias = -slopes.reshape(SWA_KV_HEADS, grp)[:, :, None, None] * dist
    key_chunk = jnp.arange(n)[:, None] - (WIN_CHUNKS - 1) + kj[None, :] // CHUNK
    valid = key_chunk >= 0
    s = jnp.where(valid[None, None, :, None, :], s + bias[:, :, None], -jnp.inf)
    sink = sinks.astype(f32).reshape(SWA_KV_HEADS, grp)[:, :, None, None, None]
    m = jnp.maximum(jnp.max(s, axis=-1, keepdims=True), sink)
    p = jnp.exp(s - m)
    p = p / (jnp.sum(p, axis=-1, keepdims=True) + jnp.exp(sink - m))
    o = jnp.einsum('bhgnqk,bnkhd->bnqhgd', p, vb)
    return o.reshape(bsz, t_len, SWA_W).astype(dtype)

def _moe(h, router_w, router_b, w_gate, w_up, w_down):
    bsz, t_len, d = h.shape
    f32 = jnp.float32
    t = h.reshape(-1, d)
    scores = jax.nn.sigmoid((t @ router_w).astype(f32))
    sel = scores + router_b.astype(f32)
    group_score = jnp.sum(lax.top_k(sel.reshape(-1, N_EXPERT_GROUPS, EXPERTS_PER_GROUP), TOP_K)[0], axis=-1)
    best = jnp.argmax(group_score, axis=-1)
    in_group = (jnp.arange(N_EXPERTS) // EXPERTS_PER_GROUP)[None, :] == best[:, None]
    _, idx = lax.top_k(jnp.where(in_group, sel, -jnp.inf), TOP_K)
    wts = jnp.take_along_axis(scores, idx, axis=-1)
    wts = wts / jnp.sum(wts, axis=-1, keepdims=True)
    gates = jnp.sum(jax.nn.one_hot(idx, N_EXPERTS, dtype=f32) * wts[..., None], axis=-2)
    y = jnp.zeros((t.shape[0], d), f32)
    for e in range(N_EXPERTS):
        he = jax.nn.silu(t @ w_gate[e]) * (t @ w_up[e])
        y = y + gates[:, e:e + 1] * (he @ w_down[e]).astype(f32)
    return y.astype(h.dtype).reshape(bsz, t_len, d)

def _normal(key, shape, scale):
    return jax.random.normal(key, shape, jnp.float32) * scale

def setup_inputs(seed: int = 0) -> dict:
    key = jax.random.key(seed)
    ks = jax.random.split(key, 29)
    d = D_MODEL
    dt = jnp.exp(jax.random.uniform(ks[12], (DEPTH, GDN_HEADS), jnp.float32,
                                    minval=math.log(1e-3), maxval=math.log(1e-1)))
    return {
        "x": _normal(ks[0], (BATCH, SEQ, d), 1.0),
        "c": _normal(ks[1], (BATCH, d), 1.0),
        "norm1": 1.0 + _normal(ks[2], (DEPTH, d), 0.02),
        "norm2": 1.0 + _normal(ks[3], (DEPTH, d), 0.02),
        "w_ada": _normal(ks[4], (DEPTH, d, 6 * d), 0.5 * d ** -0.5),
        "b_ada": _normal(ks[5], (DEPTH, 6 * d), 0.02),
        "w_in": _normal(ks[6], (DEPTH, d, D_IN), d ** -0.5),
        "b_in": _normal(ks[7], (DEPTH, D_IN), 0.02),
        "w_out": _normal(ks[8], (DEPTH, D_MIX, d), D_MIX ** -0.5),
        "b_out": _normal(ks[9], (DEPTH, d), 0.02),
        "conv_w": _normal(ks[10], (DEPTH, GDN_CONV, GDN_QKV), GDN_CONV ** -0.5),
        "a_log": jnp.log(jax.random.uniform(ks[11], (DEPTH, GDN_HEADS), jnp.float32, minval=1.0, maxval=16.0)),
        "dt_bias": dt + jnp.log(-jnp.expm1(-dt)),
        "gdn_norm": 1.0 + _normal(ks[13], (DEPTH, GDN_DV), 0.02),
        "lam_q1": _normal(ks[14], (DEPTH, DIFF_DQK), 0.1),
        "lam_k1": _normal(ks[15], (DEPTH, DIFF_DQK), 0.1),
        "lam_q2": _normal(ks[16], (DEPTH, DIFF_DQK), 0.1),
        "lam_k2": _normal(ks[17], (DEPTH, DIFF_DQK), 0.1),
        "diff_norm": 1.0 + _normal(ks[18], (DEPTH, DIFF_DV), 0.02),
        "sgu_norm": 1.0 + _normal(ks[19], (DEPTH, SGU_GROUPS, SGU_DG), 0.02),
        "sgu_w": _normal(ks[20], (DEPTH, SGU_GROUPS, SGU_LEN, SGU_LEN), SGU_LEN ** -0.5),
        "sgu_b": 1.0 + _normal(ks[21], (DEPTH, SGU_GROUPS, SGU_LEN), 0.02),
        "sinks": _normal(ks[22], (DEPTH, SWA_HEADS), 0.5),
        "router_w": _normal(ks[23], (d, N_EXPERTS), d ** -0.5),
        "router_b": _normal(ks[24], (N_EXPERTS,), 0.01),
        "w_gate": _normal(ks[25], (DEPTH, N_EXPERTS, d, D_EXPERT), d ** -0.5),
        "w_up": _normal(ks[26], (DEPTH, N_EXPERTS, d, D_EXPERT), d ** -0.5),
        "w_down": _normal(ks[27], (DEPTH, N_EXPERTS, D_EXPERT, d), D_EXPERT ** -0.5),
        "final_norm": 1.0 + _normal(ks[28], (d,), 0.02),
    }

def reference(x, c, norm1, norm2, w_ada, b_ada, w_in, b_in, w_out, b_out, conv_w, a_log, dt_bias,
              gdn_norm, lam_q1, lam_k1, lam_q2, lam_k2, diff_norm, sgu_norm, sgu_w, sgu_b, sinks,
              router_w, router_b, w_gate, w_up, w_down, final_norm):
    offsets = [int(o) for o in np.cumsum(SPLIT_SIZES)[:-1]]
    slopes = _alibi_slopes(DIFF_HEADS + SWA_HEADS)
    slopes_diff, slopes_swa = slopes[0::2], slopes[1::2]
    c_act = jax.nn.silu(c)
    for l in range(DEPTH):
        mod = c_act @ w_ada[l] + b_ada[l]
        shift1, scale1, gate1, shift2, scale2, gate2 = jnp.split(mod, 6, axis=-1)
        h = _modulate(_rms_norm(x, norm1[l]), shift1, scale1)
        z = h @ w_in[l] + b_in[l]
        a_qkv, a_gate, a_alpha, a_beta, b_q, b_k, b_v, c_uv, d_q, d_k, d_v = jnp.split(z, offsets, axis=-1)
        lam_init = 0.8 - 0.6 * math.exp(-0.3 * l)
        o_a = _mixer_gdn(a_qkv, a_gate, a_alpha, a_beta, conv_w[l], a_log[l], dt_bias[l], gdn_norm[l])
        o_b = _mixer_diff(b_q, b_k, b_v, lam_q1[l], lam_k1[l], lam_q2[l], lam_k2[l], diff_norm[l], lam_init, slopes_diff)
        o_c = _mixer_sgu(c_uv, sgu_norm[l], sgu_w[l], sgu_b[l])
        o_d = _mixer_swa(d_q, d_k, d_v, sinks[l], slopes_swa)
        y = jnp.concatenate([o_a, o_b, o_c, o_d], axis=-1) @ w_out[l] + b_out[l]
        x = x + gate1[:, None, :] * y
        h = _modulate(_rms_norm(x, norm2[l]), shift2, scale2)
        x = x + gate2[:, None, :] * _moe(h, router_w, router_b, w_gate[l], w_up[l], w_down[l])
    return _rms_norm(x, final_norm)


_drawn_inputs = setup_inputs


def setup_inputs(seed=0):
    import zlib

    import numpy as np

    out = dict(_drawn_inputs(seed))
    spreads = {}
    factors = {'norm1': 3.261,
     'norm2': 2.988,
     'b_in': 2.944,
     'b_out': 3.685,
     'a_log': 2.87,
     'gdn_norm': 5.386,
     'lam_q1': 6.881,
     'lam_k1': 8.0,
     'lam_q2': 7.321,
     'lam_k2': 7.368,
     'diff_norm': 8.0,
     'sgu_norm': 7.644,
     'sgu_b': 7.581,
     'sinks': 35.36,
     'final_norm': 2.733}
    for name, (base, spread) in spreads.items():
        noise = np.random.default_rng([zlib.crc32(name.encode()), seed]).standard_normal(out[name].shape)
        drawn = base * np.exp(spread * noise) if base else spread * noise
        out[name] = __import__('jax').numpy.asarray(drawn.astype(out[name].dtype))
    for name, factor in factors.items():
        out[name] = (out[name] * factor).astype(out[name].dtype)
    return out
```

```python
import math

import numpy as np

import concourse.bass as bass
from concourse import mybir

F32 = mybir.dt.float32
I32 = mybir.dt.int32
ALU = mybir.AluOpType
ACT = mybir.ActivationFunctionType
AX = mybir.AxisListType

P = 128
D = 1024
SEQ = 512
T = SEQ // P
K = D // P
CHUNK = 64
H = 4
DH = 64
E = 16
F = 512
D_IN = 2824
EPS = 1e-6
LAM_INIT = 0.8 - 0.6 * math.exp(0.0)
NEG = 1e30
KB = 1024
BASE = 16512

C_QKV, C_GATE, C_BQ, C_BK, C_BV, C_UV, C_DQ, C_DK, C_DV = 0, 768, 1032, 1288, 1544, 1800, 2312, 2568, 2696

INPUTS = ["x", "c", "norm1", "norm2", "w_ada", "b_ada", "w_in", "b_in", "w_out", "b_out", "conv_w", "a_log",
          "dt_bias", "gdn_norm", "lam_q1", "lam_k1", "lam_q2", "lam_k2", "diff_norm", "sgu_norm", "sgu_w",
          "sgu_b", "sinks", "router_w", "router_b", "w_gate", "w_up", "w_down", "final_norm"]


def products():
    out = [(("mod", b), "act") for b in range(4)]
    out += [(("hT", t, g), "act" if g else "dve") for t in range(T) for g in range(2)]
    for c in range(13):
        out += [(("zf", c), "act")]
        if c >= 5:
            out += [(("mod", 4 + 2 * (c - 5) + i), "act") for i in range(2)]
    out += [(("zt", t, s), "dve") for t in range(T) for s in range(4)]
    out += [(("qk_tm", t), "act") for t in range(T)] + [(("v_tm", t), "act") for t in range(T)]
    out += [(("gcum",), "dve")] + [(("grow", t), "dve") for t in range(T)]
    out += [(("kT", t), "act") for t in range(T)] + [(("qT", t), "act") for t in range(T)]
    out += [(("kk", t), "dve") for t in range(T)] + [(("kq", t), "dve") for t in range(T)]
    out += [(("M", t), "act") for t in range(T)]
    for step, who in (("L2", "act"), ("M2", "act"), ("L4", "act"), ("Ra", "dve"), ("Rb", "dve")):
        out += [((step, t), who) for t in range(T)]
    for lv in range(3):
        for step, who in (("Tm", "act"), ("Z", "act"), ("R", "dve")):
            out += [((step, lv, t), who) for t in range(T)]
    out += [(("U", t), "act") for t in range(T)] + [(("WT", t), "act") for t in range(T)]
    out += [(("QdT", t), "act") for t in range(T)]
    for ch in range(2 * T):
        out += [(("WQ", ch), "dve"), (("SU", ch), "dve")]
        if ch % 2:
            out += [(("AV", ch // 2), "dve")]
    units = attention_units()
    for n, u in enumerate(units):
        out += [(("score", n, m), "dve") for m in range(2 if u[0] == "diff" else 1)]
        if n >= 1:
            out += [(("pT", n - 1), "act")]
        if n >= 2:
            out += [(("pv", n - 2), "dve")]
    out += [(("pT", len(units) - 1), "act"), (("pv", len(units) - 2), "dve"), (("pv", len(units) - 1), "dve")]
    out += [(("sguT",), "dve")] + [(("mix", g), "dve") for g in range(H)]
    out += [(("oT", t, g), "act" if g else "dve") for t in range(T) for g in range(2)]
    out += [(("y", t, n), "dve") for t in range(T) for n in range(2)]
    out += [(("h2T", t, g), "act" if g else "dve") for t in range(T) for g in range(2)]
    out += [(("logit", t), "dve") for t in range(T)]
    out += [(("rank",), "dve")]
    return out


def attention_units():
    return [("diff", t, h) for t in range(T) for h in range(H)] + [("swa", t, h) for t in range(T) for h in range(H)]


def slopes():
    s = [2.0 ** (-8.0 * (i + 1) / 8) for i in range(8)]
    return s[0::2], s[1::2]


def build(nc, a, out):
    order = products()
    number = {name: n for n, (name, _) in enumerate(order)}
    assert len(number) == len(order)
    reader_count = []
    seen = {"act": 0, "dve": 0}
    for _, who in order:
        seen[who] += 1
        reader_count.append(seen[who])

    sems = {}

    def sem(name):
        if name not in sems:
            sems[name] = nc.alloc_semaphore(name)
        return sems[name]

    product_ready = sem("product_ready")
    banks_read = {"act": sem("banks_read_by_scalar"), "dve": sem("banks_read_by_vector")}

    def at(name, shape, dt, kb):
        t = nc.alloc_sbuf_tensor_at(name, [P] + shape, dt, offset=BASE + int(kb * KB))
        assert BASE + kb * KB + math.prod(shape) * 4 <= 229344, name
        return t.ap()

    x = at("x", [T, D], F32, 0)
    mod2 = at("mod2", [4, D], F32, 16)
    hT = at("hT", [K, SEQ], F32, 32)
    ada_rest = [at(f"ada_rest{i}", [K, 256], F32, 48 + 8 * i) for i in range(2)]
    zpad = at("zpad", [6, SEQ + 3], F32, 64)
    zb = at("zb", [7, SEQ], F32, 77)
    h_ring = [at(f"h_ring{i}", [D], F32, 77 + 4 * i) for i in range(2)]
    gab = at("gab", [T, 264], F32, 91)
    bv = at("bv", [T, 256], F32, 96)
    uv = at("uv", [T, 512], F32, 100)
    mod1 = at("mod1", [2, D], F32, 96)
    dv = at("dv", [T, 128], F32, 108)
    acc_ring = [at(f"acc_ring{i}", [512], F32, 110 + 2 * i) for i in range(2)]
    W = 114
    w_qkv = at("w_qkv", [K, 768], F32, W)
    w_b = at("w_b", [K, 512], F32, W + 24)
    w_d = at("w_d", [K, 384], F32, W + 40)
    w_g = at("w_g", [K, 264], F32, W + 52)
    w_v = at("w_v", [K, P], F32, W + 60.25)
    w_t = at("w_t", [K, 512], F32, W)
    w_u = at("w_u", [K, 256], F32, W + 16)
    ada_first = [at(f"ada_first{i}", [K, 512], F32, p) for i, p in enumerate((W + 24, W + 40, W + 56, 32))]
    btm = at("btm", [1160], F32, 186)
    n1bc = at("n1bc", [D], F32, 91)
    brow = [at(f"brow{i}", [256], F32, 191 + i) for i in range(2)]
    brow_first = at("brow_first", [512], F32, 191)
    cring = [at(f"cring{i}", [SEQ], F32, 193 + 2 * i) for i in range(2)]
    squares = at("squares", [D], F32, 86)
    o_tm = at("o_tm", [T, D], F32, W)
    qkv_tm = at("qkv_tm", [T, 768], F32, 130)
    AT = at("AT", [T, H, P], F32, 142)
    Lf = at("Lf", [T, H, P], F32, 150)
    B1 = at("B1", [T, H, P], F32, 158)
    B2 = at("B2", [T, H, P], F32, 166)
    B3 = at("B3", [T, H, P], F32, 174)
    B4 = at("B4", [T, H, P], F32, 182)
    R = at("R", [T, H, P], F32, 190)
    kT = at("kT", [T, H, P], F32, 32)
    qT = at("qT", [T, H, P], F32, 40)
    WT = at("WT", [T, H, P], F32, 150)
    QdT = at("QdT", [T, H, P], F32, 166)
    vb = at("vb", [T, H, DH], F32, 158)
    kbe = at("kbe", [T, H, DH], F32, 162)
    U = at("U", [T, H, DH], F32, 174)
    ktail = at("ktail", [T, H, DH], F32, 178)
    v_new = at("v_new", [T, H, DH], F32, 182)
    qs = at("qs", [T, H, DH], F32, 186)
    Qd = at("Qd", [T, H, DH], F32, 48)
    S = at("S", [H, DH], F32, 52)
    Stmp = at("Stmp", [H, DH], F32, 53)
    bias_diff = at("bias_diff", [H, SEQ], F32, 64)
    bias_swa = at("bias_swa", [H, 256], F32, 72)
    s_sb = [[at(f"s_sb{i}{m}", [SEQ], F32, 154 + 4 * i + 2 * m) for m in range(2)] for i in range(2)]
    p_sb = [[at(f"p_sb{i}{m}", [SEQ], F32, 162 + 4 * i + 2 * m) for m in range(2)] for i in range(2)]
    pc = [at(f"pc{i}", [SEQ], F32, 170 + 2 * i) for i in range(2)]
    pT = [at(f"pT{i}", [4, P], F32, 174 + 2 * i) for i in range(2)]
    wide = at("wide", [SEQ], F32, 110)
    bobc = at("bobc", [D], F32, 110)
    n2bc = at("n2bc", [D], F32, 130)
    junk1k = at("junk1k", [D], F32, 110)
    junk_last = at("junk_last", [D], F32, 40)
    before = at("before", [P], F32, 76)
    sixteen = [at(f"sixteen{i}", [T, E], F32, 72 + 0.25 * i) for i in range(16)]
    sgw = at("sgw", [H, P], F32, 182)
    sgT = at("sgT", [H, P], F32, 184)
    vn = at("vn", [T, H, DH], F32, 186)
    sq = at("sq", [T, 256], F32, 194)
    w_o = [at(f"w_o{i}", [K, 512], F32, 32 + 16 * i) for i in range(2)]
    oT = at("oT", [K, SEQ], F32, 64)
    ytmp = [at(f"ytmp{i}", [512], F32, 104 + 2 * i) for i in range(2)]
    h2_ring = [at(f"h2_ring{i}", [D], F32, 96 + 4 * i) for i in range(2)]
    h2T = at("h2T", [K, SEQ], F32, 80)
    off = [198.0]

    def small(name, shape, dt=F32):
        n = math.prod(shape) * 4 / KB
        off[0] = math.ceil(off[0] * 32) / 32
        off[0] += n
        return at(name, shape, dt, off[0] - n)

    ident = small("ident", [P])
    ones = small("ones", [P])
    tri = small("tri", [P])
    mask_s = small("mask_s", [P])
    mlv = [small(f"mlv{i}", [P]) for i in range(4)]
    m8T = small("m8T", [P])
    acol = small("acol", [8])
    ccol = small("ccol", [8])
    ss = small("ss", [T])
    rs = small("rs", [T])
    bcol = small("bcol", [13])
    convc = small("convc", [6, 4])
    g_ = small("g_", [T, H])
    beta = small("beta", [T, H])
    gc = small("gc", [T, H])
    egc = small("egc", [T, H])
    nss = small("nss", [T, 8])
    nrs = small("nrs", [T, 8])
    glast = small("glast", [T, H, 2])
    etail = small("etail", [T, H])
    egl = small("egl", [T, H, 2])
    alog = small("alog", [H])
    dtb = small("dtb", [H])
    sink = small("sink", [H])
    gnorm = small("gnorm", [DH])
    dnorm = small("dnorm", [DH])
    lam4 = small("lam4", [4, 32])
    lamt = small("lamt", [2, 32])
    lam = small("lam", [4])
    sgb = small("sgb", [H])
    mx = small("mx", [2, 8])
    snorm = small("snorm", [256])
    rb = small("rb", [E])
    rw = small("rw", [K, E])
    tA = small("tA", [T, H])
    tB = small("tB", [T, H])
    tC = small("tC", [T, H])
    wtok = small("wtok", [2, T])
    eps = small("eps", [1])
    junk = small("junk", [1])
    neglam = small("neglam", [1])
    iscat = small("iscat", [2, T], I32)
    pairid = small("pairid", [2, T], I32)
    rounds = small("rounds", [1], I32)
    table = small("table", [80], I32)
    tokens = small("tokens", [80], I32)
    idx_g = [small(f"idx_g{i}", [1], I32) for i in range(2)]
    idx_s = [small(f"idx_s{i}", [1], I32) for i in range(2)]
    w_exp = [[at(f"w_exp{b}{i}", [K, F] if i < 2 else [4, D], F32, p + 16 * i) for i in range(3)] for b, p in ((0, 150), (1, 102))]
    xg = [at(f"xg{b}", [D], F32, 32 + 4 * b) for b in range(2)]
    xgT = [at(f"xgT{b}", [K, P], F32, 40 + 4 * b) for b in range(2)]
    gated = [at(f"gated{b}", [F], F32, 48 + 2 * b) for b in range(2)]
    he = [at(f"he{b}", [F], F32, 52 + 2 * b) for b in range(2)]
    heT = [at(f"heT{b}", [4, P], F32, 56 + 2 * b) for b in range(2)]
    yo = [at(f"yo{b}", [D], F32, 64 + 4 * b) for b in range(2)]
    yb = [at(f"yb{b}", [2, D], F32, 80 + 8 * b) for b in range(2)]
    ym = at("ym", [D], F32, 72)
    fbc = at("fbc", [D], F32, 76)
    fout = [at(f"fout{b}", [D], F32, 32 + 4 * b) for b in range(2)]
    h2_dram = nc.dram_tensor("h2_rows", [SEQ, D], F32).ap()
    y_dram = nc.dram_tensor("expert_rows", [2 * SEQ, D], F32).ap()
    table_dram = nc.dram_tensor("slot_table", [P * 80, 1], I32).ap()


    def wait_product(eng, *name):
        eng.wait_ge(product_ready, number[name] + 1)

    def wait_read(eng, *name):
        eng.wait_ge(banks_read[order[number[name]][1]], reader_count[number[name]])

    def chain(eng, step):
        count = {}

        def link(ins, signal=step):
            count[signal] = count.get(signal, 0) + 1
            ins.then_inc(signal, 1)
            eng.wait_ge(signal, count[signal])
        return link

    def nth(eng, scale, r, p, j, plus):
        v = r * (E * scale) + p * (2 * scale) + (j * scale + plus)
        return v if isinstance(v, int) else eng.snap(v)

    def nth_of_half(eng, scale, r, p, j, plus):
        v = r * (E // 2 * scale) + p * scale + (j // 2 * scale + plus)
        return v if isinstance(v, int) else eng.snap(v)

    def in_steps(eng, r, first, step, last):
        first(r)
        with eng.Fori(0, E // 2 - 1) as p:
            for j in (1, 2):
                step(r, p, j)
        last(r)

    def over_heads(v, n):
        return v.unsqueeze(2).to_broadcast([P, H, n])

    def per_head(m):
        return m.unsqueeze(1).to_broadcast([P, H, m.shape[-1]])

    psum = nc.alloc_psum_tensor("psum", [P, 8, 512], F32).ap()

    def bank(*name):
        return psum[:, number[name] % 8]

    def row(v):
        return v.partition_broadcast(P)

    w_ada = a["w_ada"][0].rearrange("(p j) n -> p j n", j=8)
    w_in = a["w_in"][0].rearrange("(k p) n -> p k n", p=P)
    w_out = a["w_out"][0].rearrange("(k p) n -> p k n", p=P)
    b_in = a["b_in"][0]
    zf_cols = [C_QKV + P * i for i in range(6)] + [C_BQ, C_BQ + P, C_BK, C_BK + P, C_DQ, C_DQ + P, C_DK]
    zt_parts = [(w_g, C_GATE, 264, 0), (w_t, C_BV, 512, 264), (w_u, C_BV + 512, 256, 776), (w_v, C_DV, P, 1032)]
    units = attention_units()
    maxes, n_blocks, n_ = [], [], 0
    for kind, t, h in units:
        maxes.append(n_)
        n_ += 2 if kind == "diff" else 1
        n_blocks.append(t + 1 if kind == "diff" else (2 if t else 1))
    logits_, scores, sel, mask, one1, one2, m16, u16, v16, sel2 = sixteen[:10]
    grp = [at(f"grp{i}", [T, 4], F32, 76.5 + 0.0625 * i) for i in range(16)]
    col = [at(f"col{i}", [T], F32, 77.5 + 0.03125 * i) for i in range(16)]
    eidx = at("eidx", [T, E], F32, 78)
    gw = at("gw", [T, 4], F32, 78.25)
    eweight = at("eweight", [T, E], F32, 78.5)
    rank = at("rank", [T, E], F32, 78.75)
    counts = at("counts", [E], F32, 79)

    with nc.Block() as block:

        @block.sync
        def _(sp):
            sp.dma_start(ccol, a["c"][0].rearrange("(p j) -> p j", j=8)).then_inc(sem("ld_c"), 16)
            xr = a["x"][0].rearrange("(t p) d -> p t d", p=P)
            for b in range(4):
                sp.dma_start(ada_first[b], w_ada[:, :, 512 * b:512 * b + 512]).then_inc(sem(f"ld_ada{b}"), 16)
                if b == 0:
                    sp.dma_start(x, xr).then_inc(sem("ld_x"), 16)
                    sp.dma_start(n1bc, row(a["norm1"][0])).then_inc(sem("ld_n1"), 16)
            sp.dma_start(bcol[:, 0:6], b_in[0:768].rearrange("(c p) -> p c", p=P), allow_slow_non_contiguous=True).then_inc(sem("ld_bcol"), 16)
            sp.dma_start(bcol[:, 6:10], b_in[C_BQ:C_BQ + 512].rearrange("(c p) -> p c", p=P), allow_slow_non_contiguous=True).then_inc(sem("ld_bcol"), 16)
            for g in range(2):
                for kv in range(2):
                    c0 = C_DQ + (2 * kv + g) * DH
                    sp.dma_start(bcol[DH * kv:DH * kv + DH, 10 + g:11 + g], b_in[c0:c0 + DH].unsqueeze(1), allow_slow_non_contiguous=True).then_inc(sem("ld_bcol"), 16)
            sp.dma_start(bcol[:, 12:13], b_in[C_DK:C_DK + P].unsqueeze(1), allow_slow_non_contiguous=True).then_inc(sem("ld_bcol"), 16)
            sp.dma_start(w_qkv, w_in[:, :, 0:768]).then_inc(sem("ld_w0"), 16)
            for i in range(4):
                sp.dma_start(convc[:, :, i], a["conv_w"][0, i].rearrange("(c p) -> p c", p=P), allow_slow_non_contiguous=True).then_inc(sem("ld_conv"), 16)
            for nm, dst in (("a_log", alog), ("dt_bias", dtb), ("sinks", sink), ("gdn_norm", gnorm), ("diff_norm", dnorm)):
                sp.dma_start(dst, row(a[nm][0])).then_inc(sem("ld_small"), 16)
            for i, nm in enumerate(("lam_q1", "lam_k1", "lam_q2", "lam_k2")):
                sp.dma_start(lam4[:, i], row(a[nm][0])).then_inc(sem("ld_small"), 16)
            sp.dma_start(sgb, a["sgu_b"][0].rearrange("g p -> p g"), allow_slow_non_contiguous=True).then_inc(sem("ld_small"), 16)
            sp.wait_ge(sem("acc_ready"), 4)
            sp.dma_start(w_b, w_in[:, :, C_BQ:C_BQ + 512]).then_inc(sem("ld_w1"), 16)
            for g in range(2):
                for kv in range(2):
                    c0, o = C_DQ + (2 * kv + g) * DH, P * g + DH * kv
                    sp.dma_start(w_d[:, :, o:o + DH], w_in[:, :, c0:c0 + DH]).then_inc(sem("ld_w2"), 16)
            sp.dma_start(w_d[:, :, 256:384], w_in[:, :, C_DK:C_DK + P]).then_inc(sem("ld_w2"), 16)
            sp.dma_start(w_g, w_in[:, :, C_GATE:C_GATE + 264]).then_inc(sem("ld_w3"), 16)
            sp.dma_start(w_v, w_in[:, :, C_DV:C_DV + P]).then_inc(sem("ld_w6"), 16)
            for i, (_, c0, n, o) in enumerate(zt_parts):
                sp.dma_start(btm[:, o:o + n], row(b_in[c0:c0 + n])).then_inc(sem("ld_btm"), 16)
            for b in range(4, 20):
                if b == 8:
                    wait_product(sp, "zf", 5)
                    sp.dma_start(w_t, w_in[:, :, C_BV:C_BV + 512]).then_inc(sem("ld_w4"), 16)
                    sp.dma_start(w_u, w_in[:, :, C_BV + 512:C_BV + 768]).then_inc(sem("ld_w5"), 16)
                if b >= 6:
                    sp.wait_ge(sem("acc_ready"), b - 1)
                c0 = 2048 + 256 * (b - 4)
                sp.dma_start(ada_rest[b % 2], w_ada[:, :, c0:c0 + 256]).then_inc(sem(f"ld_adar{b % 2}"), 16)
                sp.dma_start(brow[b % 2][0:1], a["b_ada"][0:1, c0:c0 + 256]).then_inc(sem(f"ld_adar{b % 2}"), 16)
            wait_product(sp, "AV", T - 1)
            sp.dma_start(w_o[0], w_out[:, :, 0:512]).then_inc(sem("ld_wo"), 16)
            sp.wait_ge(sem("biases"), 1)
            sp.dma_start(bobc, row(a["b_out"][0])).then_inc(sem("ld_bo"), 16)
            sp.wait_ge(sem("gdn_done"), 1)
            sp.dma_start(sgw, a["sgu_w"][0].rearrange("g i j -> i g j")).then_inc(sem("ld_sgw"), 16)
            sp.dma_start(w_o[1], w_out[:, :, 512:1024]).then_inc(sem("ld_wo"), 16)
            sp.dma_start(n2bc, row(a["norm2"][0])).then_inc(sem("ld_n2"), 16)
            sp.dma_start(snorm, row(a["sgu_norm"][0].rearrange("g c -> (g c)"))).then_inc(sem("ld_small2"), 16)
            sp.dma_start(rb, row(a["router_b"])).then_inc(sem("ld_small2"), 16)
            sp.dma_start(rw, a["router_w"].rearrange("(k p) e -> p k e", p=P)).then_inc(sem("ld_small2"), 16)

            def load_expert(b, e, i):
                for n, (nm, used, at_) in enumerate((("w_gate", "gate_made", i + 1), ("w_up", "up_made", i + 1), ("w_down", "y_made", i * 2 + 2))):
                    src = a[nm][0, bass.ds(e, 1)].rearrange("o (k p) n -> p (o k) n", p=P)
                    sp.wait_ge(sem(used), sp.snap(at_))
                    sp.dma_start(w_exp[b][n], src).then_inc(sem(f"ld_{nm}{b}"), 16)

            def expert_pass(r):
                with sp.Fori(0, E // 2) as p:
                    for b in range(2):
                        load_expert(b, p * 2 + b, r * 16 + p * 2 + b)

            wait_read(sp, "mix", H - 1)
            for t in range(T):
                sp.wait_ge(sem("h2_ready"), t + 1)
                sp.dma_start(h2_dram[P * t:P * t + P], h2_ring[t % 2]).then_inc(sem(f"st_h2{t % 2}"), 16)
            sp.wait_ge(sem("st_h20"), 32)
            sp.wait_ge(sem("st_h21"), 32)
            expert_pass(0)
            sp.wait_ge(sem("rounds_ready"), 1)
            n_rounds = sp.value_load(rounds[0:1, 0:1], min_val=1, max_val=4)
            with sp.If(n_rounds > 1):
                with sp.Fori(1, n_rounds) as r:
                    expert_pass(r)
            sp.dma_start(fbc, row(a["final_norm"])).then_inc(sem("ld_fn"), 16)
            sp.wait_ge(sem("all_scattered"), 1)
            for t in range(T):
                if t >= 2:
                    sp.wait_ge(sem("yb_used"), t - 1)
                sp.dma_start(yb[t % 2], y_dram.rearrange("(t p k) d -> t p k d", p=P, k=2)[t]).then_inc(sem(f"ld_yb{t % 2}"), 16)
                if t >= 1:
                    sp.wait_ge(sem("out_ready"), t)
                    sp.dma_start(out[0, P * (t - 1):P * t], fout[(t - 1) % 2]).then_inc(sem(f"st_out{(t - 1) % 2}"), 16)
            sp.wait_ge(sem("out_ready"), T)
            sp.dma_start(out[0, P * (T - 1):P * T], fout[(T - 1) % 2]).then_inc(sem(f"st_out{(T - 1) % 2}"), 16)
            for i in range(2):
                sp.wait_ge(sem(f"st_out{i}"), 16 * T // 2)

        @block.gpsimd
        def _(gp):
            link = chain(gp, sem("pool_step"))
            g = nc.gpsimd

            def keep(m, pattern, base, cm, fill=0.0, op=ALU.is_ge):
                link(g.affine_select(out=m, in_=m, pattern=pattern, compare_op=op, fill=fill, base=base, channel_multiplier=cm))

            link(g.memset(ones, 1.0))
            link(g.memset(ident, 0.0))
            link(g.memset(eps, EPS))
            g.affine_select(out=ident, in_=ident, pattern=[[-1, P]], compare_op=ALU.not_equal, fill=1.0, base=0,
                            channel_multiplier=1).then_inc(sem("consts"), 1)
            for b in range(4):
                if b:
                    gp.wait_ge(sem("acc_ready"), b)
                gp.dma_start(brow_first[0:1], a["b_ada"][0:1, 512 * b:512 * b + 512]).then_inc(sem("ld_brow"), 16)
            gp.wait_ge(sem("acc_ready"), 4)
            g.memset(zpad[:, :, 0:3], 0.0).then_inc(sem("pads"), 1)
            for m, b_, cm, s in ((tri, 0, -1, 1), (mask_s, -1, 1, -1)):
                link(g.memset(m, 1.0))
                keep(m, [[s, P]], b_, cm)
            link(g.memset(tri[0:64, 64:128], 0.0))
            link(g.memset(mask_s[64:128, 0:64], 0.0))
            for i, n in enumerate((8, 16, 32, 64)):
                link(g.memset(mlv[i], 1.0))
                keep(mlv[i], [[n, P // n], [0, n]], n - 1, -1)
                if i == 0:
                    keep(mlv[i], [[-1, P]], -1, 1)
                else:
                    keep(mlv[i], [[-n // 2, 2 * P // n], [0, n // 2]], -n // 2, 1)
            link(g.memset(m8T, 1.0))
            keep(m8T, [[1, P]], -1, -1)
            link(g.affine_select(out=m8T, in_=m8T, pattern=[[-8, P // 8], [0, 8]], compare_op=ALU.is_ge, fill=0.0, base=0,
                                 channel_multiplier=1), sem("masks_ready"))
            gp.wait_ge(product_ready, number[("v_tm", T - 1)] + 1)
            sd, sw = slopes()
            for h in range(H):
                for dst, tmp, n, first, k in ((bias_diff[:, h], wide, SEQ, 384, sd[h] * 32 ** 0.5),
                                              (bias_swa[:, h], wide[:, 0:256], 256, 128, sw[h] * DH ** 0.5)):
                    link(g.iota(dst, [[-1, n]], base=first, channel_multiplier=1, allow_small_or_imprecise_dtypes=True))
                    link(g.tensor_scalar(tmp, dst, 0.0, -2 * k, ALU.max, ALU.mult))
                    link(g.tensor_scalar(dst, dst, k, None, ALU.mult))
                    link(g.tensor_tensor(dst, dst, tmp, ALU.add))
            link(g.memset(bias_diff[0:64, :, 448:512], -NEG))
            link(g.memset(bias_swa[0:64, :, 0:64], -NEG))
            link(g.memset(bias_swa[0:64, :, 192:256], -NEG))
            link(g.memset(bias_swa[64:128, :, 0:128], -NEG))
            g.memset(wide[:, 0:1], 0.0).then_inc(sem("biases"), 1)
            for t in range(T):
                gp.wait_ge(sem("decay"), 2 * t + 2)
                link(g.tensor_tensor(B1[:, t], B1[:, t], per_head(mask_s), ALU.mult))
                g.tensor_tensor(B1[:, t], B1[:, t], over_heads(beta[:, t], P), ALU.mult).then_inc(sem("decay_masked"), 1)
                g.tensor_tensor(AT[:, t], AT[:, t], per_head(tri), ALU.mult).then_inc(sem("decay_masked"), 1)
            for t in range(T):
                wait_read(gp, "M", t)
                g.tensor_tensor(B1[:, t], B4[:, t], per_head(m8T), ALU.mult).then_inc(sem("eights"), 1)
                g.tensor_tensor(B2[:, t], Lf[:, t], per_head(mlv[0]), ALU.mult).then_inc(sem("eights"), 1)
            gp.wait_ge(sem("eights"), 2 * T)
            for t in range(T):
                g.tensor_tensor(R[:, t], per_head(ident), B1[:, t], ALU.subtract).then_inc(sem("R_first"), 1)
            for lv in range(3):
                for t in range(T):
                    gp.wait_ge(product_ready, number[("M2", t) if lv == 0 else ("Z", lv - 1, t)] + 1)
                    g.tensor_tensor(B2[:, t], Lf[:, t], per_head(mlv[lv + 1]), ALU.mult).then_inc(sem("level_masked"), 1)
            gp.wait_ge(sem("level_masked"), 3 * T)
            wait_read(gp, "mod", 19)
            gp.wait_ge(sem("ld_bo"), 16)
            link(g.tensor_tensor(bobc, bobc, mod2[:, 0], ALU.mult))
            for t in range(T):
                g.tensor_tensor(x[:, t], x[:, t], bobc, ALU.add).then_inc(sem("x_biased"), 1)
            link(g.iota(table, [[1, 80]], base=4096, channel_multiplier=80))
            gp.dma_start(table_dram.rearrange("(p n) o -> p (n o)", n=80), table).then_inc(sem("table_filled"), 16)
            gp.wait_ge(sem("x1_ready"), 2 * T)
            link(g.iota(eidx, [[0, T], [1, E]], base=0, channel_multiplier=0, allow_small_or_imprecise_dtypes=True))
            link(g.iota(eweight, [[0, T], [-1, E]], base=E, channel_multiplier=0, allow_small_or_imprecise_dtypes=True))
            g.iota(gw, [[0, T], [-1, 4]], base=4, channel_multiplier=0, allow_small_or_imprecise_dtypes=True).then_inc(sem("router_consts"), 1)
            link(g.memset(before, 1.0))
            g.affine_select(out=before, in_=before, pattern=[[1, P]], compare_op=ALU.is_ge, fill=0.0, base=-1,
                            channel_multiplier=-1).then_inc(sem("before_ready"), 1)
            link(g.iota(pairid, [[1, 2], [2 * P, T]], base=0, channel_multiplier=2))
            gp.wait_ge(sem("table_filled"), 16)
            gp.wait_ge(sem("places_ready"), 2)
            for k in range(2):
                for t in range(T):
                    g.indirect_dma_start(table_dram, bass.IndirectOffsetOnAxis(iscat[:, k, t:t + 1], 0),
                                         pairid[:, k, t:t + 1], None).then_inc(sem("table_scattered"), 16)
            gp.wait_ge(sem("table_scattered"), 16 * 2 * T)
            gp.dma_start(table, table_dram.rearrange("(p n) o -> p (n o)", n=80)).then_inc(sem("ld_table"), 16)
            for b in range(2):
                g.memset(xg[b], 0.0).then_inc(sem("xg_cleared"), 1)
            gp.wait_ge(sem("xg_cleared"), 2)
            gp.wait_ge(sem("st_h20"), 32)
            gp.wait_ge(sem("st_h21"), 32)

            last_token, last_pair = gp.to_reg(SEQ - 1), gp.to_reg(2 * SEQ - 1)

            def gather(b):
                g.indirect_dma_start(xg[b], None, h2_dram, bass.IndirectOffsetOnAxis(idx_g[b], 0),
                                     bounds_check=last_token, oob_is_err=False).then_inc(sem(f"ld_xg{b}"), 16)

            def gather_next(r, p, j):
                b = j % 2
                gp.wait_ge(sem(f"idx_ready{b}"), nth_of_half(gp, 1, r, p, j, 2))
                gp.sem_inc(sem("gather_turn"), 1)
                gather(b)

            def scatter(r, p, j):
                b = j % 2
                done = nth_of_half(gp, 16, r, p, j, 16)
                gp.wait_ge(sem("y_read_act"), nth(gp, 1, r, p, j, 2))
                gp.wait_ge(sem("y_read_dve"), nth(gp, 1, r, p, j, 2))
                gp.sem_inc(sem("scatter_turn"), 1)
                g.indirect_dma_start(y_dram, bass.IndirectOffsetOnAxis(idx_s[b], 0), yo[b], None,
                                     bounds_check=last_pair, oob_is_err=False).then_inc(sem(f"scattered{b}"), 16)
                gp.wait_ge(sem(f"scattered{b}"), done)
                gp.sem_inc(sem(f"slot_free{b}"), 1)

            for b in range(2):
                gp.sem_inc(sem(f"slot_free{b}"), 1)
                gp.wait_ge(sem(f"idx_ready{b}"), 1)
                gather(b)

            def first(r):
                gather_next(r, 0, 0)
                gather_next(r, 0, 1)

            def step(r, p, j):
                gather_next(r, p, j + 1)
                scatter(r, p, j - 1)

            def last(r):
                scatter(r, 0, E - 2)
                scatter(r, 0, E - 1)

            in_steps(gp, 0, first, step, last)
            gp.wait_ge(sem("rounds_ready"), 1)
            n_rounds = gp.value_load(rounds[0:1, 0:1], min_val=1, max_val=4)
            with gp.If(n_rounds > 1):
                with gp.Fori(1, n_rounds) as r:
                    in_steps(gp, r, first, step, last)
            gathers = gp.snap((n_rounds * 8 + 1) * 16)
            for b in range(2):
                gp.wait_ge(sem(f"ld_xg{b}"), gathers)
                gp.sem_inc(sem("gather_turn"), 1)
            g.memset(wide[:, 0:1], 0.0).then_inc(sem("all_scattered"), 1)

        @block.tensor
        def _(pe):
            made = [0]
            mm, tr = nc.tensor.matmul, nc.tensor.transpose

            def begin(*name):
                n = number[name]
                assert n == made[0], (name, order[made[0]])
                made[0] += 1
                if n >= 8:
                    pe.wait_ge(banks_read[order[n - 8][1]], reader_count[n - 8])
                return psum[:, n % 8]

            def done(ins):
                ins.then_inc(product_ready, 1)

            def four(ps, t, lhs, rhs):
                for h in range(H):
                    last = mm(ps[:, P * h:P * h + P], lhs[:, t, h], rhs[:, t, h], start=True, stop=True)
                return last

            def modulation(b):
                ps = begin("mod", b)
                pe.wait_ge(sem("acc_ready"), b + 1)
                n = 512 if b < 4 else 256
                done(mm(ps[:, 0:n], ones, acc_ring[b % 2][:, 0:n], start=True, stop=True))

            pe.wait_ge(sem("consts"), 1)
            for b in range(4):
                modulation(b)
            for t in range(T):
                pe.wait_ge(sem("h_ready"), t + 1)
                for g in range(2):
                    ps = begin("hT", t, g)
                    for i in range(4):
                        last = tr(ps[:, P * i:P * i + P], h_ring[t % 2][:, P * (4 * g + i):P * (4 * g + i) + P], ident)
                    done(last)
            wait_read(pe, "hT", T - 1, 0)
            wait_read(pe, "hT", T - 1, 1)
            for c in range(13):
                ps = begin("zf", c)
                for i, s in ((0, "ld_w0"), (6, "ld_w1"), (10, "ld_w2")):
                    if c == i:
                        pe.wait_ge(sem(s), 16 if s != "ld_w2" else 80)
                for k in range(K):
                    if c < 6:
                        w = w_qkv[:, k, P * c:P * c + P]
                    elif c < 10:
                        w = w_b[:, k, P * (c - 6):P * (c - 6) + P]
                    else:
                        w = w_d[:, k, P * (c - 10):P * (c - 10) + P]
                    last = mm(ps, w, hT[:, k], start=k == 0, stop=k == K - 1)
                done(last)
                if c >= 5:
                    for i in range(2):
                        modulation(4 + 2 * (c - 5) + i)
            for s in ("ld_w3", "ld_w4", "ld_w5", "ld_w6"):
                pe.wait_ge(sem(s), 16)
            for t in range(T):
                for s, (w, _, n, _) in enumerate(zt_parts):
                    ps = begin("zt", t, s)
                    for k in range(K):
                        last = mm(ps[:, 0:n], hT[:, k, P * t:P * t + P], w[:, k, 0:n], start=k == 0, stop=k == K - 1)
                    done(last)
            pe.wait_ge(sem("silu_done"), 6)
            for nm, c0, nc_ in (("qk_tm", 0, 4), ("v_tm", 4, 2)):
                for t in range(T):
                    ps = begin(nm, t)
                    for i in range(nc_):
                        last = tr(ps[:, P * i:P * i + P], zpad[:, c0 + i, P * t:P * t + P], ident)
                    done(last)
            ps = begin("gcum")
            pe.wait_ge(sem("masks_ready"), 1)
            pe.wait_ge(sem("g_ready"), 1)
            done(mm(ps[:, 0:16], tri, g_.rearrange("p t h -> p (t h)"), start=True, stop=True))
            for t in range(T):
                ps = begin("grow", t)
                for h in range(H):
                    last = mm(ps[:, P * h:P * h + P], g_[:, t, h:h + 1].to_broadcast([P, P]), tri, start=True, stop=True)
                done(last)
            for nm, at_, s in (("kT", 4, "kn"), ("qT", 0, "qn")):
                for t in range(T):
                    ps = begin(nm, t)
                    pe.wait_ge(sem("qk_normed"), t + 1)
                    for h in range(H):
                        last = tr(ps[0:64, P * h:P * h + P], qkv_tm[:, t, 64 * (at_ + h):64 * (at_ + h) + 64], ident)
                    done(last)
            for nm, r_, cnt in (("kk", kT, "kT"), ("kq", qT, "qT")):
                for t in range(T):
                    ps = begin(nm, t)
                    wait_read(pe, cnt, t)
                    for h in range(H):
                        last = mm(ps[:, P * h:P * h + P], kT[0:64, t, h], r_[0:64, t, h], start=True, stop=True)
                    done(last)
            for t in range(T):
                ps = begin("M", t)
                wait_read(pe, "kk", t)
                for h in range(H):
                    last = tr(ps[:, P * h:P * h + P], Lf[:, t, h], ident)
                done(last)
            for nm, l_, r_ in (("L2", B1, B2), ("M2", B2, B1), ("L4", B4, B3)):
                for t in range(T):
                    ps = begin(nm, t)
                    if nm == "L2":
                        pe.wait_ge(sem("eights"), 2 * t + 2)
                    if nm == "L4":
                        wait_read(pe, "M2", t)
                    done(four(ps, t, l_, r_))
            for nm, l_ in (("Ra", B3), ("Rb", B1)):
                for t in range(T):
                    ps = begin(nm, t)
                    if nm == "Ra":
                        pe.wait_ge(sem("R_first"), t + 1)
                    else:
                        wait_read(pe, "L4", t)
                        wait_read(pe, "Ra", t)
                    done(four(ps, t, l_, R))
            for lv in range(3):
                for t in range(T):
                    ps = begin("Tm", lv, t)
                    wait_read(pe, *(("R", lv - 1, t) if lv else ("Rb", t)))
                    for h in range(H):
                        last = tr(ps[:, P * h:P * h + P], R[:, t, h], ident)
                    done(last)
                for t in range(T):
                    ps = begin("Z", lv, t)
                    pe.wait_ge(sem("level_masked"), T * lv + t + 1)
                    done(four(ps, t, B2, R))
                for t in range(T):
                    ps = begin("R", lv, t)
                    wait_read(pe, "Z", lv, t)
                    done(four(ps, t, B3, B4))
            for t in range(T):
                ps = begin("U", t)
                wait_read(pe, "R", 2, t)
                pe.wait_ge(sem("vb_ready"), t + 1)
                for h in range(H):
                    last = mm(ps[:, DH * h:DH * h + DH], R[:, t, h], vb[:, t, h], start=True, stop=True)
                done(last)
            for t in range(T):
                ps = begin("WT", t)
                for h in range(H):
                    last = mm(ps[0:64, P * h:P * h + P], kbe[:, t, h], R[:, t, h], start=True, stop=True)
                done(last)
            for t in range(T):
                ps = begin("QdT", t)
                pe.wait_ge(sem("Qd_ready"), t + 1)
                for h in range(H):
                    last = tr(ps[0:64, P * h:P * h + P], Qd[:, t, h], ident)
                done(last)
            wait_read(pe, "QdT", T - 1)
            for ch in range(2 * T):
                t, b = ch // 2, 64 * (ch % 2)
                ps = begin("WQ", ch)
                if ch:
                    wait_read(pe, "SU", ch - 1)
                else:
                    pe.wait_ge(sem("S_ready"), 1)
                for l_, c0 in ((WT, 0), (QdT, 256)):
                    for h in range(H):
                        last = mm(ps[b:b + 64, c0 + DH * h:c0 + DH * h + DH], l_[0:64, t, h, b:b + 64], S[0:64, h],
                                  start=True, stop=True)
                done(last)
                ps = begin("SU", ch)
                pe.wait_ge(sem("v_new_ready"), ch + 1)
                for h in range(H):
                    last = mm(ps[0:64, DH * h:DH * h + DH], ktail[b:b + 64, t, h], v_new[b:b + 64, t, h],
                              start=True, stop=True)
                done(last)
                if ch % 2:
                    ps = begin("AV", t)
                    for h in range(H):
                        last = mm(ps[:, DH * h:DH * h + DH], AT[:, t, h], v_new[:, t, h], start=True, stop=True)
                    done(last)
            def key_blocks(n):
                kind, t, _ = units[n]
                return list(range(t + 1)) if kind == "diff" else list(range(0 if t else 1, 2))

            def transposed(n):
                ps = begin("pT", n)
                pe.wait_ge(sem("p_ready"), n + 1)
                for i, b in enumerate(key_blocks(n)):
                    last = tr(ps[:, P * i:P * i + P], pc[n % 2][:, P * b:P * b + P], ident)
                done(last)

            def times_values(n):
                kind, t, h = units[n]
                blocks = key_blocks(n)
                ps = begin("pv", n)
                wait_read(pe, "pT", n)
                for i, b in enumerate(blocks):
                    v = bv[:, b, DH * h:DH * h + DH] if kind == "diff" else dv[:, t - 1 + b, DH * (h // 2):DH * (h // 2) + DH]
                    last = mm(ps[:, 0:DH], pT[n % 2][:, i], v, start=i == 0, stop=i == len(blocks) - 1)
                done(last)

            for n, (kind, t, h) in enumerate(units):
                if kind == "diff":
                    for m in range(2):
                        ps = begin("score", n, m)
                        b = 64 * (h % 2) + 32 * m
                        done(mm(ps[:, 0:P * (t + 1)], zb[b:b + 32, h // 2, P * t:P * t + P],
                                zb[b:b + 32, 2 + h // 2, 0:P * (t + 1)], start=True, stop=True))
                else:
                    ps = begin("score", n, 0)
                    b, u0 = 64 * (h // 2), 0 if t else P
                    done(mm(ps[:, u0:256], zb[b:b + 64, 4 + h % 2, P * t:P * t + P],
                            zb[b:b + 64, 6, P * (t - 1) + u0:P * (t + 1)], start=True, stop=True))
                if n >= 1:
                    transposed(n - 1)
                if n >= 2:
                    times_values(n - 2)
            transposed(len(units) - 1)
            times_values(len(units) - 2)
            times_values(len(units) - 1)
            ps = begin("sguT")
            pe.wait_ge(sem("ld_sgw"), 16)
            for g in range(H):
                last = tr(ps[:, P * g:P * g + P], sgw[:, g], ident)
            done(last)
            pe.wait_ge(sem("sgT_ready"), 1)
            pe.wait_ge(sem("vn_ready"), 1)
            for g in range(H):
                ps = begin("mix", g)
                done(mm(ps[:, 0:256], sgT[:, g], vn[:, :, g], start=True, stop=True))
            wait_read(pe, "mix", H - 1)
            for t in range(T):
                for g in range(2):
                    ps = begin("oT", t, g)
                    for i in range(4):
                        last = tr(ps[:, P * i:P * i + P], o_tm[:, t, P * (4 * g + i):P * (4 * g + i) + P], ident)
                    done(last)
            pe.wait_ge(sem("ld_wo"), 32)
            wait_read(pe, "oT", T - 1, 0)
            wait_read(pe, "oT", T - 1, 1)
            for t in range(T):
                for n in range(2):
                    ps = begin("y", t, n)
                    for k in range(K):
                        last = mm(ps, oT[:, k, P * t:P * t + P], w_o[n][:, k], start=k == 0, stop=k == K - 1)
                    done(last)
            for t in range(T):
                pe.wait_ge(sem("h2_ready"), t + 1)
                for g in range(2):
                    ps = begin("h2T", t, g)
                    for i in range(4):
                        last = tr(ps[:, P * i:P * i + P], h2_ring[t % 2][:, P * (4 * g + i):P * (4 * g + i) + P], ident)
                    done(last)
            wait_read(pe, "h2T", T - 1, 0)
            wait_read(pe, "h2T", T - 1, 1)
            pe.wait_ge(sem("ld_small2"), 48)
            for t in range(T):
                ps = begin("logit", t)
                for k in range(K):
                    last = mm(ps[:, 0:E], h2T[:, k, P * t:P * t + P], rw[:, k], start=k == 0, stop=k == K - 1)
                done(last)
            ps = begin("rank")
            pe.wait_ge(sem("chosen"), 1)
            pe.wait_ge(sem("before_ready"), 1)
            for t in range(T):
                for s in range(t + 1):
                    mm(ps[:, E * t:E * t + E], ones if s < t else before, mask[:, s], start=s == 0, stop=s == t)
            for s in range(T):
                last = mm(ps[:, E * T:E * T + E], ones, mask[:, s], start=s == 0, stop=s == T - 1)
            done(last)
            for who in ("act", "dve"):
                pe.wait_ge(banks_read[who], seen[who])
            for s, n in (("gate_made", 2), ("up_made", 2), ("y_made", 4)):
                pe.sem_inc(sem(s), n)

            def transpose_rows(r, p, j):
                b = j % 2
                pe.wait_ge(sem(f"ld_xg{b}"), nth_of_half(pe, 16, r, p, j, 16))
                pe.wait_ge(sem("xT_act"), nth(pe, 1, r, p, j, 1))
                pe.wait_ge(sem("xT_dve"), nth(pe, 1, r, p, j, 1))
                for k in range(K):
                    last = tr(psum[:, k // 4, P * (k % 4):P * (k % 4) + P], xg[b][:, P * k:P * k + P], ident)
                    if k % 4 == 3:
                        last.then_inc(sem("xT_made"), 1)

            def gate(r, p, j):
                b = j % 2
                pe.wait_ge(sem("xT_act"), nth(pe, 1, r, p, j, 2))
                pe.wait_ge(sem("xT_dve"), nth(pe, 1, r, p, j, 2))
                pe.wait_ge(sem(f"ld_w_gate{b}"), nth_of_half(pe, 16, r, p, j, 16))
                pe.wait_ge(sem("silu_made"), nth(pe, 1, r, p, j, 1))
                for k in range(K):
                    last = mm(psum[:, 2], xgT[b][:, k], w_exp[b][0][:, k], start=k == 0, stop=k == K - 1)
                last.then_inc(sem("gate_made"), 1)

            def up(r, p, j):
                b = j % 2
                pe.wait_ge(sem(f"ld_w_up{b}"), nth_of_half(pe, 16, r, p, j, 16))
                pe.wait_ge(sem("he_made"), nth(pe, 1, r, p, j, 1))
                for k in range(K):
                    last = mm(psum[:, 3], xgT[b][:, k], w_exp[b][1][:, k], start=k == 0, stop=k == K - 1)
                last.then_inc(sem("up_made"), 1)

            def transpose_hidden(r, p, j):
                b = j % 2
                pe.wait_ge(sem("he_made"), nth(pe, 1, r, p, j, 2))
                pe.wait_ge(sem("heT_copied"), nth(pe, 1, r, p, j, 1))
                for k in range(4):
                    last = tr(psum[:, 4, P * k:P * k + P], he[b][:, P * k:P * k + P], ident)
                last.then_inc(sem("heT_made"), 1)

            def down(r, p, j):
                b = j % 2
                pe.wait_ge(sem(f"ld_w_down{b}"), nth_of_half(pe, 16, r, p, j, 16))
                pe.wait_ge(sem("heT_copied"), nth(pe, 1, r, p, j, 2))
                pe.wait_ge(sem("y_read_act"), nth(pe, 1, r, p, j, 1))
                pe.wait_ge(sem("y_read_dve"), nth(pe, 1, r, p, j, 1))
                for n in range(2):
                    for k in range(4):
                        last = mm(psum[:, 5 + n], heT[b][:, k], w_exp[b][2][:, k, 512 * n:512 * n + 512], start=k == 0, stop=k == 3)
                    last.then_inc(sem("y_made"), 1)

            def first(r):
                transpose_rows(r, 0, 0)
                gate(r, 0, 0)
                up(r, 0, 0)
                transpose_rows(r, 0, 1)

            def step(r, p, j):
                gate(r, p, j)
                transpose_hidden(r, p, j - 1)
                up(r, p, j)
                transpose_rows(r, p, j + 1)
                down(r, p, j - 1)

            def last(r):
                gate(r, 0, E - 1)
                transpose_hidden(r, 0, E - 2)
                up(r, 0, E - 1)
                down(r, 0, E - 2)
                transpose_hidden(r, 0, E - 1)
                down(r, 0, E - 1)

            in_steps(pe, 0, first, step, last)
            pe.wait_ge(sem("rounds_ready"), 1)
            n_rounds = pe.value_load(rounds[0:1, 0:1], min_val=1, max_val=4)
            with pe.If(n_rounds > 1):
                with pe.Fori(1, n_rounds) as r:
                    in_steps(pe, r, first, step, last)

        @block.scalar
        def _(act):
            link = chain(act, sem("scalar_step"))
            A = nc.scalar.activation

            def copied(dst, name, view, func=ACT.Copy, **kw):
                wait_product(act, *name)
                link(A(dst, view, func, **kw), banks_read["act"])

            def rsqrt(dst, src, scale, signal):
                link(A(dst, src, ACT.Ln, bias=eps[:, 0:1], scale=scale))
                link(A(dst, dst, ACT.Exp, scale=-0.5), signal)

            act.wait_ge(sem("consts"), 1)
            act.wait_ge(sem("ld_c"), 16)
            link(A(acol, ccol, ACT.Silu), sem("c_ready"))
            act.wait_ge(sem("ld_x"), 16)
            for t in range(T):
                link(A(squares, x[:, t], ACT.Square, accum_out=ss[:, t:t + 1]))
            rsqrt(rs, ss, 1.0 / D, sem("rs1_ready"))
            for b in range(4):
                copied(mod1[:, b // 2, 512 * (b % 2):512 * (b % 2) + 512], ("mod", b), bank("mod", b))
            for t in range(T):
                copied(hT[:, 4:8, P * t:P * t + P], ("hT", t, 1), bank("hT", t, 1).rearrange("p (k n) -> p k n", k=4))
            act.wait_ge(sem("ld_bcol"), 16 * 7)
            act.wait_ge(sem("pads"), 1)
            for c in range(13):
                dst = zpad[:, c, 3:3 + SEQ] if c < 6 else zb[:, c - 6]
                copied(dst, ("zf", c), bank("zf", c), func=ACT.Identity, bias=bcol[:, c:c + 1])
                if c >= 5:
                    for b in range(4 + 2 * (c - 5), 6 + 2 * (c - 5)):
                        m = b - 4
                        copied(mod2[:, m // 4, 256 * (m % 4):256 * (m % 4) + 256], ("mod", b), bank("mod", b)[:, 0:256])
                if 3 <= c < 9:
                    act.wait_ge(sem("conv_ready"), c - 2)
                    link(A(zpad[:, c - 3, 0:SEQ], cring[(c - 3) % 2], ACT.Silu), sem("silu_done"))
            for t in range(T):
                wait_read(act, "zt", t, 3)
                A(gab[:, t, 0:256], gab[:, t, 0:256], ACT.Silu).then_inc(sem("gate_silu"), 1)
            for t in range(T):
                A(uv[:, t], uv[:, t], ACT.Gelu_apprx_tanh).then_inc(sem("gelu"), 1)
            act.wait_ge(sem("alpha_abs"), 1)
            link(A(tA, tA, ACT.Exp, scale=-1.0))
            link(A(tA, tA, ACT.Ln, bias=1.0))
            link(A(alog, alog, ACT.Exp))
            link(A(tB, gab[:, :, 260:264], ACT.Exp, scale=-1.0), sem("softplus"))
            for t in range(T):
                copied(qkv_tm[:, t, 0:512], ("qk_tm", t), bank("qk_tm", t))
            for t in range(T):
                copied(qkv_tm[:, t, 512:768], ("v_tm", t), bank("v_tm", t)[:, 0:256])
            act.wait_ge(sem("qk_squares"), T)
            rsqrt(nrs, nss, 1.0, sem("qk_rs"))
            wait_read(act, "gcum")
            link(A(egc, gc, ACT.Exp), sem("egc_ready"))
            for t in range(T):
                act.wait_ge(sem("gdiff"), t + 1)
                link(A(B1[:, t], B1[:, t], ACT.Exp, scale=-1.0), sem("decay"))
                link(A(AT[:, t], AT[:, t], ACT.Exp), sem("decay"))
            link(A(etail, etail, ACT.Exp))
            link(A(egl, glast, ACT.Exp), sem("tails"))
            for nm, dst in (("kT", kT), ("qT", qT)):
                for t in range(T):
                    copied(dst[0:64, t], (nm, t), bank(nm, t)[0:64].rearrange("p (h n) -> p h n", h=H))

            def heads(*name):
                return bank(*name).rearrange("p (h n) -> p h n", h=H)

            for t in range(T):
                copied(B4[:, t], ("M", t), heads("M", t))
            for nm, dst in (("L2", B3), ("M2", B4), ("L4", B1)):
                for t in range(T):
                    if nm == "L4":
                        act.wait_ge(sem("R_first"), t + 1)
                    copied(dst[:, t], (nm, t), heads(nm, t))
            for lv in range(3):
                for nm, dst in (("Tm", B3), ("Z", B4)):
                    for t in range(T):
                        copied(dst[:, t], (nm, lv, t), heads(nm, lv, t))
            for t in range(T):
                copied(U[:, t], ("U", t), bank("U", t)[:, 0:256].rearrange("p (h n) -> p h n", h=H))
            act.wait_ge(sem("level_masked"), 3 * T)
            for nm, dst in (("WT", WT), ("QdT", QdT)):
                for t in range(T):
                    copied(dst[0:64, t], (nm, t), bank(nm, t)[0:64].rearrange("p (h n) -> p h n", h=H))
            act.wait_ge(sem("gdn_squares"), 1)
            rsqrt(nrs.rearrange("p t n -> p (t n)")[:, 0:16], nss.rearrange("p t n -> p (t n)")[:, 0:16], 1.0 / DH, sem("gdn_rs"))
            act.wait_ge(sem("lam_sums"), 1)
            link(A(lam[:, 0:2], lam[:, 0:2], ACT.Exp), sem("lam_exp"))
            for n, (kind, t, h) in enumerate(units):
                cols = slice(0, P * (t + 1)) if kind == "diff" else slice(0 if t else P, 256)
                for m in range(2 if kind == "diff" else 1):
                    act.wait_ge(sem("max_ready"), maxes[n] + m + 1)
                    link(A(p_sb[n % 2][m][:, cols], s_sb[n % 2][m][:, cols], ACT.Exp, bias=mx[:, n % 2, 2 + m:3 + m],
                           accum_out=mx[:, n % 2, 4 + m:5 + m]), sem("exp_ready"))
                if kind == "swa":
                    link(A(mx[:, n % 2, 5:6], sink[:, h:h + 1], ACT.Exp, bias=mx[:, n % 2, 2:3]), sem("exp_ready"))
                if n >= 1:
                    nb = n_blocks[n - 1]
                    copied(pT[(n - 1) % 2][:, 0:nb], ("pT", n - 1), bank("pT", n - 1)[:, 0:P * nb].rearrange("p (k n) -> p k n", n=P))
            n = len(units)
            nb = n_blocks[n - 1]
            copied(pT[(n - 1) % 2][:, 0:nb], ("pT", n - 1), bank("pT", n - 1)[:, 0:P * nb].rearrange("p (k n) -> p k n", n=P))
            for i in range(2):
                act.wait_ge(sem("o_squares"), i + 1)
                rsqrt(nrs.rearrange("p t n -> p (t n)")[:, 0:16], nss.rearrange("p t n -> p (t n)")[:, 0:16], 1.0 / DH, sem("o_rs"))
            for t in range(T):
                copied(oT[:, 4:8, P * t:P * t + P], ("oT", t, 1), bank("oT", t, 1).rearrange("p (k n) -> p k n", k=4))
            for t in range(T):
                act.wait_ge(sem("x1_ready"), 2 * t + 2)
                link(A(junk1k, x[:, t], ACT.Square, accum_out=ss[:, t:t + 1]))
                rsqrt(rs[:, t:t + 1], ss[:, t:t + 1], 1.0 / D, sem("rs2_ready"))
            for t in range(T):
                copied(h2T[:, 4:8, P * t:P * t + P], ("h2T", t, 1), bank("h2T", t, 1).rearrange("p (k n) -> p k n", k=4))
            wait_read(act, "logit", T - 1)
            link(A(scores, scores, ACT.Exp, scale=-1.0), sem("exp_logits"))
            for s in ("xT_act", "silu_made", "heT_copied", "y_read_act"):
                act.sem_inc(sem(s), 1)

            def copy_rows(r, p, j):
                act.wait_ge(sem("xT_made"), nth(act, 2, r, p, j, 1))
                A(xgT[j % 2][:, 0:4], psum[:, 0].rearrange("p (k n) -> p k n", n=P), ACT.Copy).then_inc(sem("xT_act"), 1)

            def silu(r, p, j):
                act.wait_ge(sem("gate_made"), nth(act, 1, r, p, j, 3))
                A(gated[j % 2], psum[:, 2], ACT.Silu).then_inc(sem("silu_made"), 1)

            def copy_hidden(r, p, j):
                act.wait_ge(sem("heT_made"), nth(act, 1, r, p, j, 1))
                A(heT[j % 2], psum[:, 4].rearrange("p (k n) -> p k n", n=P), ACT.Copy).then_inc(sem("heT_copied"), 1)

            def copy_y(r, p, j):
                b = j % 2
                act.wait_ge(sem("y_made"), nth(act, 2, r, p, j, 5))
                act.wait_ge(sem(f"slot_free{b}"), nth_of_half(act, 1, r, p, j, 1))
                A(yo[b][:, 0:512], psum[:, 5], ACT.Copy).then_inc(sem("y_read_act"), 1)

            def first(r):
                copy_rows(r, 0, 0)
                silu(r, 0, 0)
                copy_rows(r, 0, 1)

            def step(r, p, j):
                silu(r, p, j)
                copy_hidden(r, p, j - 1)
                copy_rows(r, p, j + 1)
                copy_y(r, p, j - 1)

            def last(r):
                silu(r, 0, E - 1)
                for j in (E - 2, E - 1):
                    copy_hidden(r, 0, j)
                    copy_y(r, 0, j)

            in_steps(act, 0, first, step, last)
            act.wait_ge(sem("rounds_ready"), 1)
            n_rounds = act.value_load(rounds[0:1, 0:1], min_val=1, max_val=4)
            with act.If(n_rounds > 1):
                with act.Fori(1, n_rounds) as r:
                    in_steps(act, r, first, step, last)
            for t in range(T):
                act.wait_ge(sem("x2_ready"), t + 1)
                link(A(junk_last, x[:, t], ACT.Square, accum_out=ss[:, t:t + 1]))
                rsqrt(rs[:, t:t + 1], ss[:, t:t + 1], 1.0 / D, sem("rs3_ready"))

        @block.vector
        def _(dve):
            link = chain(dve, sem("vector_step"))
            v = nc.vector
            TT, TS, STT = v.tensor_tensor, v.tensor_scalar, v.scalar_tensor_tensor

            def read(ins):
                link(ins, banks_read["dve"])

            def conv(c):
                wait_read(dve, "zf", c)
                if c == 0:
                    dve.wait_ge(sem("ld_conv"), 64)
                if c >= 2:
                    dve.wait_ge(sem("silu_done"), c - 1)
                y = cring[c % 2]
                link(TS(y, zpad[:, c, 0:SEQ], convc[:, c, 0:1], None, ALU.mult))
                for i in range(1, 4):
                    ins = STT(y, zpad[:, c, i:i + SEQ], convc[:, c, i:i + 1], y, ALU.mult, ALU.add)
                    link(ins, sem("conv_ready") if i == 3 else sem("vector_step"))

            def ada(b):
                if b < 4:
                    w, n, br = ada_first[b], 512, brow_first
                    dve.wait_ge(sem(f"ld_ada{b}"), 16)
                else:
                    w, n, br = ada_rest[b % 2], 256, brow[b % 2]
                    dve.wait_ge(sem(f"ld_adar{b % 2}"), 32 * (b // 2 - 1))
                if b >= 2:
                    wait_product(dve, "mod", b - 2)
                acc = acc_ring[b % 2][:, 0:n]
                link(TS(acc, w[:, 0], acol[:, 0:1], None, ALU.mult))
                for j in range(1, 8):
                    link(STT(acc, w[:, j], acol[:, j:j + 1], acc, ALU.mult, ALU.add))
                if b < 4:
                    dve.wait_ge(sem("ld_brow"), 16 * (b + 1))
                link(TT(acc[0:1], acc[0:1], br[0:1], ALU.add), sem("acc_ready"))

            dve.wait_ge(sem("c_ready"), 1)
            for b in range(4):
                ada(b)
            dve.wait_ge(sem("ld_n1"), 16)
            wait_read(dve, "mod", 3)
            link(STT(mod1[:, 1], mod1[:, 1], 1.0, n1bc, ALU.add, ALU.mult))
            dve.wait_ge(sem("rs1_ready"), 1)
            dve.wait_ge(sem("ld_x"), 16)
            for t in range(T):
                if t >= 2:
                    wait_product(dve, "hT", t - 2, 1)
                hr = h_ring[t % 2]
                link(STT(hr, x[:, t], rs[:, t:t + 1], mod1[:, 1], ALU.mult, ALU.mult))
                link(TT(hr, hr, mod1[:, 0], ALU.add), sem("h_ready"))
                if t:
                    wait_product(dve, "hT", t - 1, 0)
                    read(v.tensor_copy(hT[:, 0:4, P * (t - 1):P * t], bank("hT", t - 1, 0).rearrange("p (k n) -> p k n", k=4)))
            wait_product(dve, "hT", T - 1, 0)
            read(v.tensor_copy(hT[:, 0:4, P * (T - 1):P * T], bank("hT", T - 1, 0).rearrange("p (k n) -> p k n", k=4)))
            for c in range(4):
                conv(c)
            for c in range(5, 13):
                for i in range(2):
                    ada(4 + 2 * (c - 5) + i)
                if c < 7:
                    conv(c - 1)
            dve.wait_ge(sem("ld_btm"), 64)
            parts = ((gab, 0, 264, 0), (None, 0, 512, 264), (uv, 256, 256, 776), (dv, 0, P, 1032))
            for t in range(T):
                for s, (dst, c0, n, o) in enumerate(parts):
                    wait_product(dve, "zt", t, s)
                    ps = bank("zt", t, s)
                    if s == 1:
                        link(TT(bv[:, t], ps[:, 0:256], btm[:, 264:520], ALU.add))
                        read(TT(uv[:, t, 0:256], ps[:, 256:512], btm[:, 520:776], ALU.add))
                    else:
                        read(TT(dst[:, t, c0:c0 + n], ps[:, 0:n], btm[:, o:o + n], ALU.add))
            dve.wait_ge(sem("ld_small"), 16 * 10)
            link(TT(tC, gab[:, :, 256:260], dtb.unsqueeze(1).to_broadcast([P, T, H]), ALU.add))
            link(STT(tA, tC, -1.0, tC, ALU.mult, ALU.max), sem("alpha_abs"))
            dve.wait_ge(sem("softplus"), 1)
            link(STT(tC, tC, 0.0, tA, ALU.max, ALU.add))
            link(TS(alog, alog, -1.0, None, ALU.mult))
            link(TT(g_, tC, alog.unsqueeze(1).to_broadcast([P, T, H]), ALU.mult), sem("g_ready"))
            link(TS(tB, tB, 1.0, None, ALU.add))
            link(v.reciprocal(beta, tB))
            sqf = sq.rearrange("p t n -> p (t n)")
            for t in range(T):
                wait_read(dve, "qk_tm", t)
                link(TT(sqf[:, 0:512], qkv_tm[:, t, 0:512], qkv_tm[:, t, 0:512], ALU.mult))
                ins = v.tensor_reduce(nss[:, t], sqf[:, 0:512].rearrange("p (n d) -> p n d", d=DH), AX.X, ALU.add)
                link(ins, sem("qk_squares"))
            dve.wait_ge(sem("qk_rs"), 1)
            link(TS(nrs[:, :, 0:4], nrs[:, :, 0:4], DH ** -0.5, None, ALU.mult))
            for t in range(T):
                qk = qkv_tm[:, t, 0:512].rearrange("p (n d) -> p n d", d=DH)
                link(TT(qk, qk, nrs[:, t].unsqueeze(2).to_broadcast([P, 8, DH]), ALU.mult), sem("qk_normed"))
            wait_product(dve, "gcum")
            read(v.tensor_copy(gc.rearrange("p t h -> p (t h)"), bank("gcum")[:, 0:16]))
            for t in range(T):
                wait_product(dve, "grow", t)
                ps = bank("grow", t).rearrange("p (h n) -> p h n", h=H)
                link(v.tensor_copy(glast[:, t], ps[:, :, 63::64]))
                read(TT(B1[:, t], ps, over_heads(gc[:, t], P), ALU.subtract))
                link(TS(AT[:, t], B1[:, t], 0.0, None, ALU.min))
                if t == T - 1:
                    for b in range(2):
                        r_ = slice(64 * b, 64 * b + 64)
                        link(TT(etail[r_], glast[r_, :, :, b], gc[r_], ALU.subtract))
                link(TS(B1[:, t], B1[:, t], 0.0, None, ALU.max), sem("gdiff"))

            def heads(*name):
                return bank(*name).rearrange("p (h n) -> p h n", h=H)

            for t in range(T):
                dve.wait_ge(sem("decay_masked"), 2 * t + 2)
                wait_product(dve, "kk", t)
                read(TT(Lf[:, t], heads("kk", t), B1[:, t], ALU.mult))
            for t in range(T):
                wait_product(dve, "kq", t)
                read(TT(AT[:, t], heads("kq", t), AT[:, t], ALU.mult))
            k_tm = qkv_tm[:, :, 256:512].rearrange("p t (h d) -> p t h d", d=DH)
            q_tm = qkv_tm[:, :, 0:256].rearrange("p t (h d) -> p t h d", d=DH)
            v_tm = qkv_tm[:, :, 512:768].rearrange("p t (h d) -> p t h d", d=DH)
            dve.wait_ge(sem("egc_ready"), 1)
            for t in range(T):
                link(TT(Qd[:, t], q_tm[:, t], over_heads(egc[:, t], DH), ALU.mult), sem("Qd_ready"))
            link(v.memset(S[0:64], 0.0), sem("S_ready"))
            for nm in ("Ra", "Rb"):
                for t in range(T):
                    wait_product(dve, nm, t)
                    read(TT(R[:, t], heads(nm, t), R[:, t], ALU.add))
            wait_read(dve, "v_tm", T - 1)
            for t in range(T):
                link(TT(vb[:, t], v_tm[:, t], over_heads(beta[:, t], DH), ALU.mult))
                link(TT(kbe[:, t], k_tm[:, t], over_heads(beta[:, t], DH), ALU.mult))
                link(TT(kbe[:, t], kbe[:, t], over_heads(egc[:, t], DH), ALU.mult), sem("vb_ready"))
            for lv in range(3):
                for t in range(T):
                    wait_product(dve, "R", lv, t)
                    read(TT(R[:, t], R[:, t], heads("R", lv, t), ALU.subtract))
            dve.wait_ge(sem("tails"), 1)
            for t in range(T):
                link(TT(ktail[:, t], k_tm[:, t], over_heads(etail[:, t], DH), ALU.mult))
            wait_read(dve, "U", T - 1)
            for ch in range(2 * T):
                t, b = ch // 2, 64 * (ch % 2)
                r_ = slice(b, b + 64)
                wait_product(dve, "WQ", ch)
                ps = bank("WQ", ch)[r_]
                link(TT(v_new[r_, t], U[r_, t], ps[:, 0:256].rearrange("p (h d) -> p h d", h=H), ALU.subtract), sem("v_new_ready"))
                read(v.tensor_copy(qs[r_, t], ps[:, 256:512].rearrange("p (h d) -> p h d", h=H)))
                link(TT(Stmp[0:64], S[0:64], egl[0:64, t, :, ch % 2].unsqueeze(2).to_broadcast([64, H, DH]), ALU.mult))
                wait_product(dve, "SU", ch)
                read(TT(S[0:64], Stmp[0:64], bank("SU", ch)[0:64, 0:256].rearrange("p (h d) -> p h d", h=H), ALU.add))
                if ch % 2:
                    wait_product(dve, "AV", t)
                    read(TT(o_tm[:, t, 0:256], qs[:, t].rearrange("p h d -> p (h d)"), bank("AV", t)[:, 0:256], ALU.add))

            nss16 = nss.rearrange("p t n -> p (t n)")[:, 0:16]
            nrs16 = nrs.rearrange("p t n -> p (t n)")[:, 0:16]

            def head_norm(view, gain, scale, squares_sem, rs_sem, count, final=None):
                link(TT(sq, view, view, ALU.mult))
                link(v.tensor_reduce(nss16, sq.rearrange("p t (h d) -> p (t h) d", d=DH), AX.X, ALU.add), squares_sem)
                dve.wait_ge(rs_sem, count)
                if scale != 1.0:
                    link(TS(nrs16, nrs16, scale, None, ALU.mult))
                for t in range(T):
                    o = view[:, t].rearrange("p (h d) -> p h d", d=DH)
                    link(TT(o, o, over_heads(nrs16[:, 4 * t:4 * t + 4], DH), ALU.mult))
                    link(TT(o, o, gain, ALU.mult))

            head_norm(o_tm[:, :, 0:256], per_head(gnorm), 1.0, sem("gdn_squares"), sem("gdn_rs"), 1)
            dve.wait_ge(sem("gate_silu"), T)
            link(TT(o_tm[:, :, 0:256], o_tm[:, :, 0:256], gab[:, :, 0:256], ALU.mult), sem("gdn_done"))
            link(TT(lamt[:, 0], lam4[:, 0], lam4[:, 1], ALU.mult))
            link(TT(lamt[:, 1], lam4[:, 2], lam4[:, 3], ALU.mult))
            link(v.tensor_reduce(lam[:, 0:2], lamt, AX.X, ALU.add), sem("lam_sums"))
            dve.wait_ge(sem("lam_exp"), 1)
            link(TT(lam[:, 2:3], lam[:, 1:2], lam[:, 0:1], ALU.subtract))
            link(TS(neglam, lam[:, 2:3], -LAM_INIT, None, ALU.add))
            dve.wait_ge(sem("biases"), 1)

            def spread(n):
                kind, t, h = units[n]
                return kind, t, h, slice(0, P * (t + 1)) if kind == "diff" else slice(0 if t else P, 256), mx[:, n % 2]

            def maxima(n):
                kind, t, h, cols, m8 = spread(n)
                for m in range(2 if kind == "diff" else 1):
                    wait_product(dve, "score", n, m)
                    bias = bias_diff[:, h, P * (3 - t):] if kind == "diff" else bias_swa[:, h, cols]
                    read(v.tensor_tensor_reduce(out=s_sb[n % 2][m][:, cols], in0=bank("score", n, m)[:, cols], in1=bias,
                                                scale=32 ** -0.5 if kind == "diff" else DH ** -0.5, scalar=-3e38,
                                                op0=ALU.add, op1=ALU.max, accum_out=m8[:, m:m + 1]))
                    if kind == "swa":
                        link(TT(m8[:, 0:1], m8[:, 0:1], sink[:, h:h + 1], ALU.max))
                    link(TS(m8[:, 2 + m:3 + m], m8[:, m:m + 1], -1.0, None, ALU.mult), sem("max_ready"))

            def weights(n):
                kind, t, h, cols, m8 = spread(n)
                dve.wait_ge(sem("exp_ready"), 2 * n + 2)
                if n >= 2:
                    wait_product(dve, "pT", n - 2)
                p0, p1 = (p_sb[n % 2][m][:, cols] for m in range(2))
                if kind == "diff":
                    link(v.reciprocal(m8[:, 6:8], m8[:, 4:6]))
                    link(TT(m8[:, 7:8], m8[:, 7:8], neglam, ALU.mult))
                    link(TS(p1, p1, m8[:, 7:8], None, ALU.mult))
                    link(STT(pc[n % 2][:, cols], p0, m8[:, 6:7], p1, ALU.mult, ALU.add), sem("p_ready"))
                else:
                    link(TT(m8[:, 4:5], m8[:, 4:5], m8[:, 5:6], ALU.add))
                    link(v.reciprocal(m8[:, 6:7], m8[:, 4:5]))
                    link(TS(pc[n % 2][:, cols], p0, m8[:, 6:7], None, ALU.mult), sem("p_ready"))

            def outputs(n):
                kind, t, h, cols, m8 = spread(n)
                c0 = (256 if kind == "diff" else 768) + DH * h
                wait_product(dve, "pv", n)
                read(v.tensor_copy(o_tm[:, t, c0:c0 + DH], bank("pv", n)[:, 0:DH]))

            n = len(units)
            for i in range(n):
                maxima(i)
                if i >= 1:
                    weights(i - 1)
                if i >= 2:
                    outputs(i - 2)
            weights(n - 1)
            outputs(n - 2)
            outputs(n - 1)
            head_norm(o_tm[:, :, 256:512], per_head(dnorm), 1.0 - LAM_INIT, sem("o_squares"), sem("o_rs"), 1)
            dve.wait_ge(sem("gelu"), T)
            dve.wait_ge(sem("ld_small2"), 48)
            head_norm(uv[:, :, 256:512], snorm.rearrange("p (h d) -> p h d", d=DH), 1.0, sem("o_squares"), sem("o_rs"), 2)
            link(v.tensor_copy(vn.rearrange("p t h d -> p t (h d)"), uv[:, :, 256:512]), sem("vn_ready"))
            wait_product(dve, "sguT")
            read(v.tensor_copy(sgT.rearrange("p h n -> p (h n)"), bank("sguT")))
            link(v.memset(sgT[64:128, :, 0:64], 0.0), sem("sgT_ready"))
            for g in range(H):
                wait_product(dve, "mix", g)
                ins = STT(o_tm[:, :, 512 + DH * g:512 + DH * g + DH], bank("mix", g)[:, 0:256].rearrange("p (t d) -> p t d", t=T),
                          sgb[:, g:g + 1], uv[:, :, DH * g:DH * g + DH], ALU.add, ALU.mult)
                read(ins)
            for t in range(T):
                wait_product(dve, "oT", t, 0)
                read(v.tensor_copy(oT[:, 0:4, P * t:P * t + P], bank("oT", t, 0).rearrange("p (k n) -> p k n", k=4)))
            dve.wait_ge(sem("x_biased"), T)
            dve.wait_ge(sem("ld_n2"), 16)
            link(STT(mod2[:, 2], mod2[:, 2], 1.0, n2bc, ALU.add, ALU.mult))
            for t in range(T):
                for n in range(2):
                    cols = slice(512 * n, 512 * n + 512)
                    wait_product(dve, "y", t, n)
                    read(TT(ytmp[n], bank("y", t, n), mod2[:, 0, cols], ALU.mult))
                    ins = TT(x[:, t, cols], x[:, t, cols], ytmp[n], ALU.add)
                    link(ins, sem("x1_ready"))
            for t in range(T):
                dve.wait_ge(sem("rs2_ready"), t + 1)
                if t >= 2:
                    wait_product(dve, "h2T", t - 2, 1)
                    dve.wait_ge(sem(f"st_h2{t % 2}"), 16)
                hr = h2_ring[t % 2]
                link(STT(hr, x[:, t], rs[:, t:t + 1], mod2[:, 2], ALU.mult, ALU.mult))
                link(TT(hr, hr, mod2[:, 1], ALU.add), sem("h2_ready"))
                if t:
                    wait_product(dve, "h2T", t - 1, 0)
                    read(v.tensor_copy(h2T[:, 0:4, P * (t - 1):P * t], bank("h2T", t - 1, 0).rearrange("p (k n) -> p k n", k=4)))
            wait_product(dve, "h2T", T - 1, 0)
            read(v.tensor_copy(h2T[:, 0:4, P * (T - 1):P * T], bank("h2T", T - 1, 0).rearrange("p (k n) -> p k n", k=4)))
            for t in range(T):
                wait_product(dve, "logit", t)
                read(v.tensor_copy(scores[:, t], bank("logit", t)[:, 0:E]))
            dve.wait_ge(sem("exp_logits"), 1)
            dve.wait_ge(sem("router_consts"), 1)
            link(TS(scores, scores, 1.0, None, ALU.add))
            link(v.reciprocal(scores, scores))
            link(TT(sel, scores, rb.unsqueeze(1).to_broadcast([P, T, E]), ALU.add))
            s4 = sel.rearrange("p t (g e) -> p t g e", e=4)
            hi1, hi2, lo1, lo2, top1, top2, gs, eq, geq, best = grp[:10]
            link(TT(hi1, s4[:, :, :, 0], s4[:, :, :, 1], ALU.max))
            link(TT(lo1, s4[:, :, :, 0], s4[:, :, :, 1], ALU.min))
            link(TT(hi2, s4[:, :, :, 2], s4[:, :, :, 3], ALU.max))
            link(TT(lo2, s4[:, :, :, 2], s4[:, :, :, 3], ALU.min))
            link(TT(top1, hi1, hi2, ALU.max))
            link(TT(top2, hi1, hi2, ALU.min))
            link(TT(lo1, lo1, lo2, ALU.max))
            link(TT(top2, top2, lo1, ALU.max))
            link(TT(gs, top1, top2, ALU.add))

            def first_best(dst, val, weight, c, tmp, n):
                link(v.tensor_reduce(c, val, AX.X, ALU.max))
                link(TT(tmp, val, c.unsqueeze(2).to_broadcast([P, T, n]), ALU.is_equal))
                link(TT(tmp, tmp, weight, ALU.mult))
                link(v.tensor_reduce(c, tmp, AX.X, ALU.max))
                link(TT(dst, tmp, c.unsqueeze(2).to_broadcast([P, T, n]), ALU.is_equal))

            first_best(best, gs, gw, col[0], eq, 4)
            link(TS(geq, best, NEG, -NEG, ALU.mult, ALU.add))
            m4 = m16.rearrange("p t (g e) -> p t g e", e=4)
            for t in range(T):
                link(TT(m4[:, t], s4[:, t], best[:, t].unsqueeze(2).to_broadcast([P, 4, 4]), ALU.mult))
                link(TT(m4[:, t], m4[:, t], geq[:, t].unsqueeze(2).to_broadcast([P, 4, 4]), ALU.add))
            first_best(one1, m16, eweight, col[0], u16, E)
            link(STT(sel2, one1, -NEG, m16, ALU.mult, ALU.add))
            first_best(one2, sel2, eweight, col[0], u16, E)
            link(TT(mask, one1, one2, ALU.add), sem("chosen"))
            for k, one in enumerate((one1, one2)):
                link(TT(u16, one, scores, ALU.mult))
                link(v.tensor_reduce(wtok[:, k], u16, AX.X, ALU.add))
            link(TT(col[1], wtok[:, 0], wtok[:, 1], ALU.add))
            link(v.reciprocal(col[2], col[1]))
            for k in range(2):
                link(TT(wtok[:, k], wtok[:, k], col[2], ALU.mult))
            wait_product(dve, "rank")
            link(v.tensor_copy(rank.rearrange("p t e -> p (t e)"), bank("rank")[:, 0:E * T]))
            read(v.tensor_copy(counts, bank("rank")[:, E * T:E * T + E]))
            link(TS(u16, rank, 128.0, None, ALU.is_ge))
            for n in (256.0, 384.0):
                link(TS(v16, rank, n, None, ALU.is_ge))
                link(TT(u16, u16, v16, ALU.add))
            link(TS(u16, u16, 16.0 - 80.0 * P, None, ALU.mult))
            link(STT(v16, rank, 80.0, u16, ALU.mult, ALU.add))
            link(TT(v16, v16, eidx, ALU.add))
            for k, one in enumerate((one1, one2)):
                link(TT(u16, one, v16, ALU.mult))
                ins = v.tensor_reduce(col[4 + k], u16, AX.X, ALU.add)
                link(ins)
                ins = v.tensor_copy(iscat[:, k], col[4 + k])
                link(ins, sem("places_ready"))
            link(v.tensor_reduce(col[6][:, 0:1], counts, AX.X, ALU.max))
            link(TS(col[7][:, 0:1], col[6][:, 0:1], 128.0, 1.0, ALU.is_gt, ALU.add))
            for n in (256.0, 384.0):
                link(TS(col[8][:, 0:1], col[6][:, 0:1], n, None, ALU.is_gt))
                link(TT(col[7][:, 0:1], col[7][:, 0:1], col[8][:, 0:1], ALU.add))
            link(v.tensor_copy(rounds, col[7][:, 0:1]), sem("rounds_ready"))
            dve.wait_ge(sem("ld_table"), 16)
            link(TS(tokens, table, 1, None, ALU.logical_shift_right))
            for s in ("xT_dve", "he_made", "y_read_dve"):
                dve.sem_inc(sem(s), 1)

            def gather_indices(r, p, j):
                v.tensor_copy(idx_g[j % 2], tokens[:, bass.ds(nth(dve, 1, r, p, j, 0), 1)]).then_inc(sem(f"idx_ready{j % 2}"), 1)

            def copy_rows(r, p, j):
                dve.wait_ge(sem("xT_made"), nth(dve, 2, r, p, j, 2))
                v.tensor_copy(xgT[j % 2][:, 4:8], psum[:, 1].rearrange("p (k n) -> p k n", n=P)).then_inc(sem("xT_dve"), 1)
                gather_indices(r, p, j + 2)

            def hidden(r, p, j):
                b = j % 2
                dve.wait_ge(sem("silu_made"), nth(dve, 1, r, p, j, 2))
                dve.wait_ge(sem("up_made"), nth(dve, 1, r, p, j, 3))
                TT(he[b], gated[b], psum[:, 3], ALU.mult).then_inc(sem("he_made"), 1)

            def copy_y(r, p, j):
                b = j % 2
                dve.wait_ge(sem(f"slot_free{b}"), nth_of_half(dve, 1, r, p, j, 1))
                v.tensor_copy(idx_s[b], table[:, bass.ds(nth(dve, 1, r, p, j, 0), 1)])
                dve.wait_ge(sem("y_made"), nth(dve, 2, r, p, j, 6))
                v.tensor_copy(yo[b][:, 512:1024], psum[:, 6]).then_inc(sem("y_read_dve"), 1)

            def first(r):
                copy_rows(r, 0, 0)
                hidden(r, 0, 0)
                copy_rows(r, 0, 1)

            def step(r, p, j):
                hidden(r, p, j)
                copy_rows(r, p, j + 1)
                copy_y(r, p, j - 1)

            def last(r):
                hidden(r, 0, E - 1)
                copy_y(r, 0, E - 2)
                copy_y(r, 0, E - 1)

            for j in range(2):
                gather_indices(0, 0, j)
            in_steps(dve, 0, first, step, last)
            n_rounds = dve.value_load(rounds[0:1, 0:1], min_val=1, max_val=4)
            with dve.If(n_rounds > 1):
                with dve.Fori(1, n_rounds) as r:
                    in_steps(dve, r, first, step, last)

            def store_tile(t):
                dve.wait_ge(sem("rs3_ready"), t + 1)
                if t == 0:
                    dve.wait_ge(sem("ld_fn"), 16)
                if t >= 2:
                    dve.wait_ge(sem(f"st_out{t % 2}"), 16)
                link(STT(fout[t % 2], x[:, t], rs[:, t:t + 1], fbc, ALU.mult, ALU.mult), sem("out_ready"))

            for t in range(T + 1):
                if t == T:
                    store_tile(t - 1)
                    break
                dve.wait_ge(sem(f"ld_yb{t % 2}"), 16 * (t // 2 + 1))
                link(TS(ym, yb[t % 2][:, 0], wtok[:, 0, t:t + 1], None, ALU.mult))
                link(STT(ym, yb[t % 2][:, 1], wtok[:, 1, t:t + 1], ym, ALU.mult, ALU.add), sem("yb_used"))
                link(TT(ym, ym, mod2[:, 3], ALU.mult))
                link(TT(x[:, t], x[:, t], ym, ALU.add), sem("x2_ready"))
                if t >= 1:
                    store_tile(t - 1)


def kernel(**inputs):
    from concourse import bacc
    from concourse.bass_utils import run_bass_kernel_spmd

    nc = bacc.Bacc("TRN2", target_bir_lowering=False, num_devices=1)
    arrays = {f"in_{n}": np.ascontiguousarray(inputs[n]) for n in INPUTS}
    aps = {n: nc.dram_tensor(f"in_{n}", arrays[f"in_{n}"].shape, mybir.dt.from_np(arrays[f"in_{n}"].dtype),
                             kind="ExternalInput").ap() for n in INPUTS}
    out = nc.dram_tensor("out_y", (1, SEQ, D), F32, kind="ExternalOutput").ap()
    build(nc, aps, out)
    return run_bass_kernel_spmd(nc, [arrays], core_ids=[0]).results[0]["out_y"]
```

```python
import math

import numpy as np

import concourse.bass as bass
from concourse import mybir

F32 = mybir.dt.float32
I32 = mybir.dt.int32
ALU = mybir.AluOpType
ACT = mybir.ActivationFunctionType
AX = mybir.AxisListType

P = 128
D = 1024
SEQ = 512
T = SEQ // P
K = D // P
CHUNK = 64
H = 4
DH = 64
E = 16
F = 512
D_IN = 2824
EPS = 1e-6
LAM_INIT = 0.8 - 0.6 * math.exp(0.0)
NEG = 1e30
KB = 1024
BASE = 16512

C_QKV, C_GATE, C_BQ, C_BK, C_BV, C_UV, C_DQ, C_DK, C_DV = 0, 768, 1032, 1288, 1544, 1800, 2312, 2568, 2696

INPUTS = ["x", "c", "norm1", "norm2", "w_ada", "b_ada", "w_in", "b_in", "w_out", "b_out", "conv_w", "a_log",
          "dt_bias", "gdn_norm", "lam_q1", "lam_k1", "lam_q2", "lam_k2", "diff_norm", "sgu_norm", "sgu_w",
          "sgu_b", "sinks", "router_w", "router_b", "w_gate", "w_up", "w_down", "final_norm"]


def products():
    out = [(("mod", b), "act") for b in range(4)]
    out += [(("hT", t, g), "act" if g else "dve") for t in range(T) for g in range(2)]
    for c in range(13):
        out += [(("zf", c), "act")]
        if c >= 5:
            out += [(("mod", 4 + 2 * (c - 5) + i), "act") for i in range(2)]
    out += [(("zt", t, s), "dve") for t in range(T) for s in range(4)]
    out += [(("qk_tm", t), "act") for t in range(T)] + [(("v_tm", t), "act") for t in range(T)]
    out += [(("gcum",), "dve")] + [(("grow", t), "dve") for t in range(T)]
    out += [(("kT", t), "act") for t in range(T)] + [(("qT", t), "act") for t in range(T)]
    out += [(("kk", t), "dve") for t in range(T)] + [(("kq", t), "dve") for t in range(T)]
    out += [(("M", t), "act") for t in range(T)]
    for step, who in (("L2", "act"), ("M2", "act"), ("L4", "act"), ("Ra", "dve"), ("Rb", "dve")):
        out += [((step, t), who) for t in range(T)]
    for lv in range(3):
        for step, who in (("Tm", "act"), ("Z", "act"), ("R", "dve")):
            out += [((step, lv, t), who) for t in range(T)]
    out += [(("U", t), "act") for t in range(T)] + [(("WT", t), "act") for t in range(T)]
    out += [(("QdT", t), "act") for t in range(T)]
    out += [(("sguT",), "dve")]
    for ch in range(2 * T):
        out += [(("WQ", ch), "dve"), (("SU", ch), "dve")]
        if ch % 2:
            out += [(("AV", ch // 2), "dve"), (("mix", ch // 2), "dve")]
    units = attention_units()
    out += [(("score", 0, m), "dve") for m in range(2)]
    for n in range(len(units) + 2):
        if n + 1 < len(units):
            out += [(("score", n + 1, m), "dve") for m in range(2 if units[n + 1][0] == "diff" else 1)]
        if 1 <= n <= len(units):
            out += [(("pT", n - 1), "act")]
        if n >= 2:
            out += [(("pv", n - 2), "dve")]
    out += [(("oT", t, g), "act" if g else "dve") for t in range(T) for g in range(2)]
    for t in range(T + 2):
        if t < T:
            out += [(("y", t, n), "dve") for n in range(2)]
        if 1 <= t <= T:
            out += [(("h2T", t - 1, g), "act" if g else "dve") for g in range(2)]
        if t >= 2:
            out += [(("logit", t - 2), "dve")]
    out += [(("rank",), "dve"), (("table",), "dve")]
    return out


def attention_units():
    return [("diff", t, h) for t in range(T) for h in range(H)] + [("swa", t, h) for t in range(T) for h in range(H)]


def slopes():
    s = [2.0 ** (-8.0 * (i + 1) / 8) for i in range(8)]
    return s[0::2], s[1::2]


def build(nc, a, out):
    order = products()
    number = {name: n for n, (name, _) in enumerate(order)}
    assert len(number) == len(order)
    reader_count = []
    seen = {"act": 0, "dve": 0}
    for _, who in order:
        seen[who] += 1
        reader_count.append(seen[who])

    sems = {}

    def sem(name):
        if name not in sems:
            sems[name] = nc.alloc_semaphore(name)
        return sems[name]

    product_ready = sem("product_ready")
    banks_read = {"act": sem("banks_read_by_scalar"), "dve": sem("banks_read_by_vector")}

    def at(name, shape, dt, kb):
        t = nc.alloc_sbuf_tensor_at(name, [P] + shape, dt, offset=BASE + int(kb * KB))
        assert BASE + kb * KB + math.prod(shape) * 4 <= 229344, name
        return t.ap()

    x = at("x", [T, D], F32, 0)
    mod2 = at("mod2", [4, D], F32, 16)
    hT = at("hT", [K, SEQ], F32, 32)
    ada_rest = [at(f"ada_rest{i}", [K, 256], F32, 48 + 8 * i) for i in range(2)]
    zpad = at("zpad", [6, SEQ + 3], F32, 64)
    zb = at("zb", [7, SEQ], F32, 77)
    h_ring = [at(f"h_ring{i}", [D], F32, 77 + 4 * i) for i in range(2)]
    gab = at("gab", [T, 264], F32, 91)
    bv = at("bv", [T, 256], F32, 96)
    uv = at("uv", [T, 512], F32, 100)
    mod1 = at("mod1", [2, D], F32, 96)
    dv = at("dv", [T, 128], F32, 108)
    acc_ring = [at(f"acc_ring{i}", [512], F32, 110 + 2 * i) for i in range(2)]
    W = 114
    w_qkv = at("w_qkv", [K, 768], F32, W)
    w_b = at("w_b", [K, 512], F32, W + 24)
    w_d = at("w_d", [K, 384], F32, W + 40)
    w_g = at("w_g", [K, 264], F32, W + 52)
    w_v = at("w_v", [K, P], F32, W + 60.25)
    w_t = at("w_t", [K, 512], F32, W)
    w_u = at("w_u", [K, 256], F32, W + 16)
    ada_first = [at(f"ada_first{i}", [K, 512], F32, p) for i, p in enumerate((W + 24, W + 40, W + 56, 32))]
    btm = at("btm", [1160], F32, 186)
    n1bc = at("n1bc", [D], F32, 91)
    brow = [at(f"brow{i}", [256], F32, 191 + i) for i in range(2)]
    brow_first = at("brow_first", [2048], F32, 48)
    cring = [at(f"cring{i}", [SEQ], F32, 193 + 2 * i) for i in range(2)]
    squares = at("squares", [D], F32, 86)
    o_tm = at("o_tm", [T, D], F32, W)
    qkv_tm = at("qkv_tm", [T, 768], F32, 130)
    AT = at("AT", [T, H, P], F32, 142)
    Lf = at("Lf", [T, H, P], F32, 150)
    B1 = at("B1", [T, H, P], F32, 158)
    B2 = at("B2", [T, H, P], F32, 166)
    B3 = at("B3", [T, H, P], F32, 174)
    B4 = at("B4", [T, H, P], F32, 182)
    R = at("R", [T, H, P], F32, 190)
    kT = at("kT", [T, H, P], F32, 32)
    qT = at("qT", [T, H, P], F32, 40)
    WT = at("WT", [T, H, P], F32, 150)
    QdT = at("QdT", [T, H, P], F32, 166)
    vb = at("vb", [T, H, DH], F32, 158)
    kbe = at("kbe", [T, H, DH], F32, 162)
    U = at("U", [T, H, DH], F32, 174)
    ktail = at("ktail", [T, H, DH], F32, 178)
    v_new = at("v_new", [T, H, DH], F32, 182)
    qs = at("qs", [T, H, DH], F32, 186)
    Qd = at("Qd", [T, H, DH], F32, 48)
    S = at("S", [H, DH], F32, 52)
    Stmp = at("Stmp", [H, DH], F32, 53)
    bias_diff = at("bias_diff", [H, SEQ], F32, 64)
    bias_swa = at("bias_swa", [H, 256], F32, 72)
    s_sb = [[at(f"s_sb{i}{m}", [SEQ], F32, 154 + 4 * i + 2 * m) for m in range(2)] for i in range(2)]
    p_sb = [[at(f"p_sb{i}{m}", [SEQ], F32, 162 + 4 * i + 2 * m) for m in range(2)] for i in range(2)]
    pc = [at(f"pc{i}", [SEQ], F32, 170 + 2 * i) for i in range(2)]
    pT = [at(f"pT{i}", [4, P], F32, 174 + 2 * i) for i in range(2)]
    wide = at("wide", [SEQ], F32, 110)
    bobc = at("bobc", [D], F32, 110)
    n2bc = at("n2bc", [D], F32, 130)
    junk1k = at("junk1k", [D], F32, 110)
    junk_last = at("junk_last", [D], F32, 40)
    before = at("before", [P], F32, 76)
    sixteen = [at(f"sixteen{i}", [T, E], F32, 72 + 0.25 * i) for i in range(16)]
    sq = at("sq", [2 * H * DH], F32, 194)
    sgw = at("sgw", [H, P], F32, 54)
    sgT = at("sgT", [H, P], F32, 56)
    w_o = [at(f"w_o{i}", [K, 512], F32, 32 + 16 * i) for i in range(2)]
    oT = at("oT", [K, SEQ], F32, 64)
    ytmp = [at(f"ytmp{i}", [512], F32, 104 + 2 * i) for i in range(2)]
    h2_ring = [at(f"h2_ring{i}", [D], F32, 96 + 4 * i) for i in range(2)]
    h2T = at("h2T", [K, SEQ], F32, 80)
    off = [198.0]

    def small(name, shape, dt=F32):
        n = math.prod(shape) * 4 / KB
        off[0] = math.ceil(off[0] * 32) / 32
        off[0] += n
        return at(name, shape, dt, off[0] - n)

    ident = small("ident", [P])
    ones = small("ones", [P])
    tri = small("tri", [P])
    mask_s = small("mask_s", [P])
    mlv = [small(f"mlv{i}", [P]) for i in range(4)]
    m8T = small("m8T", [P])
    acol = small("acol", [8])
    ccol = small("ccol", [8])
    ss = small("ss", [T])
    rs = small("rs", [T])
    bcol = small("bcol", [13])
    convc = small("convc", [6, 4])
    g_ = small("g_", [T, H])
    beta = small("beta", [T, H])
    gc = small("gc", [T, H])
    egc = small("egc", [T, H])
    nss = small("nss", [T, 8])
    nrs = small("nrs", [T, 8])
    head_ss = {nm: small(f"ss_{nm}", [T, H]) for nm in ("gdn", "diff", "sgu")}
    junk_head = small("junk_head", [DH])
    glast = small("glast", [T, H, 2])
    etail = small("etail", [T, H])
    egl = small("egl", [T, H, 2])
    alog = small("alog", [H])
    dtb = small("dtb", [H])
    sink = small("sink", [H])
    gnorm = small("gnorm", [DH])
    dnorm = small("dnorm", [DH])
    lam4 = small("lam4", [4, 32])
    lamt = small("lamt", [2, 32])
    lam = small("lam", [4])
    sgb = small("sgb", [H])
    mx = small("mx", [4, 8])
    snorm = small("snorm", [256])
    rb = small("rb", [E])
    rw = small("rw", [K, E])
    tA = small("tA", [T, H])
    tB = small("tB", [T, H])
    tC = small("tC", [T, H])
    wtok = small("wtok", [2, T])
    eps = small("eps", [1])
    junk = small("junk", [1])
    neglam = small("neglam", [1])
    rounds = small("rounds", [1], I32)
    table = at("table", [80], I32, 60)
    tokens = at("tokens", [80], I32, 60.5)
    idx_g = [small(f"idx_g{i}", [1], I32) for i in range(2)]
    idx_s = [small(f"idx_s{i}", [1], I32) for i in range(2)]
    w_exp = [[at(f"w_exp{b}{i}", [K, F] if i < 2 else [4, D], F32, p + 16 * i) for i in range(3)] for b, p in ((0, 150), (1, 102))]
    xg = [at(f"xg{b}", [D], F32, 32 + 4 * b) for b in range(2)]
    xgT = [at(f"xgT{b}", [K, P], F32, 40 + 4 * b) for b in range(2)]
    gated = [at(f"gated{b}", [F], F32, 48 + 2 * b) for b in range(2)]
    he = [at(f"he{b}", [F], F32, 52 + 2 * b) for b in range(2)]
    heT = [at(f"heT{b}", [4, P], F32, 56 + 2 * b) for b in range(2)]
    yo = [at(f"yo{b}", [D], F32, 64 + 4 * b) for b in range(2)]
    yb = [at(f"yb{b}", [2, D], F32, 80 + 8 * b) for b in range(2)]
    ym = at("ym", [D], F32, 72)
    fbc = at("fbc", [D], F32, 76)
    fout = [at(f"fout{b}", [D], F32, 32 + 4 * b) for b in range(2)]
    h2_dram = nc.dram_tensor("h2_rows", [SEQ, D], F32).ap()
    y_dram = nc.dram_tensor("expert_rows", [2 * SEQ, D], F32).ap()
    in_slot = at("in_slot", [2, T, P], F32, 64)
    in_table = at("in_table", [2, T, 80], F32, 68)
    slot_no = at("slot_no", [P], F32, 70.5)
    column_no = at("column_no", [80], F32, 71)
    pair = at("pair", [2, T], F32, 71.375)
    tablef = at("tablef", [80], F32, 71.5)

    def wait_product(eng, *name):
        eng.wait_ge(product_ready, number[name] + 1)

    def wait_read(eng, *name):
        eng.wait_ge(banks_read[order[number[name]][1]], reader_count[number[name]])

    def chain(eng, step):
        count = {}

        def link(ins, signal=step):
            count[signal] = count.get(signal, 0) + 1
            ins.then_inc(signal, 1)
            eng.wait_ge(signal, count[signal])
        return link

    def nth(eng, scale, r, p, j, plus):
        v = r * (E * scale) + p * (2 * scale) + (j * scale + plus)
        return v if isinstance(v, int) else eng.snap(v)

    def nth_of_half(eng, scale, r, p, j, plus):
        v = r * (E // 2 * scale) + p * scale + (j // 2 * scale + plus)
        return v if isinstance(v, int) else eng.snap(v)

    def in_steps(eng, r, first, step, last):
        first(r)
        with eng.Fori(0, E // 2 - 1) as p:
            for j in (1, 2):
                step(r, p, j)
        last(r)

    def over_heads(v, n):
        return v.unsqueeze(2).to_broadcast([P, H, n])

    def per_head(m):
        return m.unsqueeze(1).to_broadcast([P, H, m.shape[-1]])

    psum = nc.alloc_psum_tensor("psum", [P, 8, 512], F32).ap()

    def bank(*name):
        return psum[:, number[name] % 8]

    def row(v):
        return v.partition_broadcast(P)

    w_ada = a["w_ada"][0].rearrange("(p j) n -> p j n", j=8)
    w_in = a["w_in"][0].rearrange("(k p) n -> p k n", p=P)
    w_out = a["w_out"][0].rearrange("(k p) n -> p k n", p=P)
    b_in = a["b_in"][0]
    zf_cols = [C_QKV + P * i for i in range(6)] + [C_BQ, C_BQ + P, C_BK, C_BK + P, C_DQ, C_DQ + P, C_DK]
    zt_parts = [(w_g, C_GATE, 264, 0), (w_t, C_BV, 512, 264), (w_u, C_BV + 512, 256, 776), (w_v, C_DV, P, 1032)]
    units = attention_units()
    n_blocks = []
    for kind, t, h in units:
        n_blocks.append(t + 1 if kind == "diff" else (2 if t else 1))
    logits_, scores, sel, mask, one1, one2, m16, u16, v16, sel2 = sixteen[:10]
    grp = [at(f"grp{i}", [T, 4], F32, 76.5 + 0.0625 * i) for i in range(16)]
    col = [at(f"col{i}", [T], F32, 77.5 + 0.03125 * i) for i in range(16)]
    eidx = at("eidx", [T, E], F32, 78)
    gw = at("gw", [T, 4], F32, 78.25)
    eweight = at("eweight", [T, E], F32, 78.5)
    rank = at("rank", [T, E], F32, 78.75)
    counts = at("counts", [E], F32, 79)

    with nc.Block() as block:

        @block.sync
        def _(sp):
            sp.dma_start(ccol, a["c"][0].rearrange("(p j) -> p j", j=8)).then_inc(sem("ld_c"), 16)
            sp.dma_start(brow_first[0:1], a["b_ada"][0:1, 0:2048]).then_inc(sem("ld_brow"), 16)
            xr = a["x"][0].rearrange("(t p) d -> p t d", p=P)
            for b in range(4):
                sp.dma_start(ada_first[b], w_ada[:, :, 512 * b:512 * b + 512]).then_inc(sem(f"ld_ada{b}"), 16)
                if b == 0:
                    sp.dma_start(x, xr).then_inc(sem("ld_x"), 16)
                    sp.dma_start(n1bc, row(a["norm1"][0])).then_inc(sem("ld_n1"), 16)
            sp.dma_start(bcol[:, 0:6], b_in[0:768].rearrange("(c p) -> p c", p=P), allow_slow_non_contiguous=True).then_inc(sem("ld_bcol"), 16)
            sp.dma_start(bcol[:, 6:10], b_in[C_BQ:C_BQ + 512].rearrange("(c p) -> p c", p=P), allow_slow_non_contiguous=True).then_inc(sem("ld_bcol"), 16)
            for g in range(2):
                for kv in range(2):
                    c0 = C_DQ + (2 * kv + g) * DH
                    sp.dma_start(bcol[DH * kv:DH * kv + DH, 10 + g:11 + g], b_in[c0:c0 + DH].unsqueeze(1), allow_slow_non_contiguous=True).then_inc(sem("ld_bcol"), 16)
            sp.dma_start(bcol[:, 12:13], b_in[C_DK:C_DK + P].unsqueeze(1), allow_slow_non_contiguous=True).then_inc(sem("ld_bcol"), 16)
            sp.dma_start(w_qkv, w_in[:, :, 0:768]).then_inc(sem("ld_w0"), 16)
            for i in range(4):
                sp.dma_start(convc[:, :, i], a["conv_w"][0, i].rearrange("(c p) -> p c", p=P), allow_slow_non_contiguous=True).then_inc(sem("ld_conv"), 16)
            for nm, dst in (("a_log", alog), ("dt_bias", dtb), ("sinks", sink), ("gdn_norm", gnorm), ("diff_norm", dnorm)):
                sp.dma_start(dst, row(a[nm][0])).then_inc(sem("ld_small"), 16)
            for i, nm in enumerate(("lam_q1", "lam_k1", "lam_q2", "lam_k2")):
                sp.dma_start(lam4[:, i], row(a[nm][0])).then_inc(sem("ld_small"), 16)
            sp.dma_start(sgb, a["sgu_b"][0].rearrange("g p -> p g"), allow_slow_non_contiguous=True).then_inc(sem("ld_small"), 16)
            sp.dma_start(snorm, row(a["sgu_norm"][0].rearrange("g c -> (g c)"))).then_inc(sem("ld_small"), 16)
            sp.dma_start(rb, row(a["router_b"])).then_inc(sem("ld_small"), 16)
            sp.dma_start(rw, a["router_w"].rearrange("(k p) e -> p k e", p=P)).then_inc(sem("ld_small"), 16)
            sp.wait_ge(sem("acc_ready"), 4)
            sp.dma_start(w_b, w_in[:, :, C_BQ:C_BQ + 512]).then_inc(sem("ld_w1"), 16)
            for g in range(2):
                for kv in range(2):
                    c0, o = C_DQ + (2 * kv + g) * DH, P * g + DH * kv
                    sp.dma_start(w_d[:, :, o:o + DH], w_in[:, :, c0:c0 + DH]).then_inc(sem("ld_w2"), 16)
            sp.dma_start(w_d[:, :, 256:384], w_in[:, :, C_DK:C_DK + P]).then_inc(sem("ld_w2"), 16)
            sp.dma_start(w_g, w_in[:, :, C_GATE:C_GATE + 264]).then_inc(sem("ld_w3"), 16)
            sp.dma_start(w_v, w_in[:, :, C_DV:C_DV + P]).then_inc(sem("ld_w6"), 16)
            for i, (_, c0, n, o) in enumerate(zt_parts):
                sp.dma_start(btm[:, o:o + n], row(b_in[c0:c0 + n])).then_inc(sem("ld_btm"), 16)
            for b in range(4, 20):
                if b == 8:
                    wait_product(sp, "zf", 5)
                    sp.dma_start(w_t, w_in[:, :, C_BV:C_BV + 512]).then_inc(sem("ld_w4"), 16)
                    sp.dma_start(w_u, w_in[:, :, C_BV + 512:C_BV + 768]).then_inc(sem("ld_w5"), 16)
                if b >= 6:
                    sp.wait_ge(sem("acc_ready"), b - 1)
                c0 = 2048 + 256 * (b - 4)
                sp.dma_start(ada_rest[b % 2], w_ada[:, :, c0:c0 + 256]).then_inc(sem(f"ld_adar{b % 2}"), 16)
                sp.dma_start(brow[b % 2][0:1], a["b_ada"][0:1, c0:c0 + 256]).then_inc(sem(f"ld_adar{b % 2}"), 16)
            sp.wait_ge(sem("acc_ready"), 20)
            sp.dma_start(sgw, a["sgu_w"][0].rearrange("g i j -> i g j")).then_inc(sem("ld_sgw"), 16)
            wait_product(sp, "kq", T - 1)
            sp.dma_start(w_o[0], w_out[:, :, 0:512]).then_inc(sem("ld_wo"), 16)
            sp.wait_ge(sem("biases"), 1)
            sp.dma_start(bobc, row(a["b_out"][0])).then_inc(sem("ld_bo"), 16)
            wait_read(sp, "mix", H - 1)
            sp.dma_start(w_o[1], w_out[:, :, 512:1024]).then_inc(sem("ld_wo"), 16)
            sp.dma_start(n2bc, row(a["norm2"][0])).then_inc(sem("ld_n2"), 16)

            def load_expert(b, e, i):
                for n, (nm, used, at_) in enumerate((("w_gate", "gate_made", i + 1), ("w_up", "up_made", i + 1), ("w_down", "y_made", i * 2 + 2))):
                    src = a[nm][0, bass.ds(e, 1)].rearrange("o (k p) n -> p (o k) n", p=P)
                    sp.wait_ge(sem(used), sp.snap(at_))
                    sp.dma_start(w_exp[b][n], src).then_inc(sem(f"ld_{nm}{b}"), 16)

            def expert_pass(r):
                with sp.Fori(0, E // 2) as p:
                    for b in range(2):
                        load_expert(b, p * 2 + b, r * 16 + p * 2 + b)

            for t in range(T):
                sp.wait_ge(sem("h2_ready"), t + 1)
                sp.dma_start(h2_dram[P * t:P * t + P], h2_ring[t % 2]).then_inc(sem(f"st_h2{t % 2}"), 16)
            sp.wait_ge(sem("st_h20"), 32)
            sp.wait_ge(sem("st_h21"), 32)
            expert_pass(0)
            sp.wait_ge(sem("rounds_ready"), 1)
            n_rounds = sp.value_load(rounds[0:1, 0:1], min_val=1, max_val=4)
            with sp.If(n_rounds > 1):
                with sp.Fori(1, n_rounds) as r:
                    expert_pass(r)
            sp.dma_start(fbc, row(a["final_norm"])).then_inc(sem("ld_fn"), 16)
            sp.wait_ge(sem("all_scattered"), 1)
            for t in range(T):
                if t >= 2:
                    sp.wait_ge(sem("yb_used"), t - 1)
                sp.dma_start(yb[t % 2], y_dram.rearrange("(t p k) d -> t p k d", p=P, k=2)[t]).then_inc(sem(f"ld_yb{t % 2}"), 16)
                if t >= 1:
                    sp.wait_ge(sem("out_ready"), t)
                    sp.dma_start(out[0, P * (t - 1):P * t], fout[(t - 1) % 2]).then_inc(sem(f"st_out{(t - 1) % 2}"), 16)
            sp.wait_ge(sem("out_ready"), T)
            sp.dma_start(out[0, P * (T - 1):P * T], fout[(T - 1) % 2]).then_inc(sem(f"st_out{(T - 1) % 2}"), 16)
            for i in range(2):
                sp.wait_ge(sem(f"st_out{i}"), 16 * T // 2)

        @block.gpsimd
        def _(gp):
            link = chain(gp, sem("pool_step"))
            g = nc.gpsimd

            def keep(m, pattern, base, cm, fill=0.0, op=ALU.is_ge):
                link(g.affine_select(out=m, in_=m, pattern=pattern, compare_op=op, fill=fill, base=base, channel_multiplier=cm))

            link(g.memset(ones, 1.0))
            link(g.memset(ident, 0.0))
            link(g.memset(eps, EPS))
            g.affine_select(out=ident, in_=ident, pattern=[[-1, P]], compare_op=ALU.not_equal, fill=1.0, base=0,
                            channel_multiplier=1).then_inc(sem("consts"), 1)
            gp.wait_ge(sem("acc_ready"), 4)
            g.memset(zpad[:, :, 0:3], 0.0).then_inc(sem("pads"), 1)
            for m, b_, cm, s in ((tri, 0, -1, 1), (mask_s, -1, 1, -1)):
                link(g.memset(m, 1.0))
                keep(m, [[s, P]], b_, cm)
            link(g.memset(tri[0:64, 64:128], 0.0))
            link(g.memset(mask_s[64:128, 0:64], 0.0))
            for i, n in enumerate((8, 16, 32, 64)):
                link(g.memset(mlv[i], 1.0))
                keep(mlv[i], [[n, P // n], [0, n]], n - 1, -1)
                if i == 0:
                    keep(mlv[i], [[-1, P]], -1, 1)
                else:
                    keep(mlv[i], [[-n // 2, 2 * P // n], [0, n // 2]], -n // 2, 1)
            link(g.memset(m8T, 1.0))
            keep(m8T, [[1, P]], -1, -1)
            link(g.affine_select(out=m8T, in_=m8T, pattern=[[-8, P // 8], [0, 8]], compare_op=ALU.is_ge, fill=0.0, base=0,
                                 channel_multiplier=1), sem("masks_ready"))
            def scale_heads(o, t, rs_, gain, signal):
                o4 = o.rearrange("p (h d) -> p h d", d=DH)
                link(g.tensor_tensor(o4, o4, over_heads(rs_[:, t], DH), ALU.mult))
                g.tensor_tensor(o4, o4, gain, ALU.mult).then_inc(signal, 1)

            gp.wait_ge(sem("ld_small"), 16 * 13)
            link(g.tensor_scalar(dnorm, dnorm, 1.0 - LAM_INIT, None, ALU.mult))
            gp.wait_ge(sem("rs_sgu"), 1)
            for t in range(T):
                scale_heads(uv[:, t, 256:512], t, head_ss["sgu"], snorm.rearrange("p (h d) -> p h d", d=DH), sem("vn_ready"))
            gp.wait_ge(product_ready, number[("v_tm", T - 1)] + 1)
            sd, sw = slopes()
            link(g.iota(wide, [[-1, SEQ]], base=SEQ - P, channel_multiplier=1, allow_small_or_imprecise_dtypes=True))
            link(g.tensor_scalar(bias_diff[:, 0], wide, 0.0, -2.0, ALU.min, ALU.mult))
            link(g.tensor_tensor(wide, wide, bias_diff[:, 0], ALU.add))
            for h in range(H):
                link(g.tensor_scalar(bias_diff[:, h], wide, -sd[h] * 32 ** 0.5, None, ALU.mult))
                link(g.tensor_scalar(bias_swa[:, h], wide[:, 256:512], -sw[h] * DH ** 0.5, None, ALU.mult))
            link(g.memset(bias_diff[0:64, :, 448:512], -NEG))
            link(g.memset(bias_swa[0:64, :, 0:64], -NEG))
            link(g.memset(bias_swa[0:64, :, 192:256], -NEG))
            link(g.memset(bias_swa[64:128, :, 0:128], -NEG))
            g.memset(wide[:, 0:1], 0.0).then_inc(sem("biases"), 1)
            for t in range(T):
                gp.wait_ge(sem("decay"), 2 * t + 2)
                link(g.tensor_tensor(B1[:, t], B1[:, t], per_head(mask_s), ALU.mult))
                g.tensor_tensor(B1[:, t], B1[:, t], over_heads(beta[:, t], P), ALU.mult).then_inc(sem("decay_masked"), 1)
                g.tensor_tensor(AT[:, t], AT[:, t], per_head(tri), ALU.mult).then_inc(sem("decay_masked"), 1)
            for t in range(T):
                wait_read(gp, "M", t)
                g.tensor_tensor(B1[:, t], B4[:, t], per_head(m8T), ALU.mult).then_inc(sem("eights"), 1)
                g.tensor_tensor(B2[:, t], Lf[:, t], per_head(mlv[0]), ALU.mult).then_inc(sem("eights"), 1)
            gp.wait_ge(sem("eights"), 2 * T)
            for t in range(T):
                g.tensor_tensor(R[:, t], per_head(ident), B1[:, t], ALU.subtract).then_inc(sem("R_first"), 1)
            for lv in range(3):
                for t in range(T):
                    gp.wait_ge(product_ready, number[("M2", t) if lv == 0 else ("Z", lv - 1, t)] + 1)
                    g.tensor_tensor(B2[:, t], Lf[:, t], per_head(mlv[lv + 1]), ALU.mult).then_inc(sem("level_masked"), 1)
            gp.wait_ge(sem("level_masked"), 3 * T)
            wait_read(gp, "mod", 19)
            gp.wait_ge(sem("ld_bo"), 16)
            link(g.tensor_tensor(bobc, bobc, mod2[:, 0], ALU.mult))
            for t in range(T):
                g.tensor_tensor(x[:, t], x[:, t], bobc, ALU.add).then_inc(sem("x_biased"), 1)
            for t in range(T):
                gp.wait_ge(sem("rs_gdn"), t + 1)
                scale_heads(o_tm[:, t, 0:256], t, head_ss["gdn"], per_head(gnorm), sem("gdn_normed"))
                gp.wait_ge(sem("gdn_normed"), t + 1)
                g.tensor_tensor(o_tm[:, t, 0:256], o_tm[:, t, 0:256], gab[:, t, 0:256], ALU.mult).then_inc(sem("gdn_done"), 1)
            for t in range(T):
                gp.wait_ge(sem("rs_diff"), t + 1)
                scale_heads(o_tm[:, t, 256:512], t, head_ss["diff"], per_head(dnorm), sem("diff_done"))
            wait_product(gp, "y", T - 1, 1)
            link(g.iota(eidx, [[0, T], [1, E]], base=0, channel_multiplier=0, allow_small_or_imprecise_dtypes=True))
            link(g.iota(eweight, [[0, T], [-1, E]], base=E, channel_multiplier=0, allow_small_or_imprecise_dtypes=True))
            link(g.iota(slot_no, [[1, P]], base=0, channel_multiplier=0, allow_small_or_imprecise_dtypes=True))
            link(g.iota(column_no, [[1, 80]], base=0, channel_multiplier=0, allow_small_or_imprecise_dtypes=True))
            link(g.iota(pair, [[1, 2], [2 * P, T]], base=-4 * SEQ * 2, channel_multiplier=2, allow_small_or_imprecise_dtypes=True))
            g.iota(gw, [[0, T], [-1, 4]], base=4, channel_multiplier=0, allow_small_or_imprecise_dtypes=True).then_inc(sem("router_consts"), 1)
            link(g.memset(before, 1.0))
            g.affine_select(out=before, in_=before, pattern=[[1, P]], compare_op=ALU.is_ge, fill=0.0, base=-1,
                            channel_multiplier=-1).then_inc(sem("before_ready"), 1)
            for b in range(2):
                g.memset(xg[b], 0.0).then_inc(sem("xg_cleared"), 1)
            gp.wait_ge(sem("xg_cleared"), 2)
            gp.wait_ge(sem("st_h20"), 32)
            gp.wait_ge(sem("st_h21"), 32)

            last_token, last_pair = gp.to_reg(SEQ - 1), gp.to_reg(2 * SEQ - 1)

            def gather(b):
                g.indirect_dma_start(xg[b], None, h2_dram, bass.IndirectOffsetOnAxis(idx_g[b], 0),
                                     bounds_check=last_token, oob_is_err=False).then_inc(sem(f"ld_xg{b}"), 16)

            def gather_next(r, p, j):
                b = j % 2
                gp.wait_ge(sem(f"idx_ready{b}"), nth_of_half(gp, 1, r, p, j, 2))
                gp.sem_inc(sem("gather_turn"), 1)
                gather(b)

            def scatter(r, p, j):
                b = j % 2
                done = nth_of_half(gp, 16, r, p, j, 16)
                gp.wait_ge(sem("y_read_act"), nth(gp, 1, r, p, j, 2))
                gp.wait_ge(sem("y_read_dve"), nth(gp, 1, r, p, j, 2))
                gp.sem_inc(sem("scatter_turn"), 1)
                g.indirect_dma_start(y_dram, bass.IndirectOffsetOnAxis(idx_s[b], 0), yo[b], None,
                                     bounds_check=last_pair, oob_is_err=False).then_inc(sem(f"scattered{b}"), 16)
                gp.wait_ge(sem(f"scattered{b}"), done)
                gp.sem_inc(sem(f"slot_free{b}"), 1)

            for b in range(2):
                gp.sem_inc(sem(f"slot_free{b}"), 1)
                gp.wait_ge(sem(f"idx_ready{b}"), 1)
                gather(b)

            def first(r):
                gather_next(r, 0, 0)
                gather_next(r, 0, 1)

            def step(r, p, j):
                gather_next(r, p, j + 1)
                scatter(r, p, j - 1)

            def last(r):
                scatter(r, 0, E - 2)
                scatter(r, 0, E - 1)

            in_steps(gp, 0, first, step, last)
            gp.wait_ge(sem("rounds_ready"), 1)
            n_rounds = gp.value_load(rounds[0:1, 0:1], min_val=1, max_val=4)
            with gp.If(n_rounds > 1):
                with gp.Fori(1, n_rounds) as r:
                    in_steps(gp, r, first, step, last)
            gathers = gp.snap((n_rounds * 8 + 1) * 16)
            for b in range(2):
                gp.wait_ge(sem(f"ld_xg{b}"), gathers)
                gp.sem_inc(sem("gather_turn"), 1)
            g.memset(wide[:, 0:1], 0.0).then_inc(sem("all_scattered"), 1)

        @block.tensor
        def _(pe):
            made = [0]
            mm, tr = nc.tensor.matmul, nc.tensor.transpose

            def begin(*name):
                n = number[name]
                assert n == made[0], (name, order[made[0]])
                made[0] += 1
                if n >= 8:
                    pe.wait_ge(banks_read[order[n - 8][1]], reader_count[n - 8])
                return psum[:, n % 8]

            def done(ins):
                ins.then_inc(product_ready, 1)

            def four(ps, t, lhs, rhs):
                for h in range(H):
                    last = mm(ps[:, P * h:P * h + P], lhs[:, t, h], rhs[:, t, h], start=True, stop=True)
                return last

            def modulation(b):
                ps = begin("mod", b)
                pe.wait_ge(sem("acc_ready"), b + 1)
                n = 512 if b < 4 else 256
                done(mm(ps[:, 0:n], ones, acc_ring[b % 2][:, 0:n], start=True, stop=True))

            pe.wait_ge(sem("consts"), 1)
            for b in range(4):
                modulation(b)
            for t in range(T):
                pe.wait_ge(sem("h_ready"), t + 1)
                for g in range(2):
                    ps = begin("hT", t, g)
                    for i in range(4):
                        last = tr(ps[:, P * i:P * i + P], h_ring[t % 2][:, P * (4 * g + i):P * (4 * g + i) + P], ident)
                    done(last)
            wait_read(pe, "hT", T - 1, 0)
            wait_read(pe, "hT", T - 1, 1)
            for c in range(13):
                ps = begin("zf", c)
                for i, s in ((0, "ld_w0"), (6, "ld_w1"), (10, "ld_w2")):
                    if c == i:
                        pe.wait_ge(sem(s), 16 if s != "ld_w2" else 80)
                for k in range(K):
                    if c < 6:
                        w = w_qkv[:, k, P * c:P * c + P]
                    elif c < 10:
                        w = w_b[:, k, P * (c - 6):P * (c - 6) + P]
                    else:
                        w = w_d[:, k, P * (c - 10):P * (c - 10) + P]
                    last = mm(ps, w, hT[:, k], start=k == 0, stop=k == K - 1)
                done(last)
                if c >= 5:
                    for i in range(2):
                        modulation(4 + 2 * (c - 5) + i)
            for s in ("ld_w3", "ld_w4", "ld_w5", "ld_w6"):
                pe.wait_ge(sem(s), 16)
            for t in range(T):
                for s, (w, _, n, _) in enumerate(zt_parts):
                    ps = begin("zt", t, s)
                    for k in range(K):
                        last = mm(ps[:, 0:n], hT[:, k, P * t:P * t + P], w[:, k, 0:n], start=k == 0, stop=k == K - 1)
                    done(last)
            pe.wait_ge(sem("silu_done"), 6)
            for nm, c0, nc_ in (("qk_tm", 0, 4), ("v_tm", 4, 2)):
                for t in range(T):
                    ps = begin(nm, t)
                    for i in range(nc_):
                        last = tr(ps[:, P * i:P * i + P], zpad[:, c0 + i, P * t:P * t + P], ident)
                    done(last)
            ps = begin("gcum")
            pe.wait_ge(sem("masks_ready"), 1)
            pe.wait_ge(sem("g_ready"), 1)
            done(mm(ps[:, 0:16], tri, g_.rearrange("p t h -> p (t h)"), start=True, stop=True))
            for t in range(T):
                ps = begin("grow", t)
                for h in range(H):
                    last = mm(ps[:, P * h:P * h + P], g_[:, t, h:h + 1].to_broadcast([P, P]), tri, start=True, stop=True)
                done(last)
            for nm, at_, s in (("kT", 4, "kn"), ("qT", 0, "qn")):
                for t in range(T):
                    ps = begin(nm, t)
                    pe.wait_ge(sem("qk_normed"), t + 1)
                    for h in range(H):
                        last = tr(ps[0:64, P * h:P * h + P], qkv_tm[:, t, 64 * (at_ + h):64 * (at_ + h) + 64], ident)
                    done(last)
            for nm, r_, cnt in (("kk", kT, "kT"), ("kq", qT, "qT")):
                for t in range(T):
                    ps = begin(nm, t)
                    wait_read(pe, cnt, t)
                    for h in range(H):
                        last = mm(ps[:, P * h:P * h + P], kT[0:64, t, h], r_[0:64, t, h], start=True, stop=True)
                    done(last)
            for t in range(T):
                ps = begin("M", t)
                wait_read(pe, "kk", t)
                for h in range(H):
                    last = tr(ps[:, P * h:P * h + P], Lf[:, t, h], ident)
                done(last)
            for nm, l_, r_ in (("L2", B1, B2), ("M2", B2, B1), ("L4", B4, B3)):
                for t in range(T):
                    ps = begin(nm, t)
                    if nm == "L2":
                        pe.wait_ge(sem("eights"), 2 * t + 2)
                    if nm == "L4":
                        wait_read(pe, "M2", t)
                    done(four(ps, t, l_, r_))
            for nm, l_ in (("Ra", B3), ("Rb", B1)):
                for t in range(T):
                    ps = begin(nm, t)
                    if nm == "Ra":
                        pe.wait_ge(sem("R_first"), t + 1)
                    else:
                        wait_read(pe, "L4", t)
                        wait_read(pe, "Ra", t)
                    done(four(ps, t, l_, R))
            for lv in range(3):
                for t in range(T):
                    ps = begin("Tm", lv, t)
                    wait_read(pe, *(("R", lv - 1, t) if lv else ("Rb", t)))
                    for h in range(H):
                        last = tr(ps[:, P * h:P * h + P], R[:, t, h], ident)
                    done(last)
                for t in range(T):
                    ps = begin("Z", lv, t)
                    pe.wait_ge(sem("level_masked"), T * lv + t + 1)
                    done(four(ps, t, B2, R))
                for t in range(T):
                    ps = begin("R", lv, t)
                    wait_read(pe, "Z", lv, t)
                    done(four(ps, t, B3, B4))
            for t in range(T):
                ps = begin("U", t)
                wait_read(pe, "R", 2, t)
                pe.wait_ge(sem("vb_ready"), t + 1)
                for h in range(H):
                    last = mm(ps[:, DH * h:DH * h + DH], R[:, t, h], vb[:, t, h], start=True, stop=True)
                done(last)
            for t in range(T):
                ps = begin("WT", t)
                for h in range(H):
                    last = mm(ps[0:64, P * h:P * h + P], kbe[:, t, h], R[:, t, h], start=True, stop=True)
                done(last)
            for t in range(T):
                ps = begin("QdT", t)
                pe.wait_ge(sem("Qd_ready"), t + 1)
                for h in range(H):
                    last = tr(ps[0:64, P * h:P * h + P], Qd[:, t, h], ident)
                done(last)
            ps = begin("sguT")
            pe.wait_ge(sem("ld_sgw"), 16)
            for g in range(H):
                last = tr(ps[:, P * g:P * g + P], sgw[:, g], ident)
            done(last)
            wait_read(pe, "QdT", T - 1)
            for ch in range(2 * T):
                t, b = ch // 2, 64 * (ch % 2)
                ps = begin("WQ", ch)
                if ch:
                    wait_read(pe, "SU", ch - 1)
                else:
                    pe.wait_ge(sem("S_ready"), 1)
                for l_, c0 in ((WT, 0), (QdT, 256)):
                    for h in range(H):
                        last = mm(ps[b:b + 64, c0 + DH * h:c0 + DH * h + DH], l_[0:64, t, h, b:b + 64], S[0:64, h],
                                  start=True, stop=True)
                done(last)
                ps = begin("SU", ch)
                pe.wait_ge(sem("v_new_ready"), ch + 1)
                for h in range(H):
                    last = mm(ps[0:64, DH * h:DH * h + DH], ktail[b:b + 64, t, h], v_new[b:b + 64, t, h],
                              start=True, stop=True)
                done(last)
                if ch % 2:
                    ps = begin("AV", t)
                    for h in range(H):
                        last = mm(ps[:, DH * h:DH * h + DH], AT[:, t, h], v_new[:, t, h], start=True, stop=True)
                    done(last)
                    if t == 0:
                        pe.wait_ge(sem("sgT_ready"), 1)
                        pe.wait_ge(sem("vn_ready"), T)
                    ps = begin("mix", t)
                    done(mm(ps[:, 0:256], sgT[:, t], uv[:, :, 256 + DH * t:256 + DH * t + DH], start=True, stop=True))
            def key_blocks(n):
                kind, t, _ = units[n]
                return list(range(t + 1)) if kind == "diff" else list(range(0 if t else 1, 2))

            def transposed(n):
                ps = begin("pT", n)
                if units[n][0] == "diff":
                    pe.wait_ge(sem("p_ready"), n + 1)
                    p_ = pc[n % 2]
                else:
                    pe.wait_ge(sem("exp_ready"), 2 * n + 1)
                    p_ = p_sb[n % 2][0]
                for i, b in enumerate(key_blocks(n)):
                    last = tr(ps[:, P * i:P * i + P], p_[:, P * b:P * b + P], ident)
                done(last)

            def times_values(n):
                kind, t, h = units[n]
                blocks = key_blocks(n)
                ps = begin("pv", n)
                wait_read(pe, "pT", n)
                for i, b in enumerate(blocks):
                    v = bv[:, b, DH * h:DH * h + DH] if kind == "diff" else dv[:, t - 1 + b, DH * (h // 2):DH * (h // 2) + DH]
                    last = mm(ps[:, 0:DH], pT[n % 2][:, i], v, start=i == 0, stop=i == len(blocks) - 1)
                done(last)

            def score(n):
                kind, t, h = units[n]
                if kind == "diff":
                    for m in range(2):
                        ps = begin("score", n, m)
                        b = 64 * (h % 2) + 32 * m
                        done(mm(ps[:, 0:P * (t + 1)], zb[b:b + 32, h // 2, P * t:P * t + P],
                                zb[b:b + 32, 2 + h // 2, 0:P * (t + 1)], start=True, stop=True))
                else:
                    ps = begin("score", n, 0)
                    b, u0 = 64 * (h // 2), 0 if t else P
                    done(mm(ps[:, u0:256], zb[b:b + 64, 4 + h % 2, P * t:P * t + P],
                            zb[b:b + 64, 6, P * (t - 1) + u0:P * (t + 1)], start=True, stop=True))

            score(0)
            for n in range(len(units) + 2):
                if n + 1 < len(units):
                    score(n + 1)
                if 1 <= n <= len(units):
                    transposed(n - 1)
                if n >= 2:
                    times_values(n - 2)
            wait_read(pe, "pv", len(units) - 1)
            pe.wait_ge(sem("gdn_done"), T)
            pe.wait_ge(sem("diff_done"), T)
            for t in range(T):
                for g in range(2):
                    ps = begin("oT", t, g)
                    for i in range(4):
                        last = tr(ps[:, P * i:P * i + P], o_tm[:, t, P * (4 * g + i):P * (4 * g + i) + P], ident)
                    done(last)
            pe.wait_ge(sem("ld_wo"), 32)
            wait_read(pe, "oT", T - 1, 0)
            wait_read(pe, "oT", T - 1, 1)
            pe.wait_ge(sem("ld_small"), 16 * 13)
            for t in range(T + 2):
                if t < T:
                    for n in range(2):
                        ps = begin("y", t, n)
                        for k in range(K):
                            last = mm(ps, oT[:, k, P * t:P * t + P], w_o[n][:, k], start=k == 0, stop=k == K - 1)
                        done(last)
                if 1 <= t <= T:
                    u = t - 1
                    pe.wait_ge(sem("h2_ready"), u + 1)
                    for g in range(2):
                        ps = begin("h2T", u, g)
                        for i in range(4):
                            last = tr(ps[:, P * i:P * i + P], h2_ring[u % 2][:, P * (4 * g + i):P * (4 * g + i) + P], ident)
                        done(last)
                if t >= 2:
                    u = t - 2
                    wait_read(pe, "h2T", u, 0)
                    wait_read(pe, "h2T", u, 1)
                    ps = begin("logit", u)
                    for k in range(K):
                        last = mm(ps[:, 0:E], h2T[:, k, P * u:P * u + P], rw[:, k], start=k == 0, stop=k == K - 1)
                    done(last)
            ps = begin("rank")
            pe.wait_ge(sem("chosen"), 1)
            pe.wait_ge(sem("before_ready"), 1)
            for t in range(T):
                for s in range(t + 1):
                    mm(ps[:, E * t:E * t + E], ones if s < t else before, mask[:, s], start=s == 0, stop=s == t)
            for s in range(T):
                last = mm(ps[:, E * T:E * T + E], ones, mask[:, s], start=s == 0, stop=s == T - 1)
            done(last)
            ps = begin("table")
            for i in range(2 * T):
                pe.wait_ge(sem("table_parts"), i + 1)
                last = mm(ps[:, 0:80], in_slot[:, i // T, i % T], in_table[:, i // T, i % T], start=i == 0, stop=i == 2 * T - 1)
            done(last)
            for who in ("act", "dve"):
                pe.wait_ge(banks_read[who], seen[who])
            for s, n in (("gate_made", 2), ("up_made", 2), ("y_made", 4)):
                pe.sem_inc(sem(s), n)

            def transpose_rows(r, p, j):
                b = j % 2
                pe.wait_ge(sem(f"ld_xg{b}"), nth_of_half(pe, 16, r, p, j, 16))
                pe.wait_ge(sem("xT_act"), nth(pe, 1, r, p, j, 1))
                pe.wait_ge(sem("xT_dve"), nth(pe, 1, r, p, j, 1))
                for k in range(K):
                    last = tr(psum[:, k // 4, P * (k % 4):P * (k % 4) + P], xg[b][:, P * k:P * k + P], ident)
                    if k % 4 == 3:
                        last.then_inc(sem("xT_made"), 1)

            def gate(r, p, j):
                b = j % 2
                pe.wait_ge(sem("xT_act"), nth(pe, 1, r, p, j, 2))
                pe.wait_ge(sem("xT_dve"), nth(pe, 1, r, p, j, 2))
                pe.wait_ge(sem(f"ld_w_gate{b}"), nth_of_half(pe, 16, r, p, j, 16))
                pe.wait_ge(sem("silu_made"), nth(pe, 1, r, p, j, 1))
                for k in range(K):
                    last = mm(psum[:, 2], xgT[b][:, k], w_exp[b][0][:, k], start=k == 0, stop=k == K - 1)
                last.then_inc(sem("gate_made"), 1)

            def up(r, p, j):
                b = j % 2
                pe.wait_ge(sem(f"ld_w_up{b}"), nth_of_half(pe, 16, r, p, j, 16))
                pe.wait_ge(sem("he_made"), nth(pe, 1, r, p, j, 1))
                for k in range(K):
                    last = mm(psum[:, 3], xgT[b][:, k], w_exp[b][1][:, k], start=k == 0, stop=k == K - 1)
                last.then_inc(sem("up_made"), 1)

            def transpose_hidden(r, p, j):
                b = j % 2
                pe.wait_ge(sem("he_made"), nth(pe, 1, r, p, j, 2))
                pe.wait_ge(sem("heT_copied"), nth(pe, 1, r, p, j, 1))
                for k in range(4):
                    last = tr(psum[:, 4, P * k:P * k + P], he[b][:, P * k:P * k + P], ident)
                last.then_inc(sem("heT_made"), 1)

            def down(r, p, j):
                b = j % 2
                pe.wait_ge(sem(f"ld_w_down{b}"), nth_of_half(pe, 16, r, p, j, 16))
                pe.wait_ge(sem("heT_copied"), nth(pe, 1, r, p, j, 2))
                pe.wait_ge(sem("y_read_act"), nth(pe, 1, r, p, j, 1))
                pe.wait_ge(sem("y_read_dve"), nth(pe, 1, r, p, j, 1))
                for n in range(2):
                    for k in range(4):
                        last = mm(psum[:, 5 + n], heT[b][:, k], w_exp[b][2][:, k, 512 * n:512 * n + 512], start=k == 0, stop=k == 3)
                    last.then_inc(sem("y_made"), 1)

            def first(r):
                transpose_rows(r, 0, 0)
                gate(r, 0, 0)
                up(r, 0, 0)
                transpose_rows(r, 0, 1)

            def step(r, p, j):
                gate(r, p, j)
                transpose_hidden(r, p, j - 1)
                up(r, p, j)
                transpose_rows(r, p, j + 1)
                down(r, p, j - 1)

            def last(r):
                gate(r, 0, E - 1)
                transpose_hidden(r, 0, E - 2)
                up(r, 0, E - 1)
                down(r, 0, E - 2)
                transpose_hidden(r, 0, E - 1)
                down(r, 0, E - 1)

            in_steps(pe, 0, first, step, last)
            pe.wait_ge(sem("rounds_ready"), 1)
            n_rounds = pe.value_load(rounds[0:1, 0:1], min_val=1, max_val=4)
            with pe.If(n_rounds > 1):
                with pe.Fori(1, n_rounds) as r:
                    in_steps(pe, r, first, step, last)

        @block.scalar
        def _(act):
            link = chain(act, sem("scalar_step"))
            A = nc.scalar.activation

            def copied(dst, name, view, func=ACT.Copy, **kw):
                wait_product(act, *name)
                link(A(dst, view, func, **kw), banks_read["act"])

            def rsqrt(dst, src, scale, signal):
                link(A(dst, src, ACT.Ln, bias=eps[:, 0:1], scale=scale))
                link(A(dst, dst, ACT.Exp, scale=-0.5), signal)

            def head_squares(which, t, o):
                for h in range(H):
                    link(A(junk_head, o[:, DH * h:DH * h + DH], ACT.Square, accum_out=head_ss[which][:, t, h:h + 1]))

            def head_rsqrt(which, t):
                rsqrt(head_ss[which][:, t], head_ss[which][:, t], 1.0 / DH, sem(f"rs_{which}"))

            act.wait_ge(sem("consts"), 1)
            act.wait_ge(sem("ld_c"), 16)
            link(A(acol, ccol, ACT.Silu), sem("c_ready"))
            act.wait_ge(sem("ld_x"), 16)
            for t in range(T):
                link(A(squares, x[:, t], ACT.Square, accum_out=ss[:, t:t + 1]))
            rsqrt(rs, ss, 1.0 / D, sem("rs1_ready"))
            for b in range(4):
                copied(mod1[:, b // 2, 512 * (b % 2):512 * (b % 2) + 512], ("mod", b), bank("mod", b))
            for t in range(T):
                copied(hT[:, 4:8, P * t:P * t + P], ("hT", t, 1), bank("hT", t, 1).rearrange("p (k n) -> p k n", k=4))
            act.wait_ge(sem("ld_bcol"), 16 * 7)
            act.wait_ge(sem("pads"), 1)
            for c in range(13):
                dst = zpad[:, c, 3:3 + SEQ] if c < 6 else zb[:, c - 6]
                copied(dst, ("zf", c), bank("zf", c), func=ACT.Identity, bias=bcol[:, c:c + 1])
                if c >= 5:
                    for b in range(4 + 2 * (c - 5), 6 + 2 * (c - 5)):
                        m = b - 4
                        copied(mod2[:, m // 4, 256 * (m % 4):256 * (m % 4) + 256], ("mod", b), bank("mod", b)[:, 0:256])
                if 3 <= c < 9:
                    act.wait_ge(sem("conv_ready"), c - 2)
                    link(A(zpad[:, c - 3, 0:SEQ], cring[(c - 3) % 2], ACT.Silu), sem("silu_done"))
            for t in range(T):
                wait_read(act, "zt", t, 3)
                A(gab[:, t, 0:256], gab[:, t, 0:256], ACT.Silu).then_inc(sem("gate_silu"), 1)
            for t in range(T):
                link(A(uv[:, t], uv[:, t], ACT.Gelu_apprx_tanh), sem("gelu"))
                head_squares("sgu", t, uv[:, t, 256:512])
            act.wait_ge(sem("alpha_abs"), 1)
            link(A(tA, tA, ACT.Exp, scale=-1.0))
            link(A(tA, tA, ACT.Ln, bias=1.0))
            link(A(alog, alog, ACT.Exp))
            link(A(tB, gab[:, :, 260:264], ACT.Exp, scale=-1.0), sem("softplus"))
            s16 = head_ss["sgu"].rearrange("p t h -> p (t h)")
            rsqrt(s16, s16, 1.0 / DH, sem("rs_sgu"))
            for t in range(T):
                copied(qkv_tm[:, t, 0:512], ("qk_tm", t), bank("qk_tm", t))
            for t in range(T):
                copied(qkv_tm[:, t, 512:768], ("v_tm", t), bank("v_tm", t)[:, 0:256])
            act.wait_ge(sem("qk_squares"), T)
            rsqrt(nrs, nss, 1.0, sem("qk_rs"))
            wait_read(act, "gcum")
            link(A(egc, gc, ACT.Exp), sem("egc_ready"))
            for t in range(T):
                act.wait_ge(sem("gdiff"), t + 1)
                link(A(B1[:, t], B1[:, t], ACT.Exp, scale=-1.0), sem("decay"))
                link(A(AT[:, t], AT[:, t], ACT.Exp), sem("decay"))
            link(A(etail, etail, ACT.Exp))
            link(A(egl, glast, ACT.Exp), sem("tails"))
            for nm, dst in (("kT", kT), ("qT", qT)):
                for t in range(T):
                    copied(dst[0:64, t], (nm, t), bank(nm, t)[0:64].rearrange("p (h n) -> p h n", h=H))

            def heads(*name):
                return bank(*name).rearrange("p (h n) -> p h n", h=H)

            for t in range(T):
                copied(B4[:, t], ("M", t), heads("M", t))
            for nm, dst in (("L2", B3), ("M2", B4), ("L4", B1)):
                for t in range(T):
                    if nm == "L4":
                        act.wait_ge(sem("R_first"), t + 1)
                    copied(dst[:, t], (nm, t), heads(nm, t))
            for lv in range(3):
                for nm, dst in (("Tm", B3), ("Z", B4)):
                    for t in range(T):
                        copied(dst[:, t], (nm, lv, t), heads(nm, lv, t))
            for t in range(T):
                copied(U[:, t], ("U", t), bank("U", t)[:, 0:256].rearrange("p (h n) -> p h n", h=H))
            act.wait_ge(sem("level_masked"), 3 * T)
            for nm, dst in (("WT", WT), ("QdT", QdT)):
                for t in range(T):
                    copied(dst[0:64, t], (nm, t), bank(nm, t)[0:64].rearrange("p (h n) -> p h n", h=H))
            act.wait_ge(sem("lam_sums"), 1)
            link(A(lam[:, 0:2], lam[:, 0:2], ACT.Exp), sem("lam_exp"))
            for t in range(T):
                wait_read(act, "AV", t)
                head_squares("gdn", t, o_tm[:, t, 0:256])
                head_rsqrt("gdn", t)
            for n in range(len(units) + 1):
                if n < len(units):
                    kind, t, h = units[n]
                    m8 = mx[:, n % 4]
                    cols = slice(0, P * (t + 1)) if kind == "diff" else slice(0 if t else P, 256)
                    act.wait_ge(sem("max_ready"), n + 1)
                    for m in range(2 if kind == "diff" else 1):
                        link(A(p_sb[n % 2][m][:, cols], s_sb[n % 2][m][:, cols], ACT.Exp, bias=m8[:, 2 + m:3 + m],
                               accum_out=m8[:, 4 + m:5 + m]), sem("exp_ready"))
                    if kind == "swa":
                        link(A(m8[:, 5:6], sink[:, h:h + 1], ACT.Exp, bias=m8[:, 2:3]), sem("exp_ready"))
                if n >= 1:
                    nb = n_blocks[n - 1]
                    copied(pT[(n - 1) % 2][:, 0:nb], ("pT", n - 1), bank("pT", n - 1)[:, 0:P * nb].rearrange("p (k n) -> p k n", n=P))
                if n >= 7 and n % 4 == 3 and (n - 7) // 4 < T:
                    t = (n - 7) // 4
                    wait_read(act, "pv", 4 * t + 3)
                    head_squares("diff", t, o_tm[:, t, 256:512])
                    head_rsqrt("diff", t)
            for t in range(T):
                copied(oT[:, 4:8, P * t:P * t + P], ("oT", t, 1), bank("oT", t, 1).rearrange("p (k n) -> p k n", k=4))
            for t in range(T + 1):
                if t < T:
                    act.wait_ge(sem("x1_ready"), 2 * t + 2)
                    link(A(junk1k, x[:, t], ACT.Square, accum_out=ss[:, t:t + 1]))
                    rsqrt(rs[:, t:t + 1], ss[:, t:t + 1], 1.0 / D, sem("rs2_ready"))
                if t >= 1:
                    copied(h2T[:, 4:8, P * (t - 1):P * t], ("h2T", t - 1, 1), bank("h2T", t - 1, 1).rearrange("p (k n) -> p k n", k=4))
            wait_read(act, "logit", T - 1)
            link(A(scores, scores, ACT.Exp, scale=-1.0), sem("exp_logits"))
            for s in ("xT_act", "silu_made", "heT_copied", "y_read_act"):
                act.sem_inc(sem(s), 1)

            def copy_rows(r, p, j):
                act.wait_ge(sem("xT_made"), nth(act, 2, r, p, j, 1))
                A(xgT[j % 2][:, 0:4], psum[:, 0].rearrange("p (k n) -> p k n", n=P), ACT.Copy).then_inc(sem("xT_act"), 1)

            def silu(r, p, j):
                act.wait_ge(sem("gate_made"), nth(act, 1, r, p, j, 3))
                A(gated[j % 2], psum[:, 2], ACT.Silu).then_inc(sem("silu_made"), 1)

            def copy_hidden(r, p, j):
                act.wait_ge(sem("heT_made"), nth(act, 1, r, p, j, 1))
                A(heT[j % 2], psum[:, 4].rearrange("p (k n) -> p k n", n=P), ACT.Copy).then_inc(sem("heT_copied"), 1)

            def copy_y(r, p, j):
                b = j % 2
                act.wait_ge(sem("y_made"), nth(act, 2, r, p, j, 5))
                act.wait_ge(sem(f"slot_free{b}"), nth_of_half(act, 1, r, p, j, 1))
                A(yo[b][:, 0:512], psum[:, 5], ACT.Copy).then_inc(sem("y_read_act"), 1)

            def first(r):
                copy_rows(r, 0, 0)
                silu(r, 0, 0)
                copy_rows(r, 0, 1)

            def step(r, p, j):
                silu(r, p, j)
                copy_hidden(r, p, j - 1)
                copy_rows(r, p, j + 1)
                copy_y(r, p, j - 1)

            def last(r):
                silu(r, 0, E - 1)
                for j in (E - 2, E - 1):
                    copy_hidden(r, 0, j)
                    copy_y(r, 0, j)

            in_steps(act, 0, first, step, last)
            act.wait_ge(sem("rounds_ready"), 1)
            n_rounds = act.value_load(rounds[0:1, 0:1], min_val=1, max_val=4)
            with act.If(n_rounds > 1):
                with act.Fori(1, n_rounds) as r:
                    in_steps(act, r, first, step, last)
            for t in range(T):
                act.wait_ge(sem("x2_ready"), t + 1)
                link(A(junk_last, x[:, t], ACT.Square, accum_out=ss[:, t:t + 1]))
                rsqrt(rs[:, t:t + 1], ss[:, t:t + 1], 1.0 / D, sem("rs3_ready"))

        @block.vector
        def _(dve):
            link = chain(dve, sem("vector_step"))
            v = nc.vector
            TT, TS, STT = v.tensor_tensor, v.tensor_scalar, v.scalar_tensor_tensor

            def read(ins):
                link(ins, banks_read["dve"])

            def conv(c):
                wait_read(dve, "zf", c)
                if c == 0:
                    dve.wait_ge(sem("ld_conv"), 64)
                if c >= 2:
                    dve.wait_ge(sem("silu_done"), c - 1)
                y = cring[c % 2]
                link(TS(y, zpad[:, c, 0:SEQ], convc[:, c, 0:1], None, ALU.mult))
                for i in range(1, 4):
                    ins = STT(y, zpad[:, c, i:i + SEQ], convc[:, c, i:i + 1], y, ALU.mult, ALU.add)
                    link(ins, sem("conv_ready") if i == 3 else sem("vector_step"))

            def ada(b):
                if b < 4:
                    w, n, br = ada_first[b], 512, brow_first[:, 512 * b:512 * b + 512]
                    dve.wait_ge(sem(f"ld_ada{b}"), 16)
                else:
                    w, n, br = ada_rest[b % 2], 256, brow[b % 2]
                    dve.wait_ge(sem(f"ld_adar{b % 2}"), 32 * (b // 2 - 1))
                if b >= 2:
                    wait_product(dve, "mod", b - 2)
                acc = acc_ring[b % 2][:, 0:n]
                link(TS(acc, w[:, 0], acol[:, 0:1], None, ALU.mult))
                for j in range(1, 8):
                    link(STT(acc, w[:, j], acol[:, j:j + 1], acc, ALU.mult, ALU.add))
                if b == 0:
                    dve.wait_ge(sem("ld_brow"), 16)
                link(TT(acc[0:1], acc[0:1], br[0:1], ALU.add), sem("acc_ready"))

            dve.wait_ge(sem("c_ready"), 1)
            for b in range(4):
                ada(b)
            dve.wait_ge(sem("ld_n1"), 16)
            wait_read(dve, "mod", 3)
            link(STT(mod1[:, 1], mod1[:, 1], 1.0, n1bc, ALU.add, ALU.mult))
            dve.wait_ge(sem("rs1_ready"), 1)
            dve.wait_ge(sem("ld_x"), 16)
            for t in range(T):
                if t >= 2:
                    wait_product(dve, "hT", t - 2, 1)
                hr = h_ring[t % 2]
                link(STT(hr, x[:, t], rs[:, t:t + 1], mod1[:, 1], ALU.mult, ALU.mult))
                link(TT(hr, hr, mod1[:, 0], ALU.add), sem("h_ready"))
                if t:
                    wait_product(dve, "hT", t - 1, 0)
                    read(v.tensor_copy(hT[:, 0:4, P * (t - 1):P * t], bank("hT", t - 1, 0).rearrange("p (k n) -> p k n", k=4)))
            wait_product(dve, "hT", T - 1, 0)
            read(v.tensor_copy(hT[:, 0:4, P * (T - 1):P * T], bank("hT", T - 1, 0).rearrange("p (k n) -> p k n", k=4)))
            for c in range(4):
                conv(c)
            for c in range(5, 13):
                for i in range(2):
                    ada(4 + 2 * (c - 5) + i)
                if c < 7:
                    conv(c - 1)
            dve.wait_ge(sem("ld_btm"), 64)
            parts = ((gab, 0, 264, 0), (None, 0, 512, 264), (uv, 256, 256, 776), (dv, 0, P, 1032))
            for t in range(T):
                for s, (dst, c0, n, o) in enumerate(parts):
                    wait_product(dve, "zt", t, s)
                    ps = bank("zt", t, s)
                    if s == 1:
                        link(TT(bv[:, t], ps[:, 0:256], btm[:, 264:520], ALU.add))
                        read(TT(uv[:, t, 0:256], ps[:, 256:512], btm[:, 520:776], ALU.add))
                    else:
                        read(TT(dst[:, t, c0:c0 + n], ps[:, 0:n], btm[:, o:o + n], ALU.add))
            dve.wait_ge(sem("ld_small"), 16 * 10)
            link(TT(tC, gab[:, :, 256:260], dtb.unsqueeze(1).to_broadcast([P, T, H]), ALU.add))
            link(STT(tA, tC, -1.0, tC, ALU.mult, ALU.max), sem("alpha_abs"))
            dve.wait_ge(sem("softplus"), 1)
            link(STT(tC, tC, 0.0, tA, ALU.max, ALU.add))
            link(TS(alog, alog, -1.0, None, ALU.mult))
            link(TT(g_, tC, alog.unsqueeze(1).to_broadcast([P, T, H]), ALU.mult), sem("g_ready"))
            link(TS(tB, tB, 1.0, None, ALU.add))
            link(v.reciprocal(beta, tB))
            for t in range(T):
                wait_read(dve, "qk_tm", t)
                link(TT(sq, qkv_tm[:, t, 0:512], qkv_tm[:, t, 0:512], ALU.mult))
                ins = v.tensor_reduce(nss[:, t], sq.rearrange("p (n d) -> p n d", d=DH), AX.X, ALU.add)
                link(ins, sem("qk_squares"))
            dve.wait_ge(sem("qk_rs"), 1)
            link(TS(nrs[:, :, 0:4], nrs[:, :, 0:4], DH ** -0.5, None, ALU.mult))
            for t in range(T):
                qk = qkv_tm[:, t, 0:512].rearrange("p (n d) -> p n d", d=DH)
                link(TT(qk, qk, nrs[:, t].unsqueeze(2).to_broadcast([P, 8, DH]), ALU.mult), sem("qk_normed"))
            wait_product(dve, "gcum")
            read(v.tensor_copy(gc.rearrange("p t h -> p (t h)"), bank("gcum")[:, 0:16]))
            for t in range(T):
                wait_product(dve, "grow", t)
                ps = bank("grow", t).rearrange("p (h n) -> p h n", h=H)
                link(v.tensor_copy(glast[:, t], ps[:, :, 63::64]))
                read(TT(B1[:, t], ps, over_heads(gc[:, t], P), ALU.subtract))
                link(TS(AT[:, t], B1[:, t], 0.0, None, ALU.min))
                if t == T - 1:
                    for b in range(2):
                        r_ = slice(64 * b, 64 * b + 64)
                        link(TT(etail[r_], glast[r_, :, :, b], gc[r_], ALU.subtract))
                link(TS(B1[:, t], B1[:, t], 0.0, None, ALU.max), sem("gdiff"))

            def heads(*name):
                return bank(*name).rearrange("p (h n) -> p h n", h=H)

            for t in range(T):
                dve.wait_ge(sem("decay_masked"), 2 * t + 2)
                wait_product(dve, "kk", t)
                read(TT(Lf[:, t], heads("kk", t), B1[:, t], ALU.mult))
            for t in range(T):
                wait_product(dve, "kq", t)
                read(TT(AT[:, t], heads("kq", t), AT[:, t], ALU.mult))
            k_tm = qkv_tm[:, :, 256:512].rearrange("p t (h d) -> p t h d", d=DH)
            q_tm = qkv_tm[:, :, 0:256].rearrange("p t (h d) -> p t h d", d=DH)
            v_tm = qkv_tm[:, :, 512:768].rearrange("p t (h d) -> p t h d", d=DH)
            dve.wait_ge(sem("egc_ready"), 1)
            for t in range(T):
                link(TT(Qd[:, t], q_tm[:, t], over_heads(egc[:, t], DH), ALU.mult), sem("Qd_ready"))
            link(v.memset(S[0:64], 0.0), sem("S_ready"))
            for nm in ("Ra", "Rb"):
                for t in range(T):
                    wait_product(dve, nm, t)
                    read(TT(R[:, t], heads(nm, t), R[:, t], ALU.add))
            wait_read(dve, "v_tm", T - 1)
            for t in range(T):
                link(TT(vb[:, t], v_tm[:, t], over_heads(beta[:, t], DH), ALU.mult))
                link(TT(kbe[:, t], k_tm[:, t], over_heads(beta[:, t], DH), ALU.mult))
                link(TT(kbe[:, t], kbe[:, t], over_heads(egc[:, t], DH), ALU.mult), sem("vb_ready"))
            for lv in range(3):
                for t in range(T):
                    wait_product(dve, "R", lv, t)
                    read(TT(R[:, t], R[:, t], heads("R", lv, t), ALU.subtract))
            dve.wait_ge(sem("tails"), 1)
            for t in range(T):
                link(TT(ktail[:, t], k_tm[:, t], over_heads(etail[:, t], DH), ALU.mult))
            wait_read(dve, "U", T - 1)
            wait_product(dve, "sguT")
            read(v.tensor_copy(sgT.rearrange("p h n -> p (h n)"), bank("sguT")))
            link(v.memset(sgT[64:128, :, 0:64], 0.0), sem("sgT_ready"))
            link(TT(lamt[:, 0], lam4[:, 0], lam4[:, 1], ALU.mult))
            link(TT(lamt[:, 1], lam4[:, 2], lam4[:, 3], ALU.mult))
            link(v.tensor_reduce(lam[:, 0:2], lamt, AX.X, ALU.add), sem("lam_sums"))
            dve.wait_ge(sem("lam_exp"), 1)
            link(TT(lam[:, 2:3], lam[:, 1:2], lam[:, 0:1], ALU.subtract))
            link(TS(neglam, lam[:, 2:3], -LAM_INIT, None, ALU.add))
            dve.wait_ge(sem("gelu"), T)
            for ch in range(2 * T):
                t, b = ch // 2, 64 * (ch % 2)
                r_ = slice(b, b + 64)
                wait_product(dve, "WQ", ch)
                ps = bank("WQ", ch)[r_]
                link(TT(v_new[r_, t], U[r_, t], ps[:, 0:256].rearrange("p (h d) -> p h d", h=H), ALU.subtract), sem("v_new_ready"))
                read(v.tensor_copy(qs[r_, t], ps[:, 256:512].rearrange("p (h d) -> p h d", h=H)))
                link(TT(Stmp[0:64], S[0:64], egl[0:64, t, :, ch % 2].unsqueeze(2).to_broadcast([64, H, DH]), ALU.mult))
                wait_product(dve, "SU", ch)
                read(TT(S[0:64], Stmp[0:64], bank("SU", ch)[0:64, 0:256].rearrange("p (h d) -> p h d", h=H), ALU.add))
                if ch % 2:
                    wait_product(dve, "AV", t)
                    read(TT(o_tm[:, t, 0:256], qs[:, t].rearrange("p h d -> p (h d)"), bank("AV", t)[:, 0:256], ALU.add))
                    wait_product(dve, "mix", t)
                    ins = STT(o_tm[:, :, 512 + DH * t:512 + DH * t + DH], bank("mix", t)[:, 0:256].rearrange("p (t d) -> p t d", t=T),
                              sgb[:, t:t + 1], uv[:, :, DH * t:DH * t + DH], ALU.add, ALU.mult)
                    read(ins)

            dve.wait_ge(sem("biases"), 1)

            def spread(n):
                kind, t, h = units[n]
                return kind, t, h, slice(0, P * (t + 1)) if kind == "diff" else slice(0 if t else P, 256), mx[:, n % 4]

            def maxima(n):
                kind, t, h, cols, m8 = spread(n)
                for m in range(2 if kind == "diff" else 1):
                    wait_product(dve, "score", n, m)
                    bias = bias_diff[:, h, P * (3 - t):] if kind == "diff" else bias_swa[:, h, cols]
                    read(v.tensor_tensor_reduce(out=s_sb[n % 2][m][:, cols], in0=bank("score", n, m)[:, cols], in1=bias,
                                                scale=32 ** -0.5 if kind == "diff" else DH ** -0.5, scalar=-3e38,
                                                op0=ALU.add, op1=ALU.max, accum_out=m8[:, m:m + 1]))
                if kind == "swa":
                    link(TT(m8[:, 0:1], m8[:, 0:1], sink[:, h:h + 1], ALU.max))
                link(TS(m8[:, 2:4], m8[:, 0:2], -1.0, None, ALU.mult), sem("max_ready"))

            def weights(n):
                kind, t, h, cols, m8 = spread(n)
                dve.wait_ge(sem("exp_ready"), 2 * n + 2)
                if kind == "diff":
                    if n >= 2:
                        wait_product(dve, "pT", n - 2)
                    link(v.reciprocal(m8[:, 6:8], m8[:, 4:6]))
                    link(TS(m8[:, 7:8], m8[:, 7:8], neglam, m8[:, 4:5], ALU.mult, ALU.mult))
                    p0, p1 = (p_sb[n % 2][m][:, cols] for m in range(2))
                    link(STT(pc[n % 2][:, cols], p1, m8[:, 7:8], p0, ALU.mult, ALU.add), sem("p_ready"))
                else:
                    link(TT(m8[:, 4:5], m8[:, 4:5], m8[:, 5:6], ALU.add))
                    link(v.reciprocal(m8[:, 6:7], m8[:, 4:5]))

            def outputs(n):
                kind, t, h, cols, m8 = spread(n)
                c0 = (256 if kind == "diff" else 768) + DH * h
                wait_product(dve, "pv", n)
                read(TS(o_tm[:, t, c0:c0 + DH], bank("pv", n)[:, 0:DH], m8[:, 6:7], None, ALU.mult))

            for i in range(len(units) + 3):
                if i < len(units):
                    maxima(i)
                if 1 <= i <= len(units):
                    weights(i - 1)
                if i >= 3:
                    outputs(i - 3)
            for t in range(T):
                wait_product(dve, "oT", t, 0)
                read(v.tensor_copy(oT[:, 0:4, P * t:P * t + P], bank("oT", t, 0).rearrange("p (k n) -> p k n", k=4)))
            dve.wait_ge(sem("x_biased"), T)
            dve.wait_ge(sem("ld_n2"), 16)
            link(STT(mod2[:, 2], mod2[:, 2], 1.0, n2bc, ALU.add, ALU.mult))
            for t in range(T + 2):
                if t < T:
                    for n in range(2):
                        cols = slice(512 * n, 512 * n + 512)
                        wait_product(dve, "y", t, n)
                        read(TT(ytmp[n], bank("y", t, n), mod2[:, 0, cols], ALU.mult))
                        link(TT(x[:, t, cols], x[:, t, cols], ytmp[n], ALU.add), sem("x1_ready"))
                if 1 <= t <= T:
                    wait_product(dve, "h2T", t - 1, 0)
                    read(v.tensor_copy(h2T[:, 0:4, P * (t - 1):P * t], bank("h2T", t - 1, 0).rearrange("p (k n) -> p k n", k=4)))
                if t < T:
                    dve.wait_ge(sem("rs2_ready"), t + 1)
                    if t >= 2:
                        wait_product(dve, "h2T", t - 2, 1)
                        dve.wait_ge(sem(f"st_h2{t % 2}"), 16)
                    hr = h2_ring[t % 2]
                    link(STT(hr, x[:, t], rs[:, t:t + 1], mod2[:, 2], ALU.mult, ALU.mult))
                    link(TT(hr, hr, mod2[:, 1], ALU.add), sem("h2_ready"))
                if t >= 2:
                    wait_product(dve, "logit", t - 2)
                    read(v.tensor_copy(scores[:, t - 2], bank("logit", t - 2)[:, 0:E]))
            dve.wait_ge(sem("exp_logits"), 1)
            dve.wait_ge(sem("router_consts"), 1)
            link(TS(scores, scores, 1.0, None, ALU.add))
            link(v.reciprocal(scores, scores))
            link(TT(sel, scores, rb.unsqueeze(1).to_broadcast([P, T, E]), ALU.add))
            s4 = sel.rearrange("p t (g e) -> p t g e", e=4)
            hi1, hi2, lo1, lo2, top1, top2, gs, eq, geq, best = grp[:10]
            link(TT(hi1, s4[:, :, :, 0], s4[:, :, :, 1], ALU.max))
            link(TT(lo1, s4[:, :, :, 0], s4[:, :, :, 1], ALU.min))
            link(TT(hi2, s4[:, :, :, 2], s4[:, :, :, 3], ALU.max))
            link(TT(lo2, s4[:, :, :, 2], s4[:, :, :, 3], ALU.min))
            link(TT(top1, hi1, hi2, ALU.max))
            link(TT(top2, hi1, hi2, ALU.min))
            link(TT(lo1, lo1, lo2, ALU.max))
            link(TT(top2, top2, lo1, ALU.max))
            link(TT(gs, top1, top2, ALU.add))

            def first_best(dst, val, weight, c, tmp, n):
                link(v.tensor_reduce(c, val, AX.X, ALU.max))
                link(TT(tmp, val, c.unsqueeze(2).to_broadcast([P, T, n]), ALU.is_equal))
                link(TT(tmp, tmp, weight, ALU.mult))
                link(v.tensor_reduce(c, tmp, AX.X, ALU.max))
                link(TT(dst, tmp, c.unsqueeze(2).to_broadcast([P, T, n]), ALU.is_equal))

            first_best(best, gs, gw, col[0], eq, 4)
            link(TS(geq, best, NEG, -NEG, ALU.mult, ALU.add))
            m4 = m16.rearrange("p t (g e) -> p t g e", e=4)
            for t in range(T):
                link(TT(m4[:, t], s4[:, t], best[:, t].unsqueeze(2).to_broadcast([P, 4, 4]), ALU.mult))
                link(TT(m4[:, t], m4[:, t], geq[:, t].unsqueeze(2).to_broadcast([P, 4, 4]), ALU.add))
            first_best(one1, m16, eweight, col[0], u16, E)
            link(STT(sel2, one1, -NEG, m16, ALU.mult, ALU.add))
            first_best(one2, sel2, eweight, col[0], u16, E)
            link(TT(mask, one1, one2, ALU.add), sem("chosen"))
            for k, one in enumerate((one1, one2)):
                link(TT(u16, one, scores, ALU.mult))
                link(v.tensor_reduce(wtok[:, k], u16, AX.X, ALU.add))
            link(TT(col[1], wtok[:, 0], wtok[:, 1], ALU.add))
            link(v.reciprocal(col[2], col[1]))
            for k in range(2):
                link(TT(wtok[:, k], wtok[:, k], col[2], ALU.mult))
            wait_product(dve, "rank")
            link(v.tensor_copy(rank.rearrange("p t e -> p (t e)"), bank("rank")[:, 0:E * T]))
            read(v.tensor_copy(counts, bank("rank")[:, E * T:E * T + E]))
            link(TS(u16, rank, 128.0, None, ALU.is_ge))
            for n in (256.0, 384.0):
                link(TS(v16, rank, n, None, ALU.is_ge))
                link(TT(u16, u16, v16, ALU.add))
            link(STT(rank, u16, -128.0, rank, ALU.mult, ALU.add))
            link(STT(u16, u16, 16.0, eidx, ALU.mult, ALU.add))
            for k, one in enumerate((one1, one2)):
                link(TT(v16, one, rank, ALU.mult))
                link(v.tensor_reduce(col[4], v16, AX.X, ALU.add))
                link(TT(v16, one, u16, ALU.mult))
                link(v.tensor_reduce(col[5], v16, AX.X, ALU.add))
                for t in range(T):
                    link(TS(in_slot[:, k, t], slot_no, col[4][:, t:t + 1], None, ALU.is_equal))
                    link(TS(in_table[:, k, t], column_no, col[5][:, t:t + 1], pair[:, k, t:t + 1], ALU.is_equal, ALU.mult), sem("table_parts"))
            link(v.tensor_reduce(col[6][:, 0:1], counts, AX.X, ALU.max))
            link(TS(col[7][:, 0:1], col[6][:, 0:1], 128.0, 1.0, ALU.is_gt, ALU.add))
            for n in (256.0, 384.0):
                link(TS(col[8][:, 0:1], col[6][:, 0:1], n, None, ALU.is_gt))
                link(TT(col[7][:, 0:1], col[7][:, 0:1], col[8][:, 0:1], ALU.add))
            link(v.tensor_copy(rounds, col[7][:, 0:1]), sem("rounds_ready"))
            wait_product(dve, "table")
            link(TS(tablef, bank("table")[:, 0:80], 8.0 * SEQ, None, ALU.add))
            read(v.tensor_copy(table, tablef))
            link(TS(tokens, table, 1, None, ALU.logical_shift_right))
            for s in ("xT_dve", "he_made", "y_read_dve"):
                dve.sem_inc(sem(s), 1)

            def gather_indices(r, p, j):
                v.tensor_copy(idx_g[j % 2], tokens[:, bass.ds(nth(dve, 1, r, p, j, 0), 1)]).then_inc(sem(f"idx_ready{j % 2}"), 1)

            def copy_rows(r, p, j):
                dve.wait_ge(sem("xT_made"), nth(dve, 2, r, p, j, 2))
                v.tensor_copy(xgT[j % 2][:, 4:8], psum[:, 1].rearrange("p (k n) -> p k n", n=P)).then_inc(sem("xT_dve"), 1)
                gather_indices(r, p, j + 2)

            def hidden(r, p, j):
                b = j % 2
                dve.wait_ge(sem("silu_made"), nth(dve, 1, r, p, j, 2))
                dve.wait_ge(sem("up_made"), nth(dve, 1, r, p, j, 3))
                TT(he[b], gated[b], psum[:, 3], ALU.mult).then_inc(sem("he_made"), 1)

            def copy_y(r, p, j):
                b = j % 2
                dve.wait_ge(sem(f"slot_free{b}"), nth_of_half(dve, 1, r, p, j, 1))
                v.tensor_copy(idx_s[b], table[:, bass.ds(nth(dve, 1, r, p, j, 0), 1)])
                dve.wait_ge(sem("y_made"), nth(dve, 2, r, p, j, 6))
                v.tensor_copy(yo[b][:, 512:1024], psum[:, 6]).then_inc(sem("y_read_dve"), 1)

            def first(r):
                copy_rows(r, 0, 0)
                hidden(r, 0, 0)
                copy_rows(r, 0, 1)

            def step(r, p, j):
                hidden(r, p, j)
                copy_rows(r, p, j + 1)
                copy_y(r, p, j - 1)

            def last(r):
                hidden(r, 0, E - 1)
                copy_y(r, 0, E - 2)
                copy_y(r, 0, E - 1)

            for j in range(2):
                gather_indices(0, 0, j)
            in_steps(dve, 0, first, step, last)
            n_rounds = dve.value_load(rounds[0:1, 0:1], min_val=1, max_val=4)
            with dve.If(n_rounds > 1):
                with dve.Fori(1, n_rounds) as r:
                    in_steps(dve, r, first, step, last)

            def store_tile(t):
                dve.wait_ge(sem("rs3_ready"), t + 1)
                if t == 0:
                    dve.wait_ge(sem("ld_fn"), 16)
                if t >= 2:
                    dve.wait_ge(sem(f"st_out{t % 2}"), 16)
                link(STT(fout[t % 2], x[:, t], rs[:, t:t + 1], fbc, ALU.mult, ALU.mult), sem("out_ready"))

            for t in range(T + 1):
                if t == T:
                    store_tile(t - 1)
                    break
                dve.wait_ge(sem(f"ld_yb{t % 2}"), 16 * (t // 2 + 1))
                link(TS(ym, yb[t % 2][:, 0], wtok[:, 0, t:t + 1], None, ALU.mult))
                link(STT(ym, yb[t % 2][:, 1], wtok[:, 1, t:t + 1], ym, ALU.mult, ALU.add), sem("yb_used"))
                link(TT(ym, ym, mod2[:, 3], ALU.mult))
                link(TT(x[:, t], x[:, t], ym, ALU.add), sem("x2_ready"))
                if t >= 1:
                    store_tile(t - 1)


def kernel(**inputs):
    from concourse import bacc
    from concourse.bass_utils import run_bass_kernel_spmd

    nc = bacc.Bacc("TRN2", target_bir_lowering=False, num_devices=1)
    arrays = {f"in_{n}": np.ascontiguousarray(inputs[n]) for n in INPUTS}
    aps = {n: nc.dram_tensor(f"in_{n}", arrays[f"in_{n}"].shape, mybir.dt.from_np(arrays[f"in_{n}"].dtype),
                             kind="ExternalInput").ap() for n in INPUTS}
    out = nc.dram_tensor("out_y", (1, SEQ, D), F32, kind="ExternalOutput").ap()
    build(nc, aps, out)
    return run_bass_kernel_spmd(nc, [arrays], core_ids=[0]).results[0]["out_y"]
```

```python
import math

import numpy as np

import concourse.bass as bass
from concourse import mybir

F32 = mybir.dt.float32
BF16 = mybir.dt.bfloat16
I32 = mybir.dt.int32
ALU = mybir.AluOpType
ACT = mybir.ActivationFunctionType
AX = mybir.AxisListType

P = 128
D = 1024
SEQ = 512
T = SEQ // P
K = D // P
H = 4
DH = 64
E = 16
F = 512
EPS = 1e-6
LAM_INIT = 0.8 - 0.6 * math.exp(0.0)
NEG = 1e30
KB = 1024
BASE = 16512

C_QKV, C_GATE, C_BQ, C_BK, C_BV, C_UV, C_DQ, C_DK, C_DV = 0, 768, 1032, 1288, 1544, 1800, 2312, 2568, 2696

INPUTS = ["x", "c", "norm1", "norm2", "w_ada", "b_ada", "w_in", "b_in", "w_out", "b_out", "conv_w", "a_log",
          "dt_bias", "gdn_norm", "lam_q1", "lam_k1", "lam_q2", "lam_k2", "diff_norm", "sgu_norm", "sgu_w",
          "sgu_b", "sinks", "router_w", "router_b", "w_gate", "w_up", "w_down", "final_norm"]


def products():
    out = [(("mod", b), "dve") for b in range(2)]
    for t in range(T):
        if t == T - 1:
            out += [(("mod", 2), "dve")]
        out += [(("hT", t, g), "act") for g in range(2)]
    out += [(("mod", 3), "dve")]
    for c in range(13):
        out += [(("zf", c), "act")]
        if c >= 1:
            out += [(("mod", 3 + c), "act")]
    for t in range(T):
        out += [(("mod", 16 + t), "act"), (("zt", t, 0), "dve")]
    out += [(("qk_tm", t), "act") for t in range(T)] + [(("v_tm", t), "act") for t in range(T)]
    out += [(("zt", 0, s), "dve") for s in (1, 2, 3)]
    out += [(("gcum",), "dve")] + [(("zt", 1, s), "dve") for s in (1, 2, 3)]
    out += [(("grow", t), "dve") for t in range(T)]
    out += [(("zt", t, s), "dve") for t in (2, 3) for s in (1, 2, 3)]
    out += [(("kT", t), "act") for t in range(T)] + [(("qT", t), "act") for t in range(T)]
    out += [(("kk", t), "dve") for t in range(T)] + [(("kq", t), "dve") for t in range(T)]
    out += [(("sguT",), "dve")] + [(("M", t), "act") for t in range(T)]
    for step, who in (("L2", "act"), ("M2", "act"), ("L4", "act"), ("Ra", "dve"), ("Rb", "dve")):
        out += [((step, t), who) for t in range(T)]
    for lv in range(3):
        for step, who in (("Tm", "act"), ("Z", "act"), ("R", "dve")):
            out += [((step, lv, t), who) for t in range(T)]
    units = attention_units()

    def scores(n):
        return [(("score", n, m), "dve") for m in range(2 if units[n][0] == "diff" else 1)] if n < len(units) else []

    def rest(n):
        part = [(("pT", n - 1), "act")] if 1 <= n <= len(units) else []
        return part + ([(("pv", n - 2), "dve")] if n >= 2 else [])

    out += scores(0)
    out += [(("U", t), "act") for t in range(T)] + [(("WT", t), "act") for t in range(T)]
    out += [(("QdT", t), "act") for t in range(T)]
    for n in range(2 * T):
        out += [(("WQ", n), "dve")] + scores(n + 1) + [(("SU", n), "dve")] + rest(n)
        if n % 2:
            out += [(("AV", n // 2), "dve"), (("mix", n // 2), "dve")]
    for n in range(2 * T, len(units) + 2):
        out += scores(n + 1) + rest(n)
    out += [(("oT", t, g), "act" if g else "dve") for t in range(T) for g in range(2)]
    for t in range(T + 2):
        if t < T:
            out += [(("y", t, n), "dve") for n in range(2)]
        h2T = [(("h2T", t - 1, g), "act" if g else "dve") for g in range(2)] if 1 <= t <= T else []
        logit = [(("logit", t - 2), "dve")] if t >= 2 else []
        out += h2T + logit if t < T else logit + h2T
    out += [(("rank",), "dve"), (("table",), "dve")]
    return out


def attention_units():
    return [("diff", t, h) for t in reversed(range(T)) for h in range(H)] + [("swa", t, h) for t in range(T) for h in range(H)]


def slopes():
    s = [2.0 ** (-8.0 * (i + 1) / 8) for i in range(8)]
    return s[0::2], s[1::2]


def build(nc, a, out):
    order = products()
    number = {name: n for n, (name, _) in enumerate(order)}
    assert len(number) == len(order)
    reader_count = []
    seen = {"act": 0, "dve": 0}
    for _, who in order:
        seen[who] += 1
        reader_count.append(seen[who])

    sems = {}

    def sem(name):
        if name not in sems:
            sems[name] = nc.alloc_semaphore(name)
        return sems[name]

    product_ready = sem("product_ready")
    banks_read = {"act": sem("banks_read_by_scalar"), "dve": sem("banks_read_by_vector")}

    def at(name, shape, dt, kb):
        t = nc.alloc_sbuf_tensor_at(name, [P] + shape, dt, offset=BASE + int(kb * KB))
        assert BASE + kb * KB + math.prod(shape) * 4 <= 229344, name
        return t.ap()

    x = at("x", [T, D], F32, 0)
    mod2 = at("mod2", [4, D], F32, 16)
    hT = at("hT", [K, SEQ], F32, 32)
    ada_rest = [at(f"ada_rest{i}", [K, 256], F32, 48 + 8 * i) for i in range(2)]
    zpad = at("zpad", [6, SEQ + 3], F32, 64)
    zb = at("zb", [7, SEQ], F32, 77)
    h_ring = [at(f"h_ring{i}", [D], F32, 77 + 4 * i) for i in range(2)]
    gab = at("gab", [T, 264], F32, 91)
    bv = at("bv", [T, 256], F32, 96)
    uv = at("uv", [T, 512], F32, 100)
    dv = at("dv", [T, 128], F32, 108)
    acc_ring = [at(f"acc_ring{i}", [512], F32, 110 + 2 * i) for i in range(2)]
    W = 114
    w_qkv = at("w_qkv", [K, 768], F32, W)
    w_b = at("w_b", [K, 512], F32, W + 24)
    w_d = at("w_d", [K, 384], F32, W + 40)
    w_g = at("w_g", [K, 264], F32, W + 52)
    w_v = at("w_v", [K, P], F32, W + 60.25)
    w_t = at("w_t", [K, 512], F32, W)
    w_u = at("w_u", [K, 256], F32, W + 16)
    ada_first = [at(f"ada_first{i}", [K, 512], F32, p) for i, p in enumerate((W + 24, W + 40, W + 56, 91))]
    btm = at("btm", [1160], F32, 186)
    brow = [at(f"brow{i}", [256], F32, 191 + i) for i in range(2)]
    cring = [at(f"cring{i}", [SEQ], F32, 193 + 2 * i) for i in range(2)]
    squares = at("squares", [D], F32, 86)
    o_tm = at("o_tm", [T, D], F32, W)
    qkv_tm = at("qkv_tm", [T, 768], F32, 138)
    AT = at("AT", [T, H, P], F32, 158)
    Lf = at("Lf", [T, H, P], F32, 130)
    B1 = at("B1", [T, H, P], F32, 150)
    B2 = at("B2", [T, H, P], F32, 166)
    B3 = at("B3", [T, H, P], F32, 174)
    B4 = at("B4", [T, H, P], F32, 182)
    R = at("R", [T, H, P], F32, 190)
    kT = at("kT", [T, H, P], F32, 32)
    qT = at("qT", [T, H, P], F32, 40)
    WT = at("WT", [T, H, P], F32, 130)
    QdT = at("QdT", [T, H, P], F32, 166)
    vb = at("vb", [T, H, DH], F32, 150)
    kbe = at("kbe", [T, H, DH], F32, 154)
    U = at("U", [T, H, DH], F32, 174)
    ktail = at("ktail", [T, H, DH], F32, 178)
    v_new = at("v_new", [T, H, DH], F32, 182)
    qs = at("qs", [T, H, DH], F32, 186)
    Qd = at("Qd", [T, H, DH], F32, 48)
    S = at("S", [H, DH], F32, 52)
    Stmp = at("Stmp", [H, DH], F32, 53)
    bias_diff = at("bias_diff", [H, SEQ], F32, 64)
    bias_swa = at("bias_swa", [H, 256], F32, 72)
    s_sb = [[at(f"s_sb{i}{m}", [SEQ], F32, 138 + 4 * i + 2 * m) for m in range(2)] for i in range(2)]
    p_sb = [[at(f"p_sb{i}{m}", [SEQ], F32, 146 + 4 * i + 2 * m) for m in range(2)] for i in range(2)]
    pc = [at(f"pc{i}", [SEQ], F32, 154 + 2 * i) for i in range(2)]
    pT = [at(f"pT{i}", [4, P], F32, 190 + 2 * i) for i in range(2)]
    wide = at("wide", [SEQ], F32, 110)
    bobc = at("bobc", [D], F32, 110)
    n2bc = at("n2bc", [D], F32, 130)
    junk1k = at("junk1k", [D], F32, 110)
    junk_last = at("junk_last", [D], F32, 72)
    before, ones16 = (at(nm, [P], BF16, 76 + 0.25 * i) for i, nm in enumerate(("before", "ones16")))
    mask = at("mask", [T, E], BF16, 73.75)
    scores, sel, m16, u16, sel2 = (at(nm, [T, E], F32, 72 + 0.25 * i)
                                   for i, nm in enumerate(("scores", "sel", "m16", "u16", "sel2")))
    chosen_k, v32, u32 = (at(nm, [2, T, E], F32, 74 + 0.5 * i) for i, nm in enumerate(("chosen_k", "v32", "u32")))
    one1, one2 = chosen_k[:, 0], chosen_k[:, 1]
    slot, column = (at(nm, [2, T], F32, 75.5 + 0.03125 * i) for i, nm in enumerate(("slot", "column")))
    sq = at("sq", [2 * H * DH], F32, 194)
    sgw = at("sgw", [H, P], F32, 54)
    sgT = at("sgT", [H, P], F32, 56)
    w_o = [at(f"w_o{i}", [K, 512], F32, 32 + 16 * i) for i in range(2)]
    oT = at("oT", [K, SEQ], F32, 64)
    ytmp = [at(f"ytmp{i}", [512], F32, 104 + 2 * i) for i in range(2)]
    h2_ring = [at(f"h2_ring{i}", [D], F32, 96 + 4 * i) for i in range(2)]
    h2T = at("h2T", [K, SEQ], F32, 80)
    off = [198.0]

    def small(name, shape, dt=F32):
        n = math.prod(shape) * 4 / KB
        off[0] = math.ceil(off[0] * 32) / 32
        off[0] += n
        return at(name, shape, dt, off[0] - n)

    ident = small("ident", [P])
    ones = small("ones", [P])
    tri = small("tri", [P])
    mask_s = small("mask_s", [P])
    mlv = [small(f"mlv{i}", [P]) for i in range(4)]
    m8T = small("m8T", [P])
    acol = small("acol", [8])
    ccol = small("ccol", [8])
    ss = small("ss", [T])
    rs = small("rs", [T])
    bcol = small("bcol", [13])
    bmod = small("bmod", [2, K])
    modT = small("modT", [2, K])
    n1col = small("n1col", [K])
    convc = small("convc", [6, 4])
    g_ = small("g_", [T, H])
    beta = small("beta", [T, H])
    gc = small("gc", [T, H])
    egc = small("egc", [T, H])
    nss = small("nss", [T, 8])
    nrs = small("nrs", [T, 8])
    head_ss = {nm: small(f"ss_{nm}", [T, H]) for nm in ("gdn", "diff", "sgu")}
    junk_head = small("junk_head", [DH])
    glast = small("glast", [T, H, 2])
    etail = small("etail", [T, H])
    egl = small("egl", [T, H, 2])
    alog = small("alog", [H])
    dtb = small("dtb", [H])
    sink = small("sink", [H])
    gnorm = small("gnorm", [DH])
    dnorm = small("dnorm", [DH])
    lam4 = small("lam4", [4, 32])
    lamt = small("lamt", [2, 32])
    lam = small("lam", [4])
    sgb = small("sgb", [H])
    mx = small("mx", [4, 8])
    snorm = small("snorm", [256])
    rb = small("rb", [E])
    rw = small("rw", [K, E])
    tA = small("tA", [T, H])
    tB = small("tB", [T, H])
    tC = small("tC", [T, H])
    wtok = small("wtok", [2, T])
    eps = small("eps", [1])
    junk = small("junk", [1])
    neglam = small("neglam", [1])
    rounds = small("rounds", [1], I32)
    table = at("table", [80], I32, 60)
    tokens = at("tokens", [80], I32, 60.5)
    idx_g = [small(f"idx_g{i}", [1], I32) for i in range(2)]
    idx_s = [small(f"idx_s{i}", [1], I32) for i in range(2)]
    w_exp = [[at(f"w_exp{b}{i}", [K, F] if i < 2 else [4, D], F32, p + 16 * i) for i in range(3)] for b, p in ((0, 150), (1, 102))]
    xg = [at(f"xg{b}", [D], F32, 32 + 4 * b) for b in range(2)]
    xgT = [at(f"xgT{b}", [K, P], F32, 40 + 4 * b) for b in range(2)]
    gated = [at(f"gated{b}", [F], F32, 48 + 2 * b) for b in range(2)]
    he = [at(f"he{b}", [F], F32, 52 + 2 * b) for b in range(2)]
    heT = [at(f"heT{b}", [4, P], F32, 56 + 2 * b) for b in range(2)]
    yo = [at(f"yo{b}", [D], F32, 64 + 4 * b) for b in range(2)]
    yb = [at(f"yb{t}", [2, D], F32, 102 + 8 * t) for t in range(T)]
    fbc = at("fbc", [D], F32, 76)
    fout = [at(f"fout{t}", [D], F32, 32 + 4 * t) for t in range(T)]
    h2_dram = nc.dram_tensor("h2_rows", [SEQ, D], F32).ap()
    y_dram = nc.dram_tensor("expert_rows", [2 * SEQ, D], F32).ap()
    in_slot = at("in_slot", [2, T, P], F32, 64)
    in_table = at("in_table", [2, T, 80], F32, 68)
    slot_no = at("slot_no", [P], F32, 70.5)
    column_no = at("column_no", [80], F32, 71)
    pair = at("pair", [2, T], F32, 71.375)

    def wait_product(eng, *name):
        eng.wait_ge(product_ready, number[name] + 1)

    def wait_read(eng, *name):
        eng.wait_ge(banks_read[order[number[name]][1]], reader_count[number[name]])

    def chain(eng, step):
        count = {}

        def link(ins, signal=step):
            count[signal] = count.get(signal, 0) + 1
            ins.then_inc(signal, 1)
            eng.wait_ge(signal, count[signal])
        return link

    def nth(eng, scale, r, p, j, plus):
        v = r * (E * scale) + p * (2 * scale) + (j * scale + plus)
        return v if isinstance(v, int) else eng.snap(v)

    def nth_of_half(eng, scale, r, p, j, plus):
        v = r * (E // 2 * scale) + p * scale + (j // 2 * scale + plus)
        return v if isinstance(v, int) else eng.snap(v)

    def in_steps(eng, r, first, step, last):
        first(r)
        with eng.Fori(0, E // 2 - 1) as p:
            for j in (1, 2):
                step(r, p, j)
        last(r)

    def over_heads(v, n):
        return v.unsqueeze(2).to_broadcast([P, H, n])

    def per_head(m):
        return m.unsqueeze(1).to_broadcast([P, H, m.shape[-1]])

    psum = nc.alloc_psum_tensor("psum", [P, 8, 512], F32).ap()

    def bank(*name):
        return psum[:, number[name] % 8]

    def row(v):
        return v.partition_broadcast(P)

    w_ada = a["w_ada"][0].rearrange("(p j) n -> p j n", j=8)
    w_in = a["w_in"][0].rearrange("(k p) n -> p k n", p=P)
    w_out = a["w_out"][0].rearrange("(k p) n -> p k n", p=P)
    b_in = a["b_in"][0]

    def first_block(b):
        return 1024 * (b % 2) + 512 * (b // 2)

    zt_parts = [(w_g, C_GATE, 264, 0), (w_t, C_BV, 512, 264), (w_u, C_BV + 512, 256, 776), (w_v, C_DV, P, 1032)]
    units = attention_units()
    n_blocks = []
    for kind, t, h in units:
        n_blocks.append(t + 1 if kind == "diff" else (2 if t else 1))
    grp = [at(f"grp{i}", [T, 4], F32, 76.5 + 0.0625 * i) for i in range(6)]
    hi8, lo8 = (at(nm, [T, 8], F32, 79.25 + 0.125 * i) for i, nm in enumerate(("hi8", "lo8")))
    col = [at(f"col{i}", [T], F32, 77.5 + 0.03125 * i) for i in range(16)]
    eidx = at("eidx", [T, E], F32, 78)
    gw = at("gw", [T, 4], F32, 78.25)
    eweight = at("eweight", [T, E], F32, 78.5)
    rank = at("rank", [T, E], F32, 78.75)
    counts = at("counts", [E], F32, 79)

    with nc.Block() as block:

        @block.sync
        def _(sp):
            sp.dma_start(ccol, a["c"][0].rearrange("(p j) -> p j", j=8)).then_inc(sem("ld_c"), 16)
            sp.dma_start(bmod, a["b_ada"][0, 0:2048].rearrange("(w k p) -> p w k", p=P, w=2), allow_slow_non_contiguous=True).then_inc(sem("ld_n1"), 16)
            sp.dma_start(n1col, a["norm1"][0].rearrange("(k p) -> p k", p=P), allow_slow_non_contiguous=True).then_inc(sem("ld_n1"), 16)
            xr = a["x"][0].rearrange("(t p) d -> p t d", p=P)
            for b in range(4):
                c0 = first_block(b)
                sp.dma_start(ada_first[b], w_ada[:, :, c0:c0 + 512]).then_inc(sem(f"ld_ada{b}"), 16)
                if b == 1:
                    sp.dma_start(x, xr).then_inc(sem("ld_x"), 16)
            sp.dma_start(bcol[:, 0:6], b_in[0:768].rearrange("(c p) -> p c", p=P), allow_slow_non_contiguous=True).then_inc(sem("ld_bcol"), 16)
            sp.dma_start(bcol[:, 6:10], b_in[C_BQ:C_BQ + 512].rearrange("(c p) -> p c", p=P), allow_slow_non_contiguous=True).then_inc(sem("ld_bcol"), 16)
            for g in range(2):
                for kv in range(2):
                    c0 = C_DQ + (2 * kv + g) * DH
                    sp.dma_start(bcol[DH * kv:DH * kv + DH, 10 + g:11 + g], b_in[c0:c0 + DH].unsqueeze(1), allow_slow_non_contiguous=True).then_inc(sem("ld_bcol"), 16)
            sp.dma_start(bcol[:, 12:13], b_in[C_DK:C_DK + P].unsqueeze(1), allow_slow_non_contiguous=True).then_inc(sem("ld_bcol"), 16)
            sp.dma_start(w_qkv, w_in[:, :, 0:768]).then_inc(sem("ld_w0"), 16)
            for i in range(4):
                sp.dma_start(convc[:, :, i], a["conv_w"][0, i].rearrange("(c p) -> p c", p=P), allow_slow_non_contiguous=True).then_inc(sem("ld_conv"), 16)
            for nm, dst in (("a_log", alog), ("dt_bias", dtb), ("sinks", sink), ("gdn_norm", gnorm), ("diff_norm", dnorm)):
                sp.dma_start(dst, row(a[nm][0])).then_inc(sem("ld_small"), 16)
            for i, nm in enumerate(("lam_q1", "lam_k1", "lam_q2", "lam_k2")):
                sp.dma_start(lam4[:, i], row(a[nm][0])).then_inc(sem("ld_small"), 16)
            sp.dma_start(sgb, a["sgu_b"][0].rearrange("g p -> p g"), allow_slow_non_contiguous=True).then_inc(sem("ld_small"), 16)
            sp.dma_start(snorm, row(a["sgu_norm"][0].rearrange("g c -> (g c)"))).then_inc(sem("ld_small"), 16)
            sp.dma_start(rb, row(a["router_b"])).then_inc(sem("ld_small"), 16)
            sp.dma_start(rw, a["router_w"].rearrange("(k p) e -> p k e", p=P)).then_inc(sem("ld_small"), 16)
            sp.wait_ge(sem("acc_ready"), 4)
            def ada_block(b):
                if b >= 6:
                    sp.wait_ge(sem("acc_ready"), b - 1)
                c0 = 2048 + 256 * (b - 4)
                sp.dma_start(ada_rest[b % 2], w_ada[:, :, c0:c0 + 256]).then_inc(sem(f"ld_adar{b % 2}"), 16)
                sp.dma_start(brow[b % 2][0:1], a["b_ada"][0:1, c0:c0 + 256]).then_inc(sem(f"ld_adar{b % 2}"), 16)

            ada_block(4)
            ada_block(5)
            sp.dma_start(w_b, w_in[:, :, C_BQ:C_BQ + 512]).then_inc(sem("ld_w1"), 16)
            ada_block(6)
            for g in range(2):
                for kv in range(2):
                    c0, o = C_DQ + (2 * kv + g) * DH, P * g + DH * kv
                    sp.dma_start(w_d[:, :, o:o + DH], w_in[:, :, c0:c0 + DH]).then_inc(sem("ld_w2"), 16)
            sp.dma_start(w_d[:, :, 256:384], w_in[:, :, C_DK:C_DK + P]).then_inc(sem("ld_w2"), 16)
            ada_block(7)
            sp.dma_start(w_g, w_in[:, :, C_GATE:C_GATE + 264]).then_inc(sem("ld_w3"), 16)
            sp.dma_start(w_v, w_in[:, :, C_DV:C_DV + P]).then_inc(sem("ld_w6"), 16)
            for i, (_, c0, n, o) in enumerate(zt_parts):
                sp.dma_start(btm[:, o:o + n], row(b_in[c0:c0 + n])).then_inc(sem("ld_btm"), 16)
            for b in range(8, 20):
                if b == 10:
                    wait_product(sp, "zf", 5)
                    sp.dma_start(w_t, w_in[:, :, C_BV:C_BV + 512]).then_inc(sem("ld_w4"), 16)
                    sp.dma_start(w_u, w_in[:, :, C_BV + 512:C_BV + 768]).then_inc(sem("ld_w5"), 16)
                ada_block(b)
            sp.wait_ge(sem("acc_ready"), 20)
            sp.dma_start(sgw, a["sgu_w"][0].rearrange("g i j -> i g j")).then_inc(sem("ld_sgw"), 16)
            wait_product(sp, "kq", T - 1)
            sp.dma_start(w_o[0], w_out[:, :, 0:512]).then_inc(sem("ld_wo"), 16)
            sp.wait_ge(sem("biases"), 1)
            sp.dma_start(bobc, row(a["b_out"][0])).then_inc(sem("ld_bo"), 16)
            wait_read(sp, "mix", H - 1)
            sp.dma_start(w_o[1], w_out[:, :, 512:1024]).then_inc(sem("ld_wo"), 16)
            sp.dma_start(n2bc, row(a["norm2"][0])).then_inc(sem("ld_n2"), 16)

            def load_expert(b, e, i, wait=True):
                for n, (nm, used) in enumerate((("w_gate", "gate_made"), ("w_up", "up_made"), ("w_down", "y_made"))):
                    src = a[nm][0, bass.ds(e, 1)].rearrange("o (k p) n -> p (o k) n", p=P)
                    if wait:
                        sp.wait_ge(sem(used), sp.snap(i + 1))
                    sp.dma_start(w_exp[b][n], src).then_inc(sem(f"ld_{nm}{b}"), 16)

            def load_rest(r):
                with sp.Fori(0, E // 2 - 1) as p:
                    for b in range(2):
                        load_expert(b, p * 2 + (b + 2), r * E + p * 2 + (b + 2))

            wait_read(sp, "oT", T - 1, 0)
            wait_read(sp, "oT", T - 1, 1)
            load_expert(0, 0, 0, wait=False)
            for t in range(T):
                sp.wait_ge(sem("h2_ready"), t + 1)
                sp.dma_start(h2_dram[P * t:P * t + P], h2_ring[t % 2]).then_inc(sem(f"st_h2{t % 2}"), 16)
            sp.wait_ge(sem("st_h20"), 32)
            sp.wait_ge(sem("st_h21"), 32)
            wait_product(sp, "h2T", T - 1, 1)
            load_expert(1, 1, 1, wait=False)
            load_rest(0)
            sp.wait_ge(sem("rounds_ready"), 1)
            n_rounds = sp.value_load(rounds[0:1, 0:1], min_val=1, max_val=4)
            with sp.If(n_rounds > 1):
                with sp.Fori(1, n_rounds) as r:
                    for b in range(2):
                        load_expert(b, b, r * E + b)
                    load_rest(r)
            sp.dma_start(fbc, row(a["final_norm"])).then_inc(sem("ld_fn"), 16)
            sp.wait_ge(sem("all_scattered"), 1)
            for t in range(T):
                for k in range(2):
                    sp.dma_start(yb[t][:, k], y_dram.rearrange("(t p k) d -> t k p d", p=P, k=2)[t, k]).then_inc(sem(f"ld_yb{t}{k}"), 16)
            for t in range(T):
                if t < T - 2:
                    sp.wait_ge(sem("out_ready"), t + 1)
                else:
                    sp.wait_ge(sem("last_ready"), t - (T - 2) + 1)
                sp.dma_start(out[0, P * t:P * t + P], fout[t]).then_inc(sem("st_out"), 16)
            sp.wait_ge(sem("st_out"), 16 * T)

        @block.gpsimd
        def _(gp):
            link = chain(gp, sem("pool_step"))
            g = nc.gpsimd

            def keep(m, pattern, base, cm, fill=0.0, op=ALU.is_ge):
                link(g.affine_select(out=m, in_=m, pattern=pattern, compare_op=op, fill=fill, base=base, channel_multiplier=cm))

            link(g.memset(ones, 1.0))
            link(g.memset(ident, 0.0))
            link(g.memset(eps, EPS))
            g.affine_select(out=ident, in_=ident, pattern=[[-1, P]], compare_op=ALU.not_equal, fill=1.0, base=0,
                            channel_multiplier=1).then_inc(sem("consts"), 1)
            g.memset(zpad[:, :, 0:3], 0.0).then_inc(sem("pads"), 1)
            for m, b_, cm, s in ((tri, 0, -1, 1), (mask_s, -1, 1, -1)):
                link(g.memset(m, 1.0))
                keep(m, [[s, P]], b_, cm)
            link(g.memset(tri[0:64, 64:128], 0.0))
            link(g.memset(mask_s[64:128, 0:64], 0.0))
            for i, n in enumerate((8, 16, 32, 64)):
                link(g.memset(mlv[i], 1.0))
                keep(mlv[i], [[n, P // n], [0, n]], n - 1, -1)
                if i == 0:
                    keep(mlv[i], [[-1, P]], -1, 1)
                else:
                    keep(mlv[i], [[-n // 2, 2 * P // n], [0, n // 2]], -n // 2, 1)
            link(g.memset(m8T, 1.0))
            keep(m8T, [[1, P]], -1, -1)
            link(g.affine_select(out=m8T, in_=m8T, pattern=[[-8, P // 8], [0, 8]], compare_op=ALU.is_ge, fill=0.0, base=0,
                                 channel_multiplier=1), sem("masks_ready"))

            def scale_heads(o, t, rs_, gain, signal):
                o4 = o.rearrange("p (h d) -> p h d", d=DH)
                link(g.tensor_tensor(o4, o4, over_heads(rs_[:, t], DH), ALU.mult))
                g.tensor_tensor(o4, o4, gain, ALU.mult).then_inc(signal, 1)

            gp.wait_ge(sem("ld_small"), 16 * 13)
            link(g.tensor_scalar(dnorm, dnorm, 1.0 - LAM_INIT, None, ALU.mult))
            wait_product(gp, "v_tm", T - 1)
            sd, sw = slopes()
            link(g.iota(wide, [[-1, SEQ]], base=SEQ - P, channel_multiplier=1, allow_small_or_imprecise_dtypes=True))
            link(g.tensor_scalar(bias_diff[:, 0], wide, 0.0, -2.0, ALU.min, ALU.mult))
            link(g.tensor_tensor(wide, wide, bias_diff[:, 0], ALU.add))
            for h in range(H):
                link(g.tensor_scalar(bias_diff[:, h], wide, -sd[h] * 32 ** 0.5, None, ALU.mult))
                link(g.tensor_scalar(bias_swa[:, h], wide[:, 256:512], -sw[h] * DH ** 0.5, None, ALU.mult))
            link(g.memset(bias_diff[0:64, :, 448:512], -NEG))
            link(g.memset(bias_swa[0:64, :, 0:64], -NEG))
            link(g.memset(bias_swa[0:64, :, 192:256], -NEG))
            link(g.memset(bias_swa[64:128, :, 0:128], -NEG))
            g.memset(wide[:, 0:1], 0.0).then_inc(sem("biases"), 1)
            for t in range(T):
                gp.wait_ge(sem("decay"), 2 * t + 2)
                link(g.tensor_tensor(B1[:, t], B1[:, t], per_head(mask_s), ALU.mult))
                g.tensor_tensor(B1[:, t], B1[:, t], over_heads(beta[:, t], P), ALU.mult).then_inc(sem("decay_masked"), 1)
                g.tensor_tensor(AT[:, t], AT[:, t], per_head(tri), ALU.mult).then_inc(sem("decay_masked"), 1)
            for t in range(T):
                gp.wait_ge(sem("eights"), t + 1)
                g.tensor_tensor(R[:, t], per_head(ident), B1[:, t], ALU.subtract).then_inc(sem("R_first"), 1)
            for lv in range(3):
                for t in range(T):
                    gp.wait_ge(product_ready, number[("M2", t) if lv == 0 else ("Z", lv - 1, t)] + 1)
                    g.tensor_tensor(B2[:, t], Lf[:, t], per_head(mlv[lv + 1]), ALU.mult).then_inc(sem("level_masked"), 1)
            gp.wait_ge(sem("level_masked"), 3 * T)
            gp.wait_ge(sem("rs_sgu"), 1)
            for t in range(T):
                scale_heads(uv[:, t, 256:512], t, head_ss["sgu"], snorm.rearrange("p (h d) -> p h d", d=DH), sem("vn_ready"))
            wait_read(gp, "mod", 19)
            gp.wait_ge(sem("ld_bo"), 16)
            link(g.tensor_tensor(bobc, bobc, mod2[:, 0], ALU.mult))
            for t in range(T):
                g.tensor_tensor(x[:, t], x[:, t], bobc, ALU.add).then_inc(sem("x_biased"), 1)
            for t in range(T):
                if t == 0:
                    gp.wait_ge(sem("rs_gdn"), 1)
                scale_heads(o_tm[:, t, 0:256], t, head_ss["gdn"], per_head(gnorm), sem("gdn_normed"))
                gp.wait_ge(sem("gdn_normed"), t + 1)
                g.tensor_tensor(o_tm[:, t, 0:256], o_tm[:, t, 0:256], gab[:, t, 0:256], ALU.mult).then_inc(sem("gdn_done"), 1)
            for t in range(T):
                if t == 0:
                    gp.wait_ge(sem("rs_diff"), 1)
                scale_heads(o_tm[:, t, 256:512], t, head_ss["diff"], per_head(dnorm), sem("diff_done"))
            wait_product(gp, "y", T - 1, 1)
            link(g.iota(eidx, [[0, T], [1, E]], base=0, channel_multiplier=0, allow_small_or_imprecise_dtypes=True))
            link(g.iota(eweight, [[0, T], [-1, E]], base=E, channel_multiplier=0, allow_small_or_imprecise_dtypes=True))
            link(g.iota(slot_no, [[1, P]], base=0, channel_multiplier=0, allow_small_or_imprecise_dtypes=True))
            link(g.iota(column_no, [[1, 80]], base=0, channel_multiplier=0, allow_small_or_imprecise_dtypes=True))
            link(g.iota(pair, [[1, 2], [2 * P, T]], base=-4 * SEQ * 2, channel_multiplier=2, allow_small_or_imprecise_dtypes=True))
            g.iota(gw, [[0, T], [-1, 4]], base=4, channel_multiplier=0, allow_small_or_imprecise_dtypes=True).then_inc(sem("router_consts"), 1)
            link(g.memset(ones16, 1.0))
            link(g.memset(before, 1.0))
            g.affine_select(out=before, in_=before, pattern=[[1, P]], compare_op=ALU.is_ge, fill=0.0, base=-1,
                            channel_multiplier=-1).then_inc(sem("before_ready"), 1)
            for b in range(2):
                g.memset(xg[b], 0.0).then_inc(sem("xg_cleared"), 1)
            gp.wait_ge(sem("xg_cleared"), 2)
            gp.wait_ge(sem("st_h20"), 32)
            gp.wait_ge(sem("st_h21"), 32)

            last_token, last_pair = gp.to_reg(SEQ - 1), gp.to_reg(2 * SEQ - 1)

            def gather(b):
                g.indirect_dma_start(xg[b], None, h2_dram, bass.IndirectOffsetOnAxis(idx_g[b], 0),
                                     bounds_check=last_token, oob_is_err=False).then_inc(sem(f"ld_xg{b}"), 16)

            def gather_next(r, p, j):
                b = j % 2
                gp.wait_ge(sem(f"idx_ready{b}"), nth_of_half(gp, 1, r, p, j, 2))
                gp.sem_inc(sem("gather_turn"), 1)
                gather(b)

            def scatter(r, p, j):
                b = j % 2
                done = nth_of_half(gp, 16, r, p, j, 16)
                gp.wait_ge(sem("y_read"), nth(gp, 1, r, p, j, 2))
                gp.sem_inc(sem("scatter_turn"), 1)
                g.indirect_dma_start(y_dram, bass.IndirectOffsetOnAxis(idx_s[b], 0), yo[b], None,
                                     bounds_check=last_pair, oob_is_err=False).then_inc(sem(f"scattered{b}"), 16)
                gp.wait_ge(sem(f"scattered{b}"), done)
                gp.sem_inc(sem(f"slot_free{b}"), 1)

            for b in range(2):
                gp.sem_inc(sem(f"slot_free{b}"), 1)
                gp.wait_ge(sem(f"idx_ready{b}"), 1)
                gather(b)

            def first(r):
                gather_next(r, 0, 0)
                gather_next(r, 0, 1)

            def step(r, p, j):
                gather_next(r, p, j + 1)
                scatter(r, p, j - 1)

            def last(r):
                scatter(r, 0, E - 2)
                scatter(r, 0, E - 1)

            in_steps(gp, 0, first, step, last)
            gp.wait_ge(sem("rounds_ready"), 1)
            n_rounds = gp.value_load(rounds[0:1, 0:1], min_val=1, max_val=4)
            with gp.If(n_rounds > 1):
                with gp.Fori(1, n_rounds) as r:
                    in_steps(gp, r, first, step, last)
            gathers = gp.snap((n_rounds * 8 + 1) * 16)
            for b in range(2):
                gp.wait_ge(sem(f"ld_xg{b}"), gathers)
                gp.sem_inc(sem("gather_turn"), 1)
            g.memset(wide[:, 0:1], 0.0).then_inc(sem("all_scattered"), 1)
            gp.wait_ge(sem("ld_fn"), 16)
            for t in range(T - 2):
                gp.wait_ge(sem("x2_scaled"), t + 1)
                g.tensor_tensor(fout[t], fout[t], fbc, ALU.mult).then_inc(sem("out_ready"), 1)

        @block.tensor
        def _(pe):
            made = [0]
            mm, tr = nc.tensor.matmul, nc.tensor.transpose

            def begin(*name):
                n = number[name]
                assert n == made[0], (name, order[made[0]])
                made[0] += 1
                if n >= 8:
                    pe.wait_ge(banks_read[order[n - 8][1]], reader_count[n - 8])
                return psum[:, n % 8]

            def done(ins):
                ins.then_inc(product_ready, 1)

            def four(ps, t, lhs, rhs):
                for h in range(H):
                    last = mm(ps[:, P * h:P * h + P], lhs[:, t, h], rhs[:, t, h], start=True, stop=True)
                return last

            def modulation(b):
                ps = begin("mod", b)
                pe.wait_ge(sem("acc_ready"), b + 1)
                if b < 4:
                    for i in range(4):
                        last = mm(ps[:, i:i + 1], acc_ring[b % 2][:, P * i:P * i + P], ones[:, 0:1], start=True, stop=True)
                else:
                    last = mm(ps[:, 0:256], ones, acc_ring[b % 2][:, 0:256], start=True, stop=True)
                done(last)

            pe.wait_ge(sem("consts"), 1)
            for b in range(2):
                modulation(b)
            for t in range(T):
                if t == T - 1:
                    modulation(2)
                pe.wait_ge(sem("xn_ready"), t + 1)
                for g in range(2):
                    ps = begin("hT", t, g)
                    for i in range(4):
                        last = tr(ps[:, P * i:P * i + P], h_ring[t % 2][:, P * (4 * g + i):P * (4 * g + i) + P], ident)
                    done(last)
            modulation(3)
            pe.wait_ge(sem("h_by_scalar"), 4)
            for c in range(13):
                ps = begin("zf", c)
                for i, s in ((0, "ld_w0"), (6, "ld_w1"), (10, "ld_w2")):
                    if c == i:
                        pe.wait_ge(sem(s), 16 if s != "ld_w2" else 80)
                for k in range(K):
                    if c == 0 and k == 4:
                        pe.wait_ge(sem("h_by_vector"), 2)
                        pe.wait_ge(sem("h_by_scalar"), 6)
                    if c < 6:
                        w = w_qkv[:, k, P * c:P * c + P]
                    elif c < 10:
                        w = w_b[:, k, P * (c - 6):P * (c - 6) + P]
                    else:
                        w = w_d[:, k, P * (c - 10):P * (c - 10) + P]
                    last = mm(ps, w, hT[:, k], start=k == 0, stop=k == K - 1)
                done(last)
                if c >= 1:
                    modulation(3 + c)

            def token_major(t, parts):
                for s in parts:
                    w, _, n, _ = zt_parts[s]
                    ps = begin("zt", t, s)
                    for k in range(K):
                        last = mm(ps[:, 0:n], hT[:, k, P * t:P * t + P], w[:, k, 0:n], start=k == 0, stop=k == K - 1)
                    done(last)

            pe.wait_ge(sem("ld_w3"), 16)
            for t in range(T):
                modulation(16 + t)
                token_major(t, (0,))
            pe.wait_ge(sem("silu_done"), 6)
            for nm, c0, nc_ in (("qk_tm", 0, 4), ("v_tm", 4, 2)):
                for t in range(T):
                    ps = begin(nm, t)
                    for i in range(nc_):
                        last = tr(ps[:, P * i:P * i + P], zpad[:, c0 + i, P * t:P * t + P], ident)
                    done(last)
            for s in ("ld_w4", "ld_w5", "ld_w6"):
                pe.wait_ge(sem(s), 16)
            token_major(0, (1, 2, 3))
            def key_blocks(n):
                kind, t, _ = units[n]
                return list(range(t + 1)) if kind == "diff" else list(range(0 if t else 1, 2))

            def transposed(n):
                ps = begin("pT", n)
                if units[n][0] == "diff":
                    pe.wait_ge(sem("p_ready"), n + 1)
                    p_ = pc[n % 2]
                else:
                    pe.wait_ge(sem("exp_ready"), 2 * n + 1)
                    p_ = p_sb[n % 2][0]
                for i, b in enumerate(key_blocks(n)):
                    last = tr(ps[:, P * i:P * i + P], p_[:, P * b:P * b + P], ident)
                done(last)

            def times_values(n):
                kind, t, h = units[n]
                blocks = key_blocks(n)
                ps = begin("pv", n)
                wait_read(pe, "pT", n)
                for i, b in enumerate(blocks):
                    v = bv[:, b, DH * h:DH * h + DH] if kind == "diff" else dv[:, t - 1 + b, DH * (h // 2):DH * (h // 2) + DH]
                    last = mm(ps[:, 0:DH], pT[n % 2][:, i], v, start=i == 0, stop=i == len(blocks) - 1)
                done(last)

            def score(n):
                kind, t, h = units[n]
                if kind == "diff":
                    for m in range(2):
                        ps = begin("score", n, m)
                        b = 64 * (h % 2) + 32 * m
                        done(mm(ps[:, 0:P * (t + 1)], zb[b:b + 32, h // 2, P * t:P * t + P],
                                zb[b:b + 32, 2 + h // 2, 0:P * (t + 1)], start=True, stop=True))
                else:
                    ps = begin("score", n, 0)
                    b, u0 = 64 * (h // 2), 0 if t else P
                    done(mm(ps[:, u0:256], zb[b:b + 64, 4 + h % 2, P * t:P * t + P],
                            zb[b:b + 64, 6, P * (t - 1) + u0:P * (t + 1)], start=True, stop=True))

            def scores_of(n):
                if n < len(units):
                    score(n)

            def rest_of(n, before):
                if 0 <= n < len(units):
                    transposed(n)
                if before >= 0:
                    times_values(before)

            ps = begin("gcum")
            pe.wait_ge(sem("masks_ready"), 1)
            pe.wait_ge(sem("g_ready"), 1)
            done(mm(ps[:, 0:16], tri, g_.rearrange("p t h -> p (t h)"), start=True, stop=True))
            token_major(1, (1, 2, 3))
            for t in range(T):
                ps = begin("grow", t)
                for h in range(H):
                    last = mm(ps[:, P * h:P * h + P], g_[:, t, h:h + 1].to_broadcast([P, P]), tri, start=True, stop=True)
                done(last)
            for t in (2, 3):
                token_major(t, (1, 2, 3))
            for nm, at_, s in (("kT", 4, "kn"), ("qT", 0, "qn")):
                for t in range(T):
                    ps = begin(nm, t)
                    pe.wait_ge(sem("qk_normed"), t + 1)
                    for h in range(H):
                        last = tr(ps[0:64, P * h:P * h + P], qkv_tm[:, t, 64 * (at_ + h):64 * (at_ + h) + 64], ident)
                    done(last)
            for nm, r_, cnt in (("kk", kT, "kT"), ("kq", qT, "qT")):
                for t in range(T):
                    ps = begin(nm, t)
                    wait_read(pe, cnt, t)
                    for h in range(H):
                        last = mm(ps[:, P * h:P * h + P], kT[0:64, t, h], r_[0:64, t, h], start=True, stop=True)
                    done(last)
            ps = begin("sguT")
            pe.wait_ge(sem("ld_sgw"), 16)
            for g in range(H):
                last = tr(ps[:, P * g:P * g + P], sgw[:, g], ident)
            done(last)
            for t in range(T):
                ps = begin("M", t)
                wait_read(pe, "kk", t)
                for h in range(H):
                    last = tr(ps[:, P * h:P * h + P], Lf[:, t, h], ident)
                done(last)
            for nm, l_, r_ in (("L2", B1, B2), ("M2", B2, B1), ("L4", B4, B3)):
                for t in range(T):
                    ps = begin(nm, t)
                    if nm == "L2":
                        pe.wait_ge(sem("eights"), t + 1)
                    if nm == "L4":
                        wait_read(pe, "M2", t)
                    done(four(ps, t, l_, r_))
            for nm, l_ in (("Ra", B3), ("Rb", B1)):
                for t in range(T):
                    ps = begin(nm, t)
                    if nm == "Ra":
                        pe.wait_ge(sem("R_first"), t + 1)
                    else:
                        wait_read(pe, "L4", t)
                        wait_read(pe, "Ra", t)
                    done(four(ps, t, l_, R))
            for lv in range(3):
                for t in range(T):
                    ps = begin("Tm", lv, t)
                    wait_read(pe, *(("R", lv - 1, t) if lv else ("Rb", t)))
                    for h in range(H):
                        last = tr(ps[:, P * h:P * h + P], R[:, t, h], ident)
                    done(last)
                for t in range(T):
                    ps = begin("Z", lv, t)
                    pe.wait_ge(sem("level_masked"), T * lv + t + 1)
                    done(four(ps, t, B2, R))
                for t in range(T):
                    ps = begin("R", lv, t)
                    wait_read(pe, "Z", lv, t)
                    done(four(ps, t, B3, B4))
            scores_of(0)
            for t in range(T):
                ps = begin("U", t)
                wait_read(pe, "R", 2, t)
                pe.wait_ge(sem("vb_ready"), t + 1)
                for h in range(H):
                    last = mm(ps[:, DH * h:DH * h + DH], R[:, t, h], vb[:, t, h], start=True, stop=True)
                done(last)
            for t in range(T):
                ps = begin("WT", t)
                for h in range(H):
                    last = mm(ps[0:64, P * h:P * h + P], kbe[:, t, h], R[:, t, h], start=True, stop=True)
                done(last)
            for t in range(T):
                ps = begin("QdT", t)
                pe.wait_ge(sem("Qd_ready"), t + 1)
                for h in range(H):
                    last = tr(ps[0:64, P * h:P * h + P], Qd[:, t, h], ident)
                done(last)
            for ch in range(2 * T):
                t, b = ch // 2, 64 * (ch % 2)
                ps = begin("WQ", ch)
                wait_read(pe, "QdT", t)
                if ch:
                    wait_read(pe, "SU", ch - 1)
                else:
                    pe.wait_ge(sem("S_ready"), 1)
                for l_, c0 in ((WT, 0), (QdT, 256)):
                    for h in range(H):
                        last = mm(ps[b:b + 64, c0 + DH * h:c0 + DH * h + DH], l_[0:64, t, h, b:b + 64], S[0:64, h],
                                  start=True, stop=True)
                done(last)
                scores_of(ch + 1)
                ps = begin("SU", ch)
                pe.wait_ge(sem("v_new_ready"), ch + 1)
                for h in range(H):
                    last = mm(ps[0:64, DH * h:DH * h + DH], ktail[b:b + 64, t, h], v_new[b:b + 64, t, h],
                              start=True, stop=True)
                done(last)
                rest_of(ch - 1, ch - 2)
                if ch % 2:
                    ps = begin("AV", t)
                    for h in range(H):
                        last = mm(ps[:, DH * h:DH * h + DH], AT[:, t, h], v_new[:, t, h], start=True, stop=True)
                    done(last)
                    if t == 0:
                        pe.wait_ge(sem("sgT_ready"), 1)
                        pe.wait_ge(sem("vn_ready"), T)
                    ps = begin("mix", t)
                    done(mm(ps[:, 0:256], sgT[:, t], uv[:, :, 256 + DH * t:256 + DH * t + DH], start=True, stop=True))
            for n in range(2 * T, len(units) + 2):
                scores_of(n + 1)
                rest_of(n - 1, n - 2)
            wait_read(pe, "pv", len(units) - 1)
            pe.wait_ge(sem("gdn_done"), T)
            pe.wait_ge(sem("diff_done"), T)
            for t in range(T):
                for g in range(2):
                    ps = begin("oT", t, g)
                    for i in range(4):
                        last = tr(ps[:, P * i:P * i + P], o_tm[:, t, P * (4 * g + i):P * (4 * g + i) + P], ident)
                    done(last)
            pe.wait_ge(sem("ld_wo"), 32)
            wait_read(pe, "oT", T - 1, 0)
            wait_read(pe, "oT", T - 1, 1)
            pe.wait_ge(sem("ld_small"), 16 * 13)

            def router(t):
                wait_read(pe, "h2T", t, 0)
                wait_read(pe, "h2T", t, 1)
                ps = begin("logit", t)
                for k in range(K):
                    last = mm(ps[:, 0:E], h2T[:, k, P * t:P * t + P], rw[:, k], start=k == 0, stop=k == K - 1)
                done(last)

            for t in range(T + 2):
                if t < T:
                    for n in range(2):
                        ps = begin("y", t, n)
                        for k in range(K):
                            last = mm(ps, oT[:, k, P * t:P * t + P], w_o[n][:, k], start=k == 0, stop=k == K - 1)
                        done(last)
                if t == T:
                    router(t - 2)
                if 1 <= t <= T:
                    u = t - 1
                    pe.wait_ge(sem("h2_ready"), u + 1)
                    for g in range(2):
                        ps = begin("h2T", u, g)
                        for i in range(4):
                            last = tr(ps[:, P * i:P * i + P], h2_ring[u % 2][:, P * (4 * g + i):P * (4 * g + i) + P], ident)
                        done(last)
                if t >= 2 and t != T:
                    router(t - 2)
            ps = begin("rank")
            pe.wait_ge(sem("chosen"), 1)
            pe.wait_ge(sem("before_ready"), 1)
            chosen = mask.rearrange("p t e -> p (t e)")
            mm(ps[:, 0:E * T], before, chosen, start=True, stop=False)
            for n in range(1, T):
                last = mm(ps[:, E * n:E * T], ones16, mask[:, 0:T - n].rearrange("p t e -> p (t e)"), start=False, stop=n == T - 1)
            done(last)
            ps = begin("table")
            for t in range(T):
                mm(ps[:, 80:80 + E], ones16, mask[:, t], start=t == 0, stop=t == T - 1)
            for i in range(2 * T):
                pe.wait_ge(sem("table_parts"), 2 * i + 2)
                last = mm(ps[:, 0:80], in_slot[:, i // T, i % T], in_table[:, i // T, i % T], start=i == 0, stop=i == 2 * T - 1)
            done(last)
            for who in ("act", "dve"):
                pe.wait_ge(banks_read[who], seen[who])
            for s in ("gate_made", "up_made", "y_made"):
                pe.sem_inc(sem(s), 2)

            def transpose_rows(r, p, j):
                b = j % 2
                pe.wait_ge(sem(f"ld_xg{b}"), nth_of_half(pe, 16, r, p, j, 16))
                pe.wait_ge(sem("xT_copied"), nth(pe, 1, r, p, j, 1))
                for k in range(K):
                    last = tr(psum[:, k // 4, P * (k % 4):P * (k % 4) + P], xg[b][:, P * k:P * k + P], ident)
                last.then_inc(sem("xT_made"), 1)

            def gate(r, p, j):
                b = j % 2
                pe.wait_ge(sem("xT_copied"), nth(pe, 1, r, p, j, 2))
                pe.wait_ge(sem(f"ld_w_gate{b}"), nth_of_half(pe, 16, r, p, j, 16))
                pe.wait_ge(sem("silu_made"), nth(pe, 1, r, p, j, 1))
                for k in range(K):
                    last = mm(psum[:, 2], xgT[b][:, k], w_exp[b][0][:, k], start=k == 0, stop=k == K - 1)
                last.then_inc(sem("gate_made"), 1)

            def up(r, p, j):
                b = j % 2
                pe.wait_ge(sem(f"ld_w_up{b}"), nth_of_half(pe, 16, r, p, j, 16))
                pe.wait_ge(sem("he_made"), nth(pe, 1, r, p, j, 1))
                for k in range(K):
                    last = mm(psum[:, 3], xgT[b][:, k], w_exp[b][1][:, k], start=k == 0, stop=k == K - 1)
                last.then_inc(sem("up_made"), 1)

            def transpose_hidden(r, p, j):
                b = j % 2
                pe.wait_ge(sem("he_made"), nth(pe, 1, r, p, j, 2))
                pe.wait_ge(sem("heT_copied"), nth(pe, 1, r, p, j, 1))
                for k in range(4):
                    last = tr(psum[:, 4, P * k:P * k + P], he[b][:, P * k:P * k + P], ident)
                last.then_inc(sem("heT_made"), 1)

            def down(r, p, j):
                b = j % 2
                pe.wait_ge(sem(f"ld_w_down{b}"), nth_of_half(pe, 16, r, p, j, 16))
                pe.wait_ge(sem("heT_copied"), nth(pe, 1, r, p, j, 2))
                pe.wait_ge(sem("y_read"), nth(pe, 1, r, p, j, 1))
                for n in range(2):
                    for k in range(4):
                        last = mm(psum[:, 5 + n], heT[b][:, k], w_exp[b][2][:, k, 512 * n:512 * n + 512], start=k == 0, stop=k == 3)
                last.then_inc(sem("y_made"), 1)

            def first(r):
                transpose_rows(r, 0, 0)
                gate(r, 0, 0)
                up(r, 0, 0)
                transpose_rows(r, 0, 1)

            def step(r, p, j):
                gate(r, p, j)
                transpose_hidden(r, p, j - 1)
                up(r, p, j)
                transpose_rows(r, p, j + 1)
                down(r, p, j - 1)

            def last(r):
                gate(r, 0, E - 1)
                transpose_hidden(r, 0, E - 2)
                up(r, 0, E - 1)
                down(r, 0, E - 2)
                transpose_hidden(r, 0, E - 1)
                down(r, 0, E - 1)

            in_steps(pe, 0, first, step, last)
            pe.wait_ge(sem("rounds_ready"), 1)
            n_rounds = pe.value_load(rounds[0:1, 0:1], min_val=1, max_val=4)
            with pe.If(n_rounds > 1):
                with pe.Fori(1, n_rounds) as r:
                    in_steps(pe, r, first, step, last)

        @block.scalar
        def _(act):
            link = chain(act, sem("scalar_step"))
            A = nc.scalar.activation

            def copied(dst, name, view, func=ACT.Copy, **kw):
                wait_product(act, *name)
                link(A(dst, view, func, **kw), banks_read["act"])

            def rsqrt(dst, src, scale, signal):
                link(A(dst, src, ACT.Ln, bias=eps[:, 0:1], scale=scale))
                link(A(dst, dst, ACT.Exp, scale=-0.5), signal)

            def head_squares(which, t, o):
                for h in range(H):
                    link(A(junk_head, o[:, DH * h:DH * h + DH], ACT.Square, accum_out=head_ss[which][:, t, h:h + 1]))

            act.wait_ge(sem("consts"), 1)
            act.wait_ge(sem("ld_c"), 16)
            link(A(acol, ccol, ACT.Silu), sem("c_ready"))
            act.wait_ge(sem("ld_x"), 16)
            for t in range(T):
                link(A(squares, x[:, t], ACT.Square, accum_out=ss[:, t:t + 1]))
            rsqrt(rs, ss, 1.0 / D, sem("rs1_ready"))
            for t in range(T + 1):
                if t < T:
                    A(h_ring[t % 2], x[:, t], ACT.Copy, scale=rs[:, t:t + 1]).then_inc(sem("xn_ready"), 1)
                if t >= 1:
                    for g in range(2):
                        copied(hT[:, 4 * g:4 * g + 4, P * (t - 1):P * t], ("hT", t - 1, g), bank("hT", t - 1, g).rearrange("p (k n) -> p k n", k=4))
            for k in (0, 1, 2, 3, 6, 7):
                if k in (0, 6):
                    act.wait_ge(sem("modT_ready"), 1 if k == 0 else 2)
                link(A(hT[:, k], hT[:, k], ACT.Identity, scale=modT[:, 1, k:k + 1], bias=modT[:, 0, k:k + 1]), sem("h_by_scalar"))

            def copied_modulation(b):
                m = b - 4
                copied(mod2[:, m // 4, 256 * (m % 4):256 * (m % 4) + 256], ("mod", b), bank("mod", b)[:, 0:256])

            act.wait_ge(sem("ld_bcol"), 16 * 7)
            act.wait_ge(sem("pads"), 1)
            for c in range(13):
                dst = zpad[:, c, 3:3 + SEQ] if c < 6 else zb[:, c - 6]
                copied(dst, ("zf", c), bank("zf", c), func=ACT.Identity, bias=bcol[:, c:c + 1])
                if 2 <= c < 8:
                    act.wait_ge(sem("conv_ready"), c - 1)
                    link(A(zpad[:, c - 2, 0:SEQ], cring[(c - 2) % 2], ACT.Silu), sem("silu_done"))
                if c >= 1:
                    copied_modulation(3 + c)
            for b in range(16, 20):
                copied_modulation(b)
            for t in range(T):
                copied(qkv_tm[:, t, 0:512], ("qk_tm", t), bank("qk_tm", t))
            for t in range(T):
                copied(qkv_tm[:, t, 512:768], ("v_tm", t), bank("v_tm", t)[:, 0:256])
            for t in range(T):
                wait_read(act, "zt", t, 0)
                A(gab[:, t, 0:256], gab[:, t, 0:256], ACT.Silu)
            act.wait_ge(sem("alpha_abs"), 1)
            link(A(tA, tA, ACT.Exp, scale=-1.0))
            link(A(tA, tA, ACT.Ln, bias=1.0))
            link(A(alog, alog, ACT.Exp))
            link(A(tB, gab[:, :, 260:264], ACT.Exp, scale=-1.0), sem("softplus"))
            act.wait_ge(sem("lam_sums"), 1)
            link(A(lam[:, 0:2], lam[:, 0:2], ACT.Exp), sem("lam_exp"))
            act.wait_ge(sem("qk_squares"), T)
            rsqrt(nrs, nss, 1.0, sem("qk_rs"))
            wait_read(act, "gcum")
            link(A(egc, gc, ACT.Exp), sem("egc_ready"))

            def gated_mlp(t):
                wait_read(act, "zt", t, 3)
                link(A(uv[:, t], uv[:, t], ACT.Gelu_apprx_tanh), sem("gelu"))
                head_squares("sgu", t, uv[:, t, 256:512])

            gated_mlp(0)
            gated_mlp(1)
            for t in range(T):
                act.wait_ge(sem("gdiff"), t + 1)
                link(A(B1[:, t], B1[:, t], ACT.Exp, scale=-1.0), sem("decay"))
                link(A(AT[:, t], AT[:, t], ACT.Exp), sem("decay"))
            link(A(etail, etail, ACT.Exp))
            link(A(egl, glast, ACT.Exp), sem("tails"))
            gated_mlp(2)
            gated_mlp(3)
            for nm, dst in (("kT", kT), ("qT", qT)):
                for t in range(T):
                    copied(dst[0:64, t], (nm, t), bank(nm, t)[0:64].rearrange("p (h n) -> p h n", h=H))
            def heads(*name):
                return bank(*name).rearrange("p (h n) -> p h n", h=H)

            for t in range(T):
                copied(B4[:, t], ("M", t), heads("M", t))
            s16 = head_ss["sgu"].rearrange("p t h -> p (t h)")
            rsqrt(s16, s16, 1.0 / DH, sem("rs_sgu"))
            for nm, dst in (("L2", B3), ("M2", B4), ("L4", B1)):
                for t in range(T):
                    if nm == "L4":
                        act.wait_ge(sem("R_first"), t + 1)
                    copied(dst[:, t], (nm, t), heads(nm, t))
            for lv in range(3):
                for nm, dst in (("Tm", B3), ("Z", B4)):
                    for t in range(T):
                        copied(dst[:, t], (nm, lv, t), heads(nm, lv, t))
            for t in range(T):
                copied(U[:, t], ("U", t), bank("U", t)[:, 0:256].rearrange("p (h n) -> p h n", h=H))
            act.wait_ge(sem("level_masked"), 3 * T)
            for nm, dst in (("WT", WT), ("QdT", QdT)):
                for t in range(T):
                    copied(dst[0:64, t], (nm, t), bank(nm, t)[0:64].rearrange("p (h n) -> p h n", h=H))
            for n in range(len(units) + 1):
                if n < len(units):
                    kind, t, h = units[n]
                    m8 = mx[:, n % 4]
                    cols = slice(0, P * (t + 1)) if kind == "diff" else slice(0 if t else P, 256)
                    act.wait_ge(sem("max_ready"), n + 1)
                    for m in range(2 if kind == "diff" else 1):
                        link(A(p_sb[n % 2][m][:, cols], s_sb[n % 2][m][:, cols], ACT.Exp, bias=m8[:, 2 + m:3 + m],
                               accum_out=m8[:, 4 + m:5 + m]), sem("exp_ready"))
                    if kind == "swa":
                        link(A(m8[:, 5:6], sink[:, h:h + 1], ACT.Exp, bias=m8[:, 2:3]), sem("exp_ready"))
                if n >= 1:
                    nb = n_blocks[n - 1]
                    copied(pT[(n - 1) % 2][:, 0:nb], ("pT", n - 1), bank("pT", n - 1)[:, 0:P * nb].rearrange("p (k n) -> p k n", n=P))
                if n % 2 == 0 and 2 <= n <= 2 * T:
                    t = n // 2 - 1
                    wait_read(act, "AV", t)
                    head_squares("gdn", t, o_tm[:, t, 0:256])
                if n % 4 == 3 and 7 <= n < 7 + 4 * T:
                    i = (n - 7) // 4
                    wait_read(act, "pv", 4 * i + 3)
                    t = units[4 * i][1]
                    head_squares("diff", t, o_tm[:, t, 256:512])
                    if i == T - 1:
                        for which in ("gdn", "diff"):
                            s16 = head_ss[which].rearrange("p t h -> p (t h)")
                            link(A(s16, s16, ACT.Ln, bias=eps[:, 0:1], scale=1.0 / DH))
                        for which in ("gdn", "diff"):
                            s16 = head_ss[which].rearrange("p t h -> p (t h)")
                            link(A(s16, s16, ACT.Exp, scale=-0.5), sem(f"rs_{which}"))
            for t in range(T):
                copied(oT[:, 4:8, P * t:P * t + P], ("oT", t, 1), bank("oT", t, 1).rearrange("p (k n) -> p k n", k=4))
            for t in range(T + 1):
                if t < T:
                    act.wait_ge(sem("x1_ready"), 2 * t + 2)
                    link(A(junk1k, x[:, t], ACT.Square, accum_out=ss[:, t:t + 1]))
                    link(A(rs[:, t:t + 1], ss[:, t:t + 1], ACT.Sqrt, bias=eps[:, 0:1], scale=1.0 / D), sem("rms2_ready"))
                if t >= 1:
                    copied(h2T[:, 4:8, P * (t - 1):P * t], ("h2T", t - 1, 1), bank("h2T", t - 1, 1).rearrange("p (k n) -> p k n", k=4))
            wait_read(act, "logit", T - 1)
            link(A(scores, scores, ACT.Exp, scale=-1.0), sem("exp_logits"))
            for s in ("xT_copied", "silu_made", "heT_copied"):
                act.sem_inc(sem(s), 1)

            def copy_rows(r, p, j):
                act.wait_ge(sem("xT_made"), nth(act, 1, r, p, j, 1))
                A(xgT[j % 2], psum[:, 0:2].rearrange("p b (k n) -> p (b k) n", n=P), ACT.Copy).then_inc(sem("xT_copied"), 1)

            def silu(r, p, j):
                act.wait_ge(sem("gate_made"), nth(act, 1, r, p, j, 3))
                A(gated[j % 2], psum[:, 2], ACT.Silu).then_inc(sem("silu_made"), 1)

            def copy_hidden(r, p, j):
                act.wait_ge(sem("heT_made"), nth(act, 1, r, p, j, 1))
                A(heT[j % 2], psum[:, 4].rearrange("p (k n) -> p k n", n=P), ACT.Copy).then_inc(sem("heT_copied"), 1)

            def first(r):
                copy_rows(r, 0, 0)
                silu(r, 0, 0)
                copy_rows(r, 0, 1)

            def step(r, p, j):
                silu(r, p, j)
                copy_hidden(r, p, j - 1)
                copy_rows(r, p, j + 1)

            def last(r):
                silu(r, 0, E - 1)
                for j in (E - 2, E - 1):
                    copy_hidden(r, 0, j)

            in_steps(act, 0, first, step, last)
            act.wait_ge(sem("rounds_ready"), 1)
            n_rounds = act.value_load(rounds[0:1, 0:1], min_val=1, max_val=4)
            with act.If(n_rounds > 1):
                with act.Fori(1, n_rounds) as r:
                    in_steps(act, r, first, step, last)
            link(A(junk, eps, ACT.Sqrt))
            for t in range(T):
                act.wait_ge(sem("x2_ready"), t + 1)
                link(A(junk_last, x[:, t], ACT.Square, accum_out=ss[:, t:t + 1]))
                link(A(rs[:, t:t + 1], ss[:, t:t + 1], ACT.Sqrt, bias=eps[:, 0:1], scale=1.0 / D), sem("rms3_ready"))
                if t < T - 2:
                    act.wait_ge(sem("rs3_inverted"), t + 1)
                    A(fout[t], x[:, t], ACT.Copy, scale=rs[:, t:t + 1]).then_inc(sem("x2_scaled"), 1)

        @block.vector
        def _(dve):
            link = chain(dve, sem("vector_step"))
            v = nc.vector
            TT, TS, STT = v.tensor_tensor, v.tensor_scalar, v.scalar_tensor_tensor

            def read(ins):
                link(ins, banks_read["dve"])

            def conv(c):
                wait_read(dve, "zf", c)
                if c == 0:
                    dve.wait_ge(sem("ld_conv"), 64)
                if c >= 2:
                    dve.wait_ge(sem("silu_done"), c - 1)
                y = cring[c % 2]
                link(TS(y, zpad[:, c, 0:SEQ], convc[:, c, 0:1], None, ALU.mult))
                for i in range(1, 4):
                    ins = STT(y, zpad[:, c, i:i + SEQ], convc[:, c, i:i + 1], y, ALU.mult, ALU.add)
                    link(ins, sem("conv_ready") if i == 3 else sem("vector_step"))

            def ada(b):
                if b < 4:
                    w, n = ada_first[b], 512
                    dve.wait_ge(sem(f"ld_ada{b}"), 16)
                else:
                    w, n = ada_rest[b % 2], 256
                    dve.wait_ge(sem(f"ld_adar{b % 2}"), 32 * (b // 2 - 1))
                if b >= 2:
                    wait_product(dve, "mod", b - 2)
                acc = acc_ring[b % 2][:, 0:n]
                link(TS(acc, w[:, 0], acol[:, 0:1], None, ALU.mult))
                for j in range(1, 8):
                    ins = STT(acc, w[:, j], acol[:, j:j + 1], acc, ALU.mult, ALU.add)
                    link(ins, sem("acc_ready") if b < 4 and j == 7 else sem("vector_step"))
                if b >= 4:
                    link(TT(acc[0:1], acc[0:1], brow[b % 2][0:1], ALU.add), sem("acc_ready"))

            dve.wait_ge(sem("c_ready"), 1)

            def first_modulation(half):
                ks = slice(4 * half, 4 * half + 4)
                for part in range(2):
                    wait_product(dve, "mod", 2 * half + part)
                    read(TT(modT[:, part, ks], bank("mod", 2 * half + part)[:, 0:4], bmod[:, part, ks], ALU.add))
                link(STT(modT[:, 1, ks], modT[:, 1, ks], 1.0, n1col[:, ks], ALU.add, ALU.mult), sem("modT_ready"))

            for b in range(3):
                ada(b)
            dve.wait_ge(sem("ld_n1"), 32)
            first_modulation(0)
            ada(3)
            first_modulation(1)
            wait_read(dve, "hT", T - 1, 1)
            for k in (4, 5):
                link(TS(hT[:, k], hT[:, k], modT[:, 1, k:k + 1], modT[:, 0, k:k + 1], ALU.mult, ALU.add), sem("h_by_vector"))
            for c in range(6):
                conv(c)
                ada(4 + c)
            for b in range(10, 20):
                ada(b)
            dve.wait_ge(sem("ld_btm"), 64)
            parts = ((gab, 0, 264, 0), (None, 0, 512, 264), (uv, 256, 256, 776), (dv, 0, P, 1032))

            def token_major(t, which):
                for s in which:
                    dst, c0, n, o = parts[s]
                    wait_product(dve, "zt", t, s)
                    ps = bank("zt", t, s)
                    if s == 1:
                        link(TT(bv[:, t], ps[:, 0:256], btm[:, 264:520], ALU.add))
                        read(TT(uv[:, t, 0:256], ps[:, 256:512], btm[:, 520:776], ALU.add))
                    else:
                        read(TT(dst[:, t, c0:c0 + n], ps[:, 0:n], btm[:, o:o + n], ALU.add))

            for t in range(T):
                token_major(t, (0,))
            dve.wait_ge(sem("ld_small"), 16 * 10)
            link(TT(tC, gab[:, :, 256:260], dtb.unsqueeze(1).to_broadcast([P, T, H]), ALU.add))
            link(STT(tA, tC, -1.0, tC, ALU.mult, ALU.max), sem("alpha_abs"))
            dve.wait_ge(sem("softplus"), 1)
            link(STT(tC, tC, 0.0, tA, ALU.max, ALU.add))
            link(TS(alog, alog, -1.0, None, ALU.mult))
            link(TT(g_, tC, alog.unsqueeze(1).to_broadcast([P, T, H]), ALU.mult), sem("g_ready"))
            link(TS(tB, tB, 1.0, None, ALU.add))
            link(v.reciprocal(beta, tB))
            link(TT(lamt[:, 0], lam4[:, 0], lam4[:, 1], ALU.mult))
            link(TT(lamt[:, 1], lam4[:, 2], lam4[:, 3], ALU.mult))
            link(v.tensor_reduce(lam[:, 0:2], lamt, AX.X, ALU.add), sem("lam_sums"))
            dve.wait_ge(sem("lam_exp"), 1)
            link(TT(lam[:, 2:3], lam[:, 1:2], lam[:, 0:1], ALU.subtract))
            link(TS(neglam, lam[:, 2:3], -LAM_INIT, None, ALU.add))
            for t in range(T):
                wait_read(dve, "qk_tm", t)
                link(TT(sq, qkv_tm[:, t, 0:512], qkv_tm[:, t, 0:512], ALU.mult))
                ins = v.tensor_reduce(nss[:, t], sq.rearrange("p (n d) -> p n d", d=DH), AX.X, ALU.add)
                link(ins, sem("qk_squares"))
            dve.wait_ge(sem("qk_rs"), 1)
            link(TS(nrs[:, :, 0:4], nrs[:, :, 0:4], DH ** -0.5, None, ALU.mult))
            for t in range(T):
                qk = qkv_tm[:, t, 0:512].rearrange("p (n d) -> p n d", d=DH)
                link(TT(qk, qk, nrs[:, t].unsqueeze(2).to_broadcast([P, 8, DH]), ALU.mult), sem("qk_normed"))
            token_major(0, (1, 2, 3))
            wait_product(dve, "gcum")
            read(v.tensor_copy(gc.rearrange("p t h -> p (t h)"), bank("gcum")[:, 0:16]))
            token_major(1, (1, 2, 3))
            for t in range(T):
                wait_product(dve, "grow", t)
                ps = bank("grow", t).rearrange("p (h n) -> p h n", h=H)
                link(v.tensor_copy(glast[:, t], ps[:, :, 63::64]))
                read(TT(B1[:, t], ps, over_heads(gc[:, t], P), ALU.subtract))
                link(TS(AT[:, t], B1[:, t], 0.0, None, ALU.min))
                if t == T - 1:
                    for b in range(2):
                        r_ = slice(64 * b, 64 * b + 64)
                        link(TT(etail[r_], glast[r_, :, :, b], gc[r_], ALU.subtract))
                link(TS(B1[:, t], B1[:, t], 0.0, None, ALU.max), sem("gdiff"))
            for t in (2, 3):
                token_major(t, (1, 2, 3))

            def heads(*name):
                return bank(*name).rearrange("p (h n) -> p h n", h=H)

            for t in range(T):
                dve.wait_ge(sem("decay_masked"), 2 * t + 2)
                wait_product(dve, "kk", t)
                read(TT(Lf[:, t], heads("kk", t), B1[:, t], ALU.mult))
                link(TT(B2[:, t], Lf[:, t], per_head(mlv[0]), ALU.mult))
            for t in range(T):
                wait_product(dve, "kq", t)
                read(TT(AT[:, t], heads("kq", t), AT[:, t], ALU.mult))
            wait_product(dve, "sguT")
            read(v.tensor_copy(sgT.rearrange("p h n -> p (h n)"), bank("sguT")))
            link(v.memset(sgT[64:128, :, 0:64], 0.0), sem("sgT_ready"))
            for t in range(T):
                wait_read(dve, "M", t)
                link(TT(B1[:, t], B4[:, t], per_head(m8T), ALU.mult), sem("eights"))
            k_tm = qkv_tm[:, :, 256:512].rearrange("p t (h d) -> p t h d", d=DH)
            q_tm = qkv_tm[:, :, 0:256].rearrange("p t (h d) -> p t h d", d=DH)
            v_tm = qkv_tm[:, :, 512:768].rearrange("p t (h d) -> p t h d", d=DH)
            dve.wait_ge(sem("egc_ready"), 1)
            for t in range(T):
                link(TT(Qd[:, t], q_tm[:, t], over_heads(egc[:, t], DH), ALU.mult), sem("Qd_ready"))
            link(v.memset(S[0:64], 0.0), sem("S_ready"))
            for nm in ("Ra", "Rb"):
                for t in range(T):
                    wait_product(dve, nm, t)
                    read(TT(R[:, t], heads(nm, t), R[:, t], ALU.add))
            wait_read(dve, "v_tm", T - 1)
            for t in range(T):
                link(TT(vb[:, t], v_tm[:, t], over_heads(beta[:, t], DH), ALU.mult))
                link(TT(kbe[:, t], k_tm[:, t], over_heads(beta[:, t], DH), ALU.mult))
                link(TT(kbe[:, t], kbe[:, t], over_heads(egc[:, t], DH), ALU.mult), sem("vb_ready"))
            for lv in range(3):
                for t in range(T):
                    wait_product(dve, "R", lv, t)
                    read(TT(R[:, t], R[:, t], heads("R", lv, t), ALU.subtract))
            dve.wait_ge(sem("tails"), 1)
            for t in range(T):
                link(TT(ktail[:, t], k_tm[:, t], over_heads(etail[:, t], DH), ALU.mult))
            def spread(n):
                kind, t, h = units[n]
                return kind, t, h, slice(0, P * (t + 1)) if kind == "diff" else slice(0 if t else P, 256), mx[:, n % 4]

            def maxima(n):
                kind, t, h, cols, m8 = spread(n)
                for m in range(2 if kind == "diff" else 1):
                    wait_product(dve, "score", n, m)
                    bias = bias_diff[:, h, P * (3 - t):] if kind == "diff" else bias_swa[:, h, cols]
                    read(v.tensor_tensor_reduce(out=s_sb[n % 2][m][:, cols], in0=bank("score", n, m)[:, cols], in1=bias,
                                                scale=32 ** -0.5 if kind == "diff" else DH ** -0.5, scalar=-3e38,
                                                op0=ALU.add, op1=ALU.max, accum_out=m8[:, m:m + 1]))
                if kind == "swa":
                    link(TT(m8[:, 0:1], m8[:, 0:1], sink[:, h:h + 1], ALU.max))
                link(TS(m8[:, 2:4], m8[:, 0:2], -1.0, None, ALU.mult), sem("max_ready"))

            def weights(n):
                kind, t, h, cols, m8 = spread(n)
                dve.wait_ge(sem("exp_ready"), 2 * n + 2)
                if kind == "diff":
                    if n >= 2:
                        wait_product(dve, "pT", n - 2)
                    link(v.reciprocal(m8[:, 6:8], m8[:, 4:6]))
                    link(TS(m8[:, 7:8], m8[:, 7:8], neglam, m8[:, 4:5], ALU.mult, ALU.mult))
                    p0, p1 = (p_sb[n % 2][m][:, cols] for m in range(2))
                    link(STT(pc[n % 2][:, cols], p1, m8[:, 7:8], p0, ALU.mult, ALU.add), sem("p_ready"))
                else:
                    link(TT(m8[:, 4:5], m8[:, 4:5], m8[:, 5:6], ALU.add))
                    link(v.reciprocal(m8[:, 6:7], m8[:, 4:5]))

            def outputs(n):
                kind, t, h, cols, m8 = spread(n)
                c0 = (256 if kind == "diff" else 768) + DH * h
                wait_product(dve, "pv", n)
                read(TS(o_tm[:, t, c0:c0 + DH], bank("pv", n)[:, 0:DH], m8[:, 6:7], None, ALU.mult))

            dve.wait_ge(sem("biases"), 1)
            maxima(0)
            wait_read(dve, "U", T - 1)
            dve.wait_ge(sem("gelu"), T)
            for ch in range(2 * T):
                t, b = ch // 2, 64 * (ch % 2)
                r_ = slice(b, b + 64)
                wait_product(dve, "WQ", ch)
                ps = bank("WQ", ch)[r_]
                link(TT(v_new[r_, t], U[r_, t], ps[:, 0:256].rearrange("p (h d) -> p h d", h=H), ALU.subtract), sem("v_new_ready"))
                read(v.tensor_copy(qs[r_, t], ps[:, 256:512].rearrange("p (h d) -> p h d", h=H)))
                link(TT(Stmp[0:64], S[0:64], egl[0:64, t, :, ch % 2].unsqueeze(2).to_broadcast([64, H, DH]), ALU.mult))
                maxima(ch + 1)
                wait_product(dve, "SU", ch)
                read(TT(S[0:64], Stmp[0:64], bank("SU", ch)[0:64, 0:256].rearrange("p (h d) -> p h d", h=H), ALU.add))
                weights(ch)
                if ch >= 2:
                    outputs(ch - 2)
                if ch % 2:
                    wait_product(dve, "AV", t)
                    read(TT(o_tm[:, t, 0:256], qs[:, t].rearrange("p h d -> p (h d)"), bank("AV", t)[:, 0:256], ALU.add))
                    wait_product(dve, "mix", t)
                    ins = STT(o_tm[:, :, 512 + DH * t:512 + DH * t + DH], bank("mix", t)[:, 0:256].rearrange("p (t d) -> p t d", t=T),
                              sgb[:, t:t + 1], uv[:, :, DH * t:DH * t + DH], ALU.add, ALU.mult)
                    read(ins)

            for i in range(2 * T + 1, len(units) + 3):
                if i < len(units):
                    maxima(i)
                if 1 <= i <= len(units):
                    weights(i - 1)
                if i >= 3:
                    outputs(i - 3)
            for t in range(T):
                wait_product(dve, "oT", t, 0)
                read(v.tensor_copy(oT[:, 0:4, P * t:P * t + P], bank("oT", t, 0).rearrange("p (k n) -> p k n", k=4)))

            def read_logits(t):
                wait_product(dve, "logit", t)
                read(v.tensor_copy(scores[:, t], bank("logit", t)[:, 0:E]))

            dve.wait_ge(sem("x_biased"), T)
            dve.wait_ge(sem("ld_n2"), 16)
            link(STT(mod2[:, 2], mod2[:, 2], 1.0, n2bc, ALU.add, ALU.mult))
            for t in range(T + 2):
                if t < T:
                    for n in range(2):
                        cols = slice(512 * n, 512 * n + 512)
                        wait_product(dve, "y", t, n)
                        read(TT(ytmp[n], bank("y", t, n), mod2[:, 0, cols], ALU.mult))
                        link(TT(x[:, t, cols], x[:, t, cols], ytmp[n], ALU.add), sem("x1_ready"))
                if t == T:
                    read_logits(t - 2)
                if 1 <= t <= T:
                    wait_product(dve, "h2T", t - 1, 0)
                    read(v.tensor_copy(h2T[:, 0:4, P * (t - 1):P * t], bank("h2T", t - 1, 0).rearrange("p (k n) -> p k n", k=4)))
                if t < T:
                    dve.wait_ge(sem("rms2_ready"), t + 1)
                    link(v.reciprocal(rs[:, t:t + 1], rs[:, t:t + 1]))
                    if t >= 2:
                        wait_product(dve, "h2T", t - 2, 1)
                        dve.wait_ge(sem(f"st_h2{t % 2}"), 16)
                    hr = h2_ring[t % 2]
                    link(STT(hr, x[:, t], rs[:, t:t + 1], mod2[:, 2], ALU.mult, ALU.mult))
                    link(TT(hr, hr, mod2[:, 1], ALU.add), sem("h2_ready"))
                if t >= 2 and t != T:
                    read_logits(t - 2)
            dve.wait_ge(sem("exp_logits"), 1)
            dve.wait_ge(sem("router_consts"), 1)
            link(TS(scores, scores, 1.0, None, ALU.add))
            link(v.reciprocal(scores, scores))
            link(TT(sel, scores, rb.unsqueeze(1).to_broadcast([P, T, E]), ALU.add))
            pairs = sel.rearrange("p t (n e) -> p (t n) e", e=2)
            hi, lo, gs, eq, geq, best = grp
            flat = [m.rearrange("p t n -> p (t n)") for m in (hi8, lo8)]
            link(TT(flat[0], pairs[:, :, 0], pairs[:, :, 1], ALU.max))
            link(TT(flat[1], pairs[:, :, 0], pairs[:, :, 1], ALU.min))
            hi4, lo4 = (m.rearrange("p t (g e) -> p (t g) e", e=2) for m in (hi8, lo8))
            f = {m: q.rearrange("p t g -> p (t g)") for m, q in (("hi", hi), ("lo", lo), ("gs", gs))}
            link(TT(f["hi"], hi4[:, :, 0], hi4[:, :, 1], ALU.min))
            link(TT(f["lo"], lo4[:, :, 0], lo4[:, :, 1], ALU.max))
            link(TT(f["gs"], hi4[:, :, 0], hi4[:, :, 1], ALU.max))
            link(TT(hi, hi, lo, ALU.max))
            link(TT(gs, gs, hi, ALU.add))

            def first_best(dst, val, weight, c, tmp, n):
                link(v.tensor_reduce(c, val, AX.X, ALU.max))
                link(TT(tmp, val, c.unsqueeze(2).to_broadcast([P, T, n]), ALU.is_equal))
                link(TT(tmp, tmp, weight, ALU.mult))
                link(v.tensor_reduce(c, tmp, AX.X, ALU.max))
                link(TT(dst, tmp, c.unsqueeze(2).to_broadcast([P, T, n]), ALU.is_equal))

            first_best(best, gs, gw, col[0], eq, 4)
            link(TS(geq, best, 2 * NEG, -NEG, ALU.mult, ALU.add))
            s4, m4 = (m.rearrange("p t (g e) -> p (t g) e", e=4) for m in (sel, m16))
            link(TT(m4, s4, geq.rearrange("p t g -> p (t g)").unsqueeze(2).to_broadcast([P, 4 * T, 4]), ALU.min))
            first_best(one1, m16, eweight, col[0], u16, E)
            link(STT(sel2, one1, -NEG, m16, ALU.mult, ALU.add))
            first_best(one2, sel2, eweight, col[0], u16, E)
            link(TT(mask, one1, one2, ALU.add), sem("chosen"))
            wait_product(dve, "rank")
            read(v.tensor_copy(rank.rearrange("p t e -> p (t e)"), bank("rank")[:, 0:E * T]))
            link(TS(u16, rank, 128.0, None, ALU.is_ge))
            for n in (256.0, 384.0):
                link(STT(u16, rank, n, u16, ALU.is_ge, ALU.add))
            link(STT(rank, u16, -128.0, rank, ALU.mult, ALU.add))
            link(STT(u16, u16, 16.0, eidx, ALU.mult, ALU.add))
            TT(v32, chosen_k, rank.unsqueeze(1).to_broadcast([P, 2, T, E]), ALU.mult).then_inc(sem("picked"), 1)
            TT(u32, chosen_k, u16.unsqueeze(1).to_broadcast([P, 2, T, E]), ALU.mult).then_inc(sem("picked"), 1)
            dve.wait_ge(sem("picked"), 1)
            v.tensor_reduce(slot, v32, AX.X, ALU.add).then_inc(sem("picked"), 1)
            dve.wait_ge(sem("picked"), 2)
            v.tensor_reduce(column, u32, AX.X, ALU.add).then_inc(sem("picked"), 1)
            dve.wait_ge(sem("picked"), 4)
            for k in range(2):
                for t in range(T):
                    TS(in_slot[:, k, t], slot_no, slot[:, k, t:t + 1], None, ALU.is_equal).then_inc(sem("table_parts"), 1)
                    TS(in_table[:, k, t], column_no, column[:, k, t:t + 1], pair[:, k, t:t + 1],
                       ALU.is_equal, ALU.mult).then_inc(sem("table_parts"), 1)
            link(TT(v32, chosen_k, scores.unsqueeze(1).to_broadcast([P, 2, T, E]), ALU.mult))
            link(v.tensor_reduce(wtok, v32, AX.X, ALU.add))
            link(TT(col[1], wtok[:, 0], wtok[:, 1], ALU.add))
            link(v.reciprocal(col[2], col[1]))
            link(TT(wtok, wtok, col[2].unsqueeze(1).to_broadcast([P, 2, T]), ALU.mult))
            wait_product(dve, "table")
            link(TS(table, bank("table")[:, 0:80], 8.0 * SEQ, None, ALU.add))
            link(TS(tokens, table, 1, None, ALU.logical_shift_right))
            for s in ("he_made", "y_read"):
                dve.sem_inc(sem(s), 1)

            def gather_indices(r, p, j):
                v.tensor_copy(idx_g[j % 2], tokens[:, bass.ds(nth(dve, 1, r, p, j, 0), 1)]).then_inc(sem(f"idx_ready{j % 2}"), 1)

            def next_indices(r, p, j):
                dve.wait_ge(sem("xT_made"), nth(dve, 1, r, p, j, 1))
                gather_indices(r, p, j + 2)

            def hidden(r, p, j):
                b = j % 2
                dve.wait_ge(sem("silu_made"), nth(dve, 1, r, p, j, 2))
                dve.wait_ge(sem("up_made"), nth(dve, 1, r, p, j, 3))
                TT(he[b], gated[b], psum[:, 3], ALU.mult).then_inc(sem("he_made"), 1)

            def gated_y(r, p, j):
                b = j % 2
                dve.wait_ge(sem(f"slot_free{b}"), nth_of_half(dve, 1, r, p, j, 1))
                v.tensor_copy(idx_s[b], table[:, bass.ds(nth(dve, 1, r, p, j, 0), 1)])
                dve.wait_ge(sem("y_made"), nth(dve, 1, r, p, j, 3))
                TT(yo[b], psum[:, 5:7].rearrange("p b n -> p (b n)"), mod2[:, 3], ALU.mult).then_inc(sem("y_read"), 1)

            def first(r):
                next_indices(r, 0, 0)
                hidden(r, 0, 0)
                next_indices(r, 0, 1)

            def step(r, p, j):
                hidden(r, p, j)
                next_indices(r, p, j + 1)
                gated_y(r, p, j - 1)

            def last(r):
                hidden(r, 0, E - 1)
                gated_y(r, 0, E - 2)
                gated_y(r, 0, E - 1)

            for j in range(2):
                gather_indices(0, 0, j)
            read(v.tensor_copy(counts, bank("table")[:, 80:80 + E]))
            link(v.tensor_reduce(col[6][:, 0:1], counts, AX.X, ALU.max))
            link(TS(col[7][:, 0:1], col[6][:, 0:1], 128.0, 1.0, ALU.is_gt, ALU.add))
            for n in (256.0, 384.0):
                link(TS(col[8][:, 0:1], col[6][:, 0:1], n, None, ALU.is_gt))
                link(TT(col[7][:, 0:1], col[7][:, 0:1], col[8][:, 0:1], ALU.add))
            link(v.tensor_copy(rounds, col[7][:, 0:1]), sem("rounds_ready"))
            in_steps(dve, 0, first, step, last)
            n_rounds = dve.value_load(rounds[0:1, 0:1], min_val=1, max_val=4)
            with dve.If(n_rounds > 1):
                with dve.Fori(1, n_rounds) as r:
                    in_steps(dve, r, first, step, last)

            def invert(t):
                dve.wait_ge(sem("rms3_ready"), t + 1)
                link(v.reciprocal(rs[:, t:t + 1], rs[:, t:t + 1]), sem("rs3_inverted"))

            for t in range(T):
                dve.wait_ge(sem(f"ld_yb{t}0"), 16)
                link(STT(x[:, t], yb[t][:, 0], wtok[:, 0, t:t + 1], x[:, t], ALU.mult, ALU.add))
                if t >= 1:
                    invert(t - 1)
                dve.wait_ge(sem(f"ld_yb{t}1"), 16)
                link(STT(x[:, t], yb[t][:, 1], wtok[:, 1, t:t + 1], x[:, t], ALU.mult, ALU.add), sem("x2_ready"))
            dve.wait_ge(sem("ld_fn"), 16)
            for t in (T - 2, T - 1):
                if t == T - 1:
                    invert(t)
                STT(fout[t], x[:, t], rs[:, t:t + 1], fbc, ALU.mult, ALU.mult).then_inc(sem("last_ready"), 1)


def kernel(**inputs):
    from concourse import bacc
    from concourse.bass_utils import run_bass_kernel_spmd

    nc = bacc.Bacc("TRN2", target_bir_lowering=False, num_devices=1)
    arrays = {f"in_{n}": np.ascontiguousarray(inputs[n]) for n in INPUTS}
    aps = {n: nc.dram_tensor(f"in_{n}", arrays[f"in_{n}"].shape, mybir.dt.from_np(arrays[f"in_{n}"].dtype),
                             kind="ExternalInput").ap() for n in INPUTS}
    out = nc.dram_tensor("out_y", (1, SEQ, D), F32, kind="ExternalOutput").ap()
    build(nc, aps, out)
    return run_bass_kernel_spmd(nc, [arrays], core_ids=[0]).results[0]["out_y"]
```
